# Optimizing a Trainium2 kernel written in Bass

```python
import jax, jax.numpy as jnp
from jax import lax
import numpy as np
import math

D_MODEL = 1024
BATCH = 1
SEQ = 1024
DEPTH = 2

GRID_W = 64
CTX_LEN = 256
HEAD_DIM = 64
CONV_W = 256
CONV_GROUPS = 4
CONV_K = 3
RET_HEADS = 6
RET_W = RET_HEADS * HEAD_DIM
NA_HEADS = 6
NA_W = NA_HEADS * HEAD_DIM
MIX_W = CONV_W + RET_W + NA_W
RET_CHUNK = 128
WIN_H = 8
WIN_W = 16
ROPE_BASE = 10000.0
LN_EPS = 1e-5
DEEPNORM_ALPHA = (2 * DEPTH) ** 0.25
DEEPNORM_BETA = (8 * DEPTH) ** -0.25

PROJ_SPLITS = (RET_W, RET_W, NA_W, NA_W,
               RET_W, RET_W, NA_W, NA_W,
               CONV_W, CONV_W, CONV_W, CONV_W)
PROJ_W = sum(PROJ_SPLITS)
KV_W = 2 * RET_W + 2 * NA_W


F32 = jnp.float32

def split_cols(p, sizes):
    idx = np.cumsum(sizes)[:-1].tolist()
    return jnp.split(p, idx, axis=-1)

def to_heads(t, n_heads):
    b, l, _ = t.shape
    return t.reshape(b, l, n_heads, HEAD_DIM).transpose(0, 2, 1, 3)

def from_heads(t):
    b, h, l, d = t.shape
    return t.transpose(0, 2, 1, 3).reshape(b, l, h * d)

def layer_norm(x, g, b):
    xf = x.astype(F32)
    mu = jnp.mean(xf, axis=-1, keepdims=True)
    var = jnp.mean(jnp.square(xf - mu), axis=-1, keepdims=True)
    return ((xf - mu) * lax.rsqrt(var + LN_EPS) * g + b).astype(x.dtype)

def head_norm(o):
    of = o.astype(F32)
    mu = jnp.mean(of, axis=-1, keepdims=True)
    var = jnp.mean(jnp.square(of - mu), axis=-1, keepdims=True)
    return (of - mu) * lax.rsqrt(var + LN_EPS)

def axial_rope_angles(n):
    t = jnp.arange(n)
    row = (t // GRID_W).astype(F32)
    col = (t % GRID_W).astype(F32)
    nf = HEAD_DIM // 4
    inv = ROPE_BASE ** (-jnp.arange(nf, dtype=F32) / nf)
    return row[:, None] * inv, col[:, None] * inv

def rotate(xp, ang):
    a, b = jnp.split(xp, 2, axis=-1)
    cos, sin = jnp.cos(ang), jnp.sin(ang)
    return jnp.concatenate([a * cos - b * sin, a * sin + b * cos], axis=-1)

def apply_axial_rope(x, ang_r, ang_c):
    xr, xc = jnp.split(x, 2, axis=-1)
    return jnp.concatenate([rotate(xr, ang_r), rotate(xc, ang_c)], axis=-1).astype(x.dtype)

def short_conv_branch(h, bg, cg, z, w, b):
    u = cg * h
    up = jnp.pad(u, ((0, 0), (1, 1), (0, 0)))
    conv = up[:, :-2] * w[0] + up[:, 1:-1] * w[1] + up[:, 2:] * w[2] + b
    return bg * conv * jax.nn.silu(z)

def ret_final_state(k, v, lg):
    l = k.shape[2]
    w = jnp.exp((l - 1 - jnp.arange(l, dtype=F32))[None, :] * lg[:, None])
    return jnp.einsum('bhld,hl,bhle->bhde', k, w, v)

def chunk_retention(q, k, v, lg, s0, inclusive):
    b, h, l, dk = q.shape
    dv = v.shape[-1]
    c = min(RET_CHUNK, l)
    nc = l // c
    qc = q.reshape(b, h, nc, c, dk)
    kc = k.reshape(b, h, nc, c, dk)
    vc = v.reshape(b, h, nc, c, dv)
    i = jnp.arange(c, dtype=F32)
    diff = i[:, None] - i[None, :]
    mask = diff >= 0 if inclusive else diff > 0
    dmat = jnp.where(mask[None], jnp.exp(jnp.where(mask, diff, 0.0)[None] * lg[:, None, None]), 0.0)
    scores = jnp.einsum('bhnid,bhnjd->bhnij', qc, kc) * dmat[None, :, None]
    o_inner = jnp.einsum('bhnij,bhnje->bhnie', scores, vc)
    wk = jnp.exp((c - 1 - i)[None, :] * lg[:, None])
    u = jnp.einsum('bhnjd,hj,bhnje->bhnde', kc, wk, vc)
    g_chunk = jnp.exp(c * lg)[:, None, None]

    def step(s, u_n):
        return g_chunk * s + u_n, s

    _, s_prev = lax.scan(step, s0, jnp.moveaxis(u, 2, 0))
    s_prev = jnp.moveaxis(s_prev, 0, 2)
    wq = jnp.exp((i + 1)[None, :] * lg[:, None])
    o_cross = jnp.einsum('bhnid,hi,bhnde->bhnie', qc, wq, s_prev)
    return (o_inner + o_cross).reshape(b, h, l, dv)

def bidir_retention(q, k, v, lg_f, lg_b, s_f, s_b):
    fwd = chunk_retention(q, k, v, lg_f, s_f, True)
    bwd = chunk_retention(jnp.flip(q, 2), jnp.flip(k, 2), jnp.flip(v, 2), lg_b, s_b, False)
    return fwd + jnp.flip(bwd, 2)

def retention_branch(q, k, v, g, kc, vc, qc, gc, decay_logit, need_ctx):
    n = q.shape[1]
    kscale = HEAD_DIM ** -0.5
    ang_r, ang_c = axial_rope_angles(n)
    qh = apply_axial_rope(to_heads(q, RET_HEADS), ang_r, ang_c)
    kh = apply_axial_rope(to_heads(k, RET_HEADS), ang_r, ang_c) * kscale
    vh = to_heads(v, RET_HEADS)
    kch = to_heads(kc, RET_HEADS) * kscale
    vch = to_heads(vc, RET_HEADS)
    lg = jax.nn.log_sigmoid(decay_logit.astype(F32))
    lg_f, lg_b = lg[0], lg[1]
    s_f = ret_final_state(kch, vch, lg_f)
    s_b = ret_final_state(jnp.flip(kch, 2), jnp.flip(vch, 2), lg_b)
    o = bidir_retention(qh, kh, vh, lg_f, lg_b, s_f, s_b)
    y = from_heads(head_norm(o)) * jax.nn.silu(g)
    if not need_ctx:
        return y, None
    qch = to_heads(qc, RET_HEADS)
    zero = jnp.zeros_like(s_f)
    oc = bidir_retention(qch, kch, vch, lg_f, lg_b, zero, zero)
    yc = from_heads(head_norm(oc)) * jax.nn.silu(gc)
    return y, yc

def neighbourhood_branch(q, k, v, g, kc, vc, qc, gc, rpb, need_ctx):
    b, n, _ = q.shape
    rows = n // GRID_W
    win_h = min(WIN_H, rows)
    n_loc = win_h * WIN_W
    scale = HEAD_DIM ** -0.5

    def grid(t):
        return to_heads(t, NA_HEADS).reshape(b, NA_HEADS, rows, GRID_W, HEAD_DIM)

    qg, kg, vg = grid(q), grid(k), grid(v)
    kch, vch = to_heads(kc, NA_HEADS), to_heads(vc, NA_HEADS)
    r = np.arange(rows)
    row_start = np.clip(r - win_h // 2, 0, rows - win_h)
    d_row = row_start[:, None] + np.arange(win_h)[None, :] - r[:, None]
    cpos = np.arange(GRID_W)
    col_idx = np.clip(cpos - WIN_W // 2, 0, GRID_W - WIN_W)[:, None] + np.arange(WIN_W)[None, :]
    d_col = col_idx - cpos[:, None]

    def row_block(args):
        q_r, rs, dr = args
        k_band = lax.dynamic_slice_in_dim(kg, rs, win_h, axis=2)
        v_band = lax.dynamic_slice_in_dim(vg, rs, win_h, axis=2)
        k_win = k_band[:, :, :, col_idx]
        v_win = v_band[:, :, :, col_idx]
        s_loc = jnp.einsum('bhcd,bhrckd->bhcrk', q_r, k_win).astype(F32) * scale
        bias = rpb[:, dr[:, None, None] + (WIN_H - 1), d_col[None] + (WIN_W - 1)]
        s_loc = s_loc + bias.transpose(0, 2, 1, 3)[None].astype(F32)
        s_ctx = jnp.einsum('bhcd,bhjd->bhcj', q_r, kch).astype(F32) * scale
        p = jax.nn.softmax(jnp.concatenate([s_loc.reshape(b, NA_HEADS, GRID_W, n_loc), s_ctx], axis=-1), axis=-1)
        p_loc = p[..., :n_loc].reshape(b, NA_HEADS, GRID_W, win_h, WIN_W).astype(v.dtype)
        p_ctx = p[..., n_loc:].astype(v.dtype)
        return (jnp.einsum('bhcrk,bhrckd->bhcd', p_loc, v_win)
                + jnp.einsum('bhcj,bhjd->bhcd', p_ctx, vch))

    o = lax.map(row_block, (jnp.moveaxis(qg, 2, 0),
                            jnp.asarray(row_start, jnp.int32),
                            jnp.asarray(d_row, jnp.int32)))
    y = o.transpose(1, 0, 3, 2, 4).reshape(b, n, NA_W) * jax.nn.silu(g)
    if not need_ctx:
        return y, None
    qch = to_heads(qc, NA_HEADS)
    s = jnp.einsum('bhid,bhjd->bhij', qch, kch).astype(F32) * scale
    oc = jnp.einsum('bhij,bhjd->bhid', jax.nn.softmax(s, axis=-1).astype(vc.dtype), vch)
    yc = from_heads(oc) * jax.nn.silu(gc)
    return y, yc

def hybrid_layer(x, xc, c_act, cc_act, w_mod, b_mod, w_in, conv_w, conv_b,
                 ret_decay, na_rpb, w_out, ln_g, ln_b, need_ctx):
    shift, scale, gate = jnp.split(c_act @ w_mod + b_mod, 3, axis=-1)
    h = x * (1 + scale[:, None]) + shift[:, None]
    rk, rv, nk, nv, rq, rg, nq, ng, ch, cb, ccg, cz = split_cols(h @ w_in, PROJ_SPLITS)
    n_mod = 3 if need_ctx else 2
    mod_c = jnp.split(cc_act @ w_mod[:, :n_mod * D_MODEL] + b_mod[:n_mod * D_MODEL], n_mod)
    hc = xc * (1 + mod_c[1]) + mod_c[0]
    if need_ctx:
        pc = split_cols(hc @ w_in, PROJ_SPLITS)
    else:
        pc = split_cols(hc @ w_in[:, :KV_W], PROJ_SPLITS[:4]) + [None] * 8
    rkc, rvc, nkc, nvc, rqc, rgc, nqc, ngc, chc, cbc, ccc, czc = pc

    y_conv = short_conv_branch(ch, cb, ccg, cz, conv_w, conv_b)
    y_ret, yc_ret = retention_branch(rq, rk, rv, rg, rkc, rvc, rqc, rgc, ret_decay, need_ctx)
    y_na, yc_na = neighbourhood_branch(nq, nk, nv, ng, nkc, nvc, nqc, ngc, na_rpb, need_ctx)
    y = jnp.concatenate([y_conv, y_ret, y_na], axis=-1) @ w_out
    x_new = layer_norm(DEEPNORM_ALPHA * x + gate[:, None] * y, ln_g, ln_b)
    if not need_ctx:
        return x_new, None
    yc_conv = short_conv_branch(chc, cbc, ccc, czc, conv_w, conv_b)
    yc = jnp.concatenate([yc_conv, yc_ret, yc_na], axis=-1) @ w_out
    xc_new = layer_norm(DEEPNORM_ALPHA * xc + mod_c[2] * yc, ln_g, ln_b)
    return x_new, xc_new

def first_inputs(seed: int = 0) -> dict:
    key = jax.random.key(seed)
    ks = jax.random.split(key, 14)
    nrm = jax.random.normal
    x = nrm(ks[0], (BATCH, SEQ, D_MODEL), F32)
    c = nrm(ks[1], (BATCH, D_MODEL), F32)
    ctx = nrm(ks[2], (BATCH, CTX_LEN, D_MODEL), F32)
    c_ctx = nrm(ks[3], (D_MODEL,), F32)
    w_mod = nrm(ks[4], (DEPTH, D_MODEL, 3 * D_MODEL), F32) * (0.5 * D_MODEL ** -0.5)
    b_mod = 0.01 * nrm(ks[5], (DEPTH, 3 * D_MODEL), F32)
    w_in = nrm(ks[6], (DEPTH, D_MODEL, PROJ_W), F32) * (D_MODEL ** -0.5)
    conv_w = nrm(ks[7], (DEPTH, CONV_K, CONV_W), F32) * (CONV_K ** -0.5)
    conv_b = 0.01 * nrm(ks[8], (DEPTH, CONV_W), F32)
    gamma = 1.0 - 2.0 ** (-5.0 - np.arange(RET_HEADS))
    decay_init = np.log(gamma / (1.0 - gamma)).astype(np.float32)
    ret_decay = jnp.asarray(decay_init)[None, None, :] + 0.1 * nrm(ks[9], (DEPTH, 2, RET_HEADS), F32)
    na_rpb = 0.05 * nrm(ks[10], (DEPTH, NA_HEADS, 2 * WIN_H - 1, 2 * WIN_W - 1), F32)
    w_out = nrm(ks[11], (DEPTH, MIX_W, D_MODEL), F32) * (DEEPNORM_BETA * MIX_W ** -0.5)
    ln_g = 1.0 + 0.01 * nrm(ks[12], (DEPTH, D_MODEL), F32)
    ln_b = 0.01 * nrm(ks[13], (DEPTH, D_MODEL), F32)
    return {'x': x, 'c': c, 'ctx': ctx, 'c_ctx': c_ctx, 'w_mod': w_mod, 'b_mod': b_mod,
            'w_in': w_in, 'conv_w': conv_w, 'conv_b': conv_b, 'ret_decay': ret_decay,
            'na_rpb': na_rpb, 'w_out': w_out, 'ln_g': ln_g, 'ln_b': ln_b}

def first_block(x, c, ctx, c_ctx, w_mod, b_mod, w_in, conv_w, conv_b, ret_decay, na_rpb,
              w_out, ln_g, ln_b):
    c_act = jax.nn.silu(c)
    cc_act = jax.nn.silu(c_ctx)
    xc = ctx
    for l in range(DEPTH):
        x, xc = hybrid_layer(x, xc, c_act, cc_act, w_mod[l], b_mod[l], w_in[l], conv_w[l], conv_b[l],
                             ret_decay[l], na_rpb[l], w_out[l], ln_g[l], ln_b[l],
                             need_ctx=(l < DEPTH - 1))
    return x


DEPTH_2 = 1

GDN_HEADS = 4
GDN_HEAD_DIM = 128
GDN_WIDTH = GDN_HEADS * GDN_HEAD_DIM
CONV_WIDTH = 4
CHUNK = 64
SWA_HEADS = 8
SWA_HEAD_DIM = 64
SWA_WIDTH = SWA_HEADS * SWA_HEAD_DIM
DILATED_PATTERNS = ((128, 1), (512, 4), (2048, 16))
NUM_BUCKETS = 32
MAX_DISTANCE = 2048
MIX_WIDTH = GDN_WIDTH + SWA_WIDTH
IN_SIZES = (GDN_WIDTH, GDN_WIDTH, GDN_WIDTH, GDN_WIDTH, GDN_HEADS, GDN_HEADS,
            SWA_WIDTH, SWA_WIDTH, SWA_WIDTH)
IN_COLS = sum(IN_SIZES)
D_FF = ((-(-8 * D_MODEL // 3)) + 255) // 256 * 256
RMS_EPS = 1e-6


def rmsnorm(x, g):
    xf = x.astype(jnp.float32)
    y = xf * lax.rsqrt(jnp.mean(xf * xf, axis=-1, keepdims=True) + RMS_EPS)
    return (y * g.astype(jnp.float32)).astype(x.dtype)

def l2norm(x):
    return x * lax.rsqrt(jnp.sum(x * x, axis=-1, keepdims=True) + 1e-6)

def causal_depthwise_conv(x, w):
    K, C = w.shape
    return lax.conv_general_dilated(x, w[:, None, :].astype(x.dtype), (1,), ((K - 1, 0),),
                                    dimension_numbers=('NWC', 'WIO', 'NWC'),
                                    feature_group_count=C)

def chunk_gated_delta_rule(q, k, v, g, beta):
    Bn, S, H, Dk = q.shape
    Dv = v.shape[-1]
    N = S // CHUNK

    def chunks(t):
        t = t.reshape((Bn, N, CHUNK, H) + t.shape[3:])
        return jnp.moveaxis(jnp.moveaxis(t, 1, 0), 3, 2)

    qc, kc, vc = chunks(q), chunks(k), chunks(v)
    bc = chunks(beta)
    gc = jnp.cumsum(chunks(g), axis=-1)
    idx = jnp.arange(CHUNK)
    causal = idx[:, None] >= idx[None, :]
    strict = idx[:, None] > idx[None, :]
    decay = jnp.exp(jnp.where(causal, gc[..., :, None] - gc[..., None, :], -jnp.inf))
    kb = kc * bc[..., None]
    a = jnp.where(strict, jnp.einsum('nbhid,nbhjd->nbhij', kb, kc) * decay, 0.0)
    eye = jnp.eye(CHUNK, dtype=q.dtype)
    t_inv = lax.linalg.triangular_solve(eye + a, jnp.broadcast_to(eye, a.shape),
                                        left_side=True, lower=True)
    u = t_inv @ (vc * bc[..., None])
    w = t_inv @ (kb * jnp.exp(gc)[..., None])
    attn = jnp.einsum('nbhid,nbhjd->nbhij', qc, kc) * decay
    q_dec = qc * jnp.exp(gc)[..., None]
    k_dec = kc * jnp.exp(gc[..., -1:] - gc)[..., None]
    g_end = jnp.exp(gc[..., -1])

    def step(state, inp):
        u_i, w_i, attn_i, qd_i, kd_i, ge_i = inp
        v_new = u_i - jnp.einsum('bhck,bhkv->bhcv', w_i, state)
        o_i = (jnp.einsum('bhck,bhkv->bhcv', qd_i, state)
               + jnp.einsum('bhij,bhjv->bhiv', attn_i, v_new))
        state = state * ge_i[..., None, None] + jnp.einsum('bhck,bhcv->bhkv', kd_i, v_new)
        return state, o_i

    s0 = jnp.zeros((Bn, H, Dk, Dv), q.dtype)
    _, o = lax.scan(step, s0, (u, w, attn, q_dec, k_dec, g_end))
    return jnp.moveaxis(o, 0, 1).transpose(0, 1, 3, 2, 4).reshape(Bn, S, H, Dv)

def gated_deltanet(q, k, v, gate, beta_logit, a_logit, conv_w, a_log, dt_bias, onorm_g):
    f32 = jnp.float32
    Bn, S, _ = q.shape
    qkv = jax.nn.silu(causal_depthwise_conv(jnp.concatenate([q, k, v], axis=-1), conv_w)).astype(f32)
    q, k, v = jnp.split(qkv, 3, axis=-1)
    heads = lambda t: t.reshape(Bn, S, GDN_HEADS, GDN_HEAD_DIM)
    q = l2norm(heads(q)) * GDN_HEAD_DIM ** -0.5
    k = l2norm(heads(k))
    v = heads(v)
    beta = jax.nn.sigmoid(beta_logit.astype(f32))
    g = -jnp.exp(a_log.astype(f32)) * jax.nn.softplus(a_logit.astype(f32) + dt_bias.astype(f32))
    o = chunk_gated_delta_rule(q, k, v, g, beta)
    o = o * lax.rsqrt(jnp.mean(o * o, axis=-1, keepdims=True) + RMS_EPS) * onorm_g.astype(f32)
    o = o * jax.nn.silu(heads(gate).astype(f32))
    return o.reshape(Bn, S, GDN_WIDTH).astype(gate.dtype)

def t5_causal_bucket(dist):
    max_exact = NUM_BUCKETS // 2
    d = jnp.maximum(dist, 1).astype(jnp.float32)
    log_b = max_exact + (jnp.log(d / max_exact) / math.log(MAX_DISTANCE / max_exact)
                         * (NUM_BUCKETS - max_exact)).astype(jnp.int32)
    return jnp.where(dist < max_exact, dist, jnp.minimum(log_b, NUM_BUCKETS - 1))

def dilated_band(q, k, v, rel_bias, window, dilation):
    Bn, S, H, Dh = q.shape
    w = window // dilation
    L = S // dilation
    nb = -(-L // w)
    Lp = nb * w

    def to_sub(t):
        t = t.reshape(Bn, L, dilation, H, Dh).transpose(0, 3, 2, 1, 4)
        return jnp.pad(t, ((0, 0), (0, 0), (0, 0), (0, Lp - L), (0, 0)))

    blocks = lambda t: t.reshape(Bn, H, dilation, nb, w, Dh)

    def band(t):
        prev = jnp.pad(t, ((0, 0), (0, 0), (0, 0), (w, 0), (0, 0)))[:, :, :, :Lp]
        return jnp.concatenate([blocks(prev), blocks(t)], axis=-2)

    qb, kb, vb = blocks(to_sub(q)), band(to_sub(k)), band(to_sub(v))
    qi = jnp.arange(w)[:, None]
    kj = jnp.arange(2 * w)[None, :]
    rel = qi + w - kj
    blk = jnp.arange(nb)[:, None, None]
    valid = (rel >= 0) & (rel <= w) & (blk * w + kj - w >= 0)
    bias_steps = rel_bias[t5_causal_bucket(jnp.arange(w + 1) * dilation)]
    bias = jnp.moveaxis(bias_steps[jnp.clip(rel, 0, w)], -1, 0).astype(jnp.float32)
    logits = jnp.einsum('bhrnqd,bhrnkd->bhrnqk', qb, kb) * Dh ** -0.5 + bias[None, :, None, None]
    logits = jnp.where(valid, logits, -jnp.inf)
    m = jnp.max(logits, axis=-1)
    p = jnp.exp(logits - m[..., None])
    s = jnp.sum(p, axis=-1)
    num = jnp.einsum('bhrnqk,bhrnkd->bhrnqd', p, vb)

    def from_sub(t):
        rest = t.shape[5:]
        t = t.reshape((Bn, H, dilation, Lp) + rest)[:, :, :, :L]
        t = t.transpose((0, 3, 2, 1) + tuple(range(4, t.ndim)))
        return t.reshape((Bn, S, H) + rest)

    return from_sub(num), from_sub(m), from_sub(s)

def dilated_attention(q, k, v, rel_bias):
    Bn, S, _ = q.shape
    heads = lambda t: t.reshape(Bn, S, SWA_HEADS, SWA_HEAD_DIM).astype(jnp.float32)
    qh, kh, vh = heads(q), heads(k), heads(v)
    parts = [dilated_band(qh, kh, vh, rel_bias, win, dil) for win, dil in DILATED_PATTERNS]
    nums = jnp.stack([pt[0] for pt in parts])
    ms = jnp.stack([pt[1] for pt in parts])
    ss = jnp.stack([pt[2] for pt in parts])
    wts = jnp.exp(ms - jnp.max(ms, axis=0, keepdims=True))
    out = jnp.sum(wts[..., None] * nums, axis=0) / jnp.sum(wts * ss, axis=0)[..., None]
    return out.reshape(Bn, S, SWA_WIDTH).astype(q.dtype)

def second_inputs(seed: int = 0) -> dict:
    key = jax.random.key(seed)
    ks = jax.random.split(key, 16)
    f32 = jnp.float32
    nrm = lambda k_, shape, scale: jax.random.normal(k_, shape, f32) * scale
    dt = jnp.exp(jax.random.uniform(ks[4], (DEPTH_2, GDN_HEADS), f32, math.log(1e-3), math.log(1e-1)))
    return {
        'x': nrm(ks[0], (BATCH, SEQ, D_MODEL), 1.0),
        'w_in': nrm(ks[1], (DEPTH_2, D_MODEL, IN_COLS), D_MODEL ** -0.5),
        'conv_w': nrm(ks[2], (DEPTH_2, CONV_WIDTH, 3 * GDN_WIDTH), CONV_WIDTH ** -0.5),
        'a_log': jnp.log(jax.random.uniform(ks[3], (DEPTH_2, GDN_HEADS), f32, 1.0, 16.0)),
        'dt_bias': dt + jnp.log(-jnp.expm1(-dt)),
        'onorm_g': 1.0 + nrm(ks[5], (DEPTH_2, GDN_HEAD_DIM), 0.1),
        'rel_bias': nrm(ks[6], (NUM_BUCKETS, SWA_HEADS), 0.2),
        'w_out': nrm(ks[7], (DEPTH_2, MIX_WIDTH, D_MODEL), MIX_WIDTH ** -0.5),
        'g_mix_pre': 1.0 + nrm(ks[8], (DEPTH_2, D_MODEL), 0.1),
        'g_mix_post': 1.0 + nrm(ks[9], (DEPTH_2, D_MODEL), 0.1),
        'w_gate': nrm(ks[10], (DEPTH_2, D_MODEL, D_FF), D_MODEL ** -0.5),
        'w_up': nrm(ks[11], (DEPTH_2, D_MODEL, D_FF), D_MODEL ** -0.5),
        'w_down': nrm(ks[12], (DEPTH_2, D_FF, D_MODEL), D_FF ** -0.5),
        'g_ffn_pre': 1.0 + nrm(ks[13], (DEPTH_2, D_MODEL), 0.1),
        'g_ffn_post': 1.0 + nrm(ks[14], (DEPTH_2, D_MODEL), 0.1),
    }

def second_block(x, w_in, conv_w, a_log, dt_bias, onorm_g, rel_bias, w_out, g_mix_pre, g_mix_post,
              w_gate, w_up, w_down, g_ffn_pre, g_ffn_post):
    split_at = [int(c) for c in np.cumsum(IN_SIZES)[:-1]]
    for l in range(DEPTH_2):
        h = rmsnorm(x, g_mix_pre[l])
        proj = h @ w_in[l]
        qa, ka, va, gate_a, beta_a, alpha_a, qb, kb, vb = jnp.split(proj, split_at, axis=-1)
        out_a = gated_deltanet(qa, ka, va, gate_a, beta_a, alpha_a,
                               conv_w[l], a_log[l], dt_bias[l], onorm_g[l])
        out_b = dilated_attention(qb, kb, vb, rel_bias)
        mix = jnp.concatenate([out_a, out_b], axis=-1) @ w_out[l]
        x = x + rmsnorm(mix, g_mix_post[l])
        h = rmsnorm(x, g_ffn_pre[l])
        f = (jax.nn.silu(h @ w_gate[l]) * (h @ w_up[l])) @ w_down[l]
        x = x + rmsnorm(f, g_ffn_post[l])
    return x


def setup_inputs(seed=0):
    out = dict(first_inputs(seed))
    for name, value in second_inputs(seed + 1).items():
        if name != "x":
            out[name + "_2"] = value
    return out


def reference(
    x, c, ctx, c_ctx, w_mod, b_mod, w_in, conv_w, conv_b, ret_decay, na_rpb, w_out, ln_g, ln_b,
    w_in_2, conv_w_2, a_log_2, dt_bias_2, onorm_g_2, rel_bias_2, w_out_2, g_mix_pre_2,
    g_mix_post_2, w_gate_2, w_up_2, w_down_2, g_ffn_pre_2, g_ffn_post_2,
):
    x = first_block(
        x, c, ctx, c_ctx, w_mod, b_mod, w_in, conv_w, conv_b, ret_decay, na_rpb, w_out, ln_g,
        ln_b,
    )
    return second_block(
        x, w_in_2, conv_w_2, a_log_2, dt_bias_2, onorm_g_2, rel_bias_2, w_out_2, g_mix_pre_2,
        g_mix_post_2, w_gate_2, w_up_2, w_down_2, g_ffn_pre_2, g_ffn_post_2,
    )


_drawn_inputs = setup_inputs


def setup_inputs(seed=0):
    import zlib

    import numpy as np

    out = dict(_drawn_inputs(seed))
    spreads = {}
    factors = {'b_mod': 8.0, 'conv_b': 64.0, 'na_rpb': 64.0, 'ctx': 2.695}
    for name, (base, spread) in spreads.items():
        noise = np.random.default_rng([zlib.crc32(name.encode()), seed]).standard_normal(out[name].shape)
        drawn = base * np.exp(spread * noise) if base else spread * noise
        out[name] = __import__('jax').numpy.asarray(drawn.astype(out[name].dtype))
    for name, factor in factors.items():
        out[name] = (out[name] * factor).astype(out[name].dtype)
    return out
```

```python
from contextlib import ExitStack

import numpy as np

import concourse.bass as bass
from concourse import mybir

F32 = mybir.dt.float32
F32R = mybir.dt.float32r
ALU = mybir.AluOpType
ACT = mybir.ActivationFunctionType
AX_X = mybir.AxisListType.X

P = 128
D = 1024
KT = D // P
CTX, SEQ = 256, 1024
T = CTX + SEQ
LAYERS = 2
HD = 64
PAIRS = 3
NCH = T // P
GRID_W, GRID_H, WIN_H = 64, 16, 8
RPB_H, RPB_W = 15, 31
ALPHA = (2 * LAYERS) ** 0.25
GH = 4
NC2 = SEQ // P
SWA_PAIRS = 4
DFF = 2816
FT = DFF // P
BUCKETS = 32
TB = 1152
CHUNKS = [(0, CTX), (CTX, 512), (CTX + 512, 512)]
MAIN = CHUNKS[1:]
NEG = -1.0e30
INV_LEVELS = 7

C1 = {}
C2 = {}


def _place(table, names):
    at = 0
    for name, n in names:
        table[name] = (at, n)
        at += n
    return at


N1 = _place(C1, [("ident", P), ("rot", P), ("center", P), ("headmean", P), ("pairmask", P), ("flip64", P),
                 ("ip1", P), ("rev", P), ("fwd", P), ("bwd", P), ("mean", P), ("wincol", GRID_W),
                 ("jrev", 1), ("j", 1), ("eps", 1)])
N2 = _place(C2, [("ident", P), ("mean", P), ("eps", 1), ("ones", P), ("headmean", P), ("upto", P), ("causalT", P),
                 ("strict", P), ("flip", P), ("low0", P)] + [(f"lowT{k}", P) for k in range(INV_LEVELS)])


def constants():
    f = np.float32
    i = np.arange(P)
    eye = np.eye(P, dtype=f)
    half = (i[:, None] // HD == i[None, :] // HD).astype(f)
    rot = np.zeros((P, P), f)
    for b in range(0, P, 32):
        for k in range(16):
            rot[b + 16 + k, b + k] = -1.0
            rot[b + k, b + 16 + k] = 1.0
    flip64 = np.zeros((P, P), f)
    for b in (0, HD):
        for k in range(HD):
            flip64[b + k, b + HD - 1 - k] = 1.0
    c = np.arange(GRID_W)
    start = np.clip(c - 8, 0, GRID_W - 16)
    inside = (c[None, :] >= start[:, None]) & (c[None, :] < start[:, None] + 16)
    wincol = np.where(inside, 0.0, NEG).astype(f)
    row = lambda v: np.broadcast_to(np.asarray(v, f), (P, P))
    parts = {
        "ident": eye, "rot": rot, "center": eye - half / HD, "headmean": half / HD, "pairmask": half, "flip64": flip64,
        "ip1": row(i + 1), "rev": row(P - i), "fwd": np.maximum(i[None, :] - i[:, None], 0),
        "bwd": np.maximum(i[:, None] - i[None, :], 0), "mean": np.full((P, P), 1.0 / D),
        "wincol": np.concatenate([wincol, wincol]), "jrev": (P - 1 - i)[:, None], "j": i[:, None],
        "eps": np.full((P, 1), 1e-5),
    }
    c1 = np.concatenate([np.asarray(parts[n], f) for n in C1], axis=1)
    parts = {
        "ident": eye, "mean": np.full((P, P), 1.0 / D), "ones": np.ones((P, P)), "headmean": np.full((P, P), 1.0 / P),
        "upto": (i[:, None] <= i[None, :]), "causalT": np.where(i[None, :] >= i[:, None], 0.0, NEG),
        "strict": np.where(i[:, None] > i[None, :], 0.0, NEG), "flip": eye[::-1], "eps": np.full((P, 1), 1e-6),
    }
    for k in range(INV_LEVELS):
        b = i >> k
        low = ((b[:, None] % 2 == 1) & (b[None, :] == b[:, None] - 1)).astype(f)
        parts[f"lowT{k}"] = low.T
        if k == 0:
            parts["low0"] = low
    c2 = np.concatenate([np.asarray(parts[n], f) for n in C2], axis=1)
    nf = HD // 4
    inv = (f(10000.0) ** (-np.arange(nf, dtype=f) / f(nf))).astype(f)
    t = np.arange(SEQ)
    ang_r = (t // GRID_W).astype(f)[:, None] * inv
    ang_c = (t % GRID_W).astype(f)[:, None] * inv
    ang = np.concatenate([ang_r, ang_r, ang_c, ang_c], axis=1).T
    ang = np.concatenate([ang, ang], axis=0).astype(f)
    cos = np.concatenate([np.ones((P, CTX), f), np.cos(ang)], axis=1)
    sin = np.concatenate([np.zeros((P, CTX), f), np.sin(ang)], axis=1)
    dist = 1023 - np.arange(TB)
    d = np.maximum(dist, 1).astype(f)
    far = 16 + (np.log(d / f(16)) / f(np.log(2048 / 16)) * f(16)).astype(np.int32)
    bucket = np.where(dist < 16, dist, np.minimum(far, 31))
    times = ((dist <= 128).astype(int) + ((dist % 4 == 0) & (dist <= 512)) + ((dist % 16 == 0) & (dist <= 2048)))
    times = np.where(dist >= 0, times, 0)
    buckets = np.zeros((BUCKETS + 1, TB), f)
    for y in range(TB):
        if times[y] > 0:
            buckets[bucket[y], y] = 1.0
            buckets[BUCKETS, y] = np.log(f(times[y]))
        else:
            buckets[BUCKETS, y] = NEG
    return {"c1": c1, "c2": c2, "cos": cos, "sin": sin, "buckets": buckets}


SHARED = """
rot=g_gb tp=g_ss u=g_tp rs=g_qk ro=g_tat rcen=g_py rvar=g_pz nfl=g_uw ntp=g_ws ns=g_kv nta=g_o ntb=g_ov
no=stp mu=sfl var=r_var
rope=g_conv qf=g_n kw=g_kd um=g_tk S=g_S rsc=g_tv ryr=g_d nt=g_att nm=g_a npn=g_ot npb=g_x ny=g_vn
ylo=r_lo res=r_rt cen=p_t nrm=p_x
vt=g_gbc ros=g_eg rsq=g_silu rrs=g_sq reta=g_rs nvt=g_kdc ne=g_dx npa=g_at yhi=r_hi lna=g_y sq=r_sq rstd=r_rs fin=g_u
nf=sf
"""


class Count:

    def __init__(self, sem, base):
        self.sem, self.base = sem, base

    def at(self, n):
        return self.sem, self.base + n


class Chain:

    def __init__(self, eng, sem):
        self.eng, self.sem, self.n = eng, sem, 0

    def __call__(self, ins):
        self.n += 1
        ins.then_inc(self.sem, 1)
        self.eng.wait_ge(self.sem, self.n)


def build(nc, I, out, scratch, upto=None):
    top = ExitStack()
    uid = [0]

    def sb(name, shape, dt=F32, stack=None):
        uid[0] += 1
        return (stack or top).enter_context(nc.sbuf_tensor(f"{name}_{uid[0]}", shape, dt))

    handles, raised = {}, {}
    signals = {}
    for a in SHARED.split():
        one, two = a.split("=")
        signals[one] = signals[two] = f"{one}_{two}"

    def sem(name, total=0):
        if name in signals:
            name = signals[name]
        if name not in handles:
            handles[name] = top.enter_context(nc.semaphore(name))
            raised[name] = 0
        raised[name] += total
        return Count(handles[name], raised[name] - total)

    with top:
        bank = [top.enter_context(nc.psum_tensor(f"bank{i}", [P, 512], F32)) for i in range(8)]

        RAW, SPLIT = 2, 2
        raw = sb("raw", [P, RAW, KT * P])
        ws = sb("ws", [P, SPLIT, 2, KT * P], F32R)
        s_raw = [sem(f"raw{i}") for i in range(RAW)]
        s_whi, s_wlo = sem("w_hi"), sem("w_lo")
        s_gemm = sem("gemm")
        s_evac = sem("evac")
        s_modmm = sem("mod_mm")
        s_unit = sem("unit")

        dmas = []
        raw_free = []
        blocks = []
        n_piece, n_out, n_units = [0], [0], [0]

        def mod_block(src):
            dmas.append((src, KT * P))
            raw_free.append(s_modmm.at(len(raw_free) + 1))
            return len(dmas) - 1

        def block(src, kts, chunks, rhs, k0=0, first=True, last=True):
            b = len(blocks)
            dmas.append((src, kts * P))
            raw_free.append(s_wlo.at(b + 1))
            o0 = n_out[0]
            blocks.append(dict(b=b, r=len(dmas) - 1, kts=kts, chunks=chunks, rhs=rhs, k0=k0, first=first, last=last,
                               piece=n_piece[0], out=o0))
            n_piece[0] += len(chunks)
            if last:
                n_out[0] += len(chunks)
            return blocks[-1]

        def sp_weights(sp):
            for r, (src, n) in enumerate(dmas):
                if r >= RAW:
                    sp.wait_ge(*raw_free[r - RAW])
                sp.dma_start(raw[:, r % RAW, 0:n], src).then_inc(s_raw[r % RAW].sem, 16)

        def act_split(act, b):
            if b >= len(blocks):
                return
            blk = blocks[b]
            n = blk["kts"] * P
            act.wait_ge(*s_raw[blk["r"] % RAW].at(16 * (blk["r"] // RAW + 1)))
            if b >= SPLIT:
                prev = blocks[b - SPLIT]
                act.wait_ge(*s_gemm.at(prev["piece"] + len(prev["chunks"])))
            act.activation(ws[:, b % SPLIT, 0, 0:n], raw[:, blk["r"] % RAW, 0:n], ACT.Copy).then_inc(s_whi.sem, 1)

        def dve_split(dve, b):
            if b >= len(blocks):
                return
            blk = blocks[b]
            n = blk["kts"] * P
            dve.wait_ge(*s_whi.at(b + 1))
            dve.tensor_tensor(ws[:, b % SPLIT, 1, 0:n], raw[:, blk["r"] % RAW, 0:n],
                              ws[:, b % SPLIT, 0, 0:n].bitcast(F32), ALU.subtract).then_inc(s_wlo.sem, 1)

        def pe_block(pe, blk):
            b = blk["b"]
            pe.wait_ge(*s_wlo.at(b + 1))
            for ci, (t0, n) in enumerate(blk["chunks"]):
                o = blk["out"] + ci
                if blk["first"] and o >= 2:
                    pe.wait_ge(*s_evac.at(o - 1))
                mm = None
                for k in range(blk["kts"]):
                    for part, (wp, xp) in enumerate(((0, 0), (0, 1), (1, 0))):
                        mm = pe.matmul(bank[o % 2][:, 0:n], ws[:, b % SPLIT, wp, k * P:(k + 1) * P],
                                       blk["rhs"](xp, blk["k0"] + k, t0, n),
                                       start=blk["first"] and k == 0 and part == 0,
                                       stop=blk["last"] and k == blk["kts"] - 1 and part == 2)
                mm.then_inc(s_gemm.sem, 1)

        def act_block(act, blk, evac):
            if blk["last"]:
                for ci, (t0, n) in enumerate(blk["chunks"]):
                    act.wait_ge(*s_gemm.at(blk["piece"] + ci + 1))
                    evac(ci, t0, n, bank[(blk["out"] + ci) % 2][:, 0:n]).then_inc(s_evac.sem, 1)
            act_split(act, blk["b"] + SPLIT)

        def out_done(blk, ci=None):
            return blk["out"] + (len(blk["chunks"]) if ci is None else ci + 1)

        order = {}

        def dve_chain(v):
            if "dve" not in order:
                order["dve"] = Chain(v, sem("dve_order").sem)
            return order["dve"]

        Y = sb("Y", [P, KT, T])
        gp2 = sb("gp2", [P, 4, KT])
        s_const = sem("const")
        phases = []

        b1 = top.enter_context(ExitStack())
        HH = sb("HH", [P, 2, KT, T], F32R, b1)
        c1 = sb("c1", [P, N1], F32, b1)
        arena_n = 11008
        arena = sb("arena", [P, arena_n], F32, b1)
        modv = sb("modv", [P, LAYERS, 24, 2], F32, b1)
        cact = sb("cact", [P, KT, 2], F32, b1)
        bmod = sb("bmod", [P, LAYERS, 24], F32, b1)
        lnp = sb("lnp", [P, LAYERS, 2, KT], F32, b1)
        convp = sb("convp", [P, LAYERS, 2, 4], F32, b1)
        LG = sb("LG", [P, LAYERS, 18], F32, b1)
        DT = sb("DT", [P, 6, P], F32, b1)
        WQ = sb("WQ", [P, 2, PAIRS, P], F32, b1)
        WK = sb("WK", [P, 2, 6], F32, b1)
        G128 = sb("G128", [P, 6], F32, b1)
        small = sb("small", [P, 64], F32, b1)

        def k1(name):
            a, n = C1[name]
            return c1[:, a:a + n]

        spots = {}

        def spot(name, n, at):
            assert at + n <= arena_n, (name, at + n)
            spots[name] = (at, n)
            return arena[:, at:at + n]

        PXs = [spot(f"px{i}", T, i * T) for i in range(4)]
        a0 = 4 * T
        lgt = PXs[1][:, 0:4 * LAYERS * 18].rearrange("q (a c) -> q a c", a=4)
        TMP = spot("tmp", 512, a0)
        COS = spot("cos", T, a0 + 512)
        SIN = spot("sin", T, a0 + 512 + T)
        SF, SB = COS, SIN
        QF = spot("qf", T, a0 + 512 + 2 * T)
        r0 = a0 + 512 + 3 * T
        UM = spot("um", 512, r0)
        SC = spot("sc", 1024, r0 + 512)
        QB = spot("qb", 20 * P, a0 + 512)
        NT = spot("nt", RPB_H * GRID_W, a0 + 512 + 20 * P)
        n0 = a0 + 512 + 20 * P + RPB_H * GRID_W
        PR = [spot(f"pr{i}", 768, n0 + i * 768) for i in range(2)]
        assert n0 + 1536 <= arena_n, n0 + 1536
        NF = arena[:, n0:n0 + RPB_H * GRID_W]

        def rhs_hh(part, k, t0, n):
            return HH[:, part, k, t0:t0 + n]

        s_x0 = sem("x0")

        def mod_phase():
            ids = [[mod_block(I["wmod"][l, m]) for m in range(24)] for l in range(LAYERS)]
            s_ca, s_mod, s_lg, s_chain, s_achain = sem("cact"), sem("mod"), sem("lg"), sem("modchain"), sem("modact")
            s_e = sem("lge")

            def pool(g):
                g.dma_start(c1[:, :], I["c1"]).then_inc(s_const.sem, 16)
                g.dma_start(cact[:, :, :], I["c2t"]).then_inc(s_const.sem, 16)
                g.dma_start(bmod[:, :, :], I["bmod"]).then_inc(s_const.sem, 16)
                g.dma_start(lnp[:, :, :, :], I["lnp"]).then_inc(s_const.sem, 16)
                g.dma_start(convp[:, :, :, :], I["convp"]).then_inc(s_const.sem, 16)
                rd = I["decay_t"]
                for l in range(LAYERS):
                    g.dma_start(LG[:, l, 0:12], bass.AP(tensor=rd, offset=l * 12, ap=[[0, P], [1, 12]])).then_inc(s_const.sem, 16)
                    for e in range(2):
                        g.dma_start(LG[64 * e:64 * e + 64, l, 12:18],
                                    bass.AP(tensor=I["decayp_t"], offset=(l * 2 + e) * 6, ap=[[0, 64], [1, 6]])).then_inc(s_const.sem, 16)
                g.dma_start(Y[:, :, :], I["xt"]).then_inc(s_x0.sem, 16)

            NCONST = 5 + LAYERS * 3

            def act(a):
                a.wait_ge(*s_const.at(16 * NCONST))
                ch = Chain(a, s_achain.sem)
                ch(a.activation(cact[:, :, :], cact[:, :, :], ACT.Silu))
                a.wait_ge(*s_e.at(1))
                ch(a.activation(lgt[:, 1, :], lgt[:, 0, :], ACT.Exp))
                ch(a.activation(lgt[:, 2, :], lgt[:, 1, :], ACT.Ln, bias=1.0))

            def pe(p):
                p.wait_ge(*s_achain.at(1))
                for l in range(LAYERS):
                    for m in range(24):
                        r = ids[l][m]
                        p.wait_ge(*s_raw[r % RAW].at(16 * (r // RAW + 1)))
                        for k in range(KT):
                            mm = p.matmul(bank[2 + l][:, 2 * m:2 * m + 2], raw[:, r % RAW, k * P:(k + 1) * P], cact[:, k, :],
                                          start=k == 0, stop=k == KT - 1)
                        mm.then_inc(s_modmm.sem, 1)

            def dve(v):
                ch = dve_chain(v)
                v.wait_ge(*s_const.at(16 * NCONST))
                x = LG[:, :, :].rearrange("p l c -> p (l c)")
                v.scalar_tensor_tensor(lgt[:, 0, :], x, -1.0, x, ALU.mult, ALU.min).then_inc(s_e.sem, 1)
                v.wait_ge(*s_achain.at(3))
                e, l1 = lgt[:, 1, :], lgt[:, 2, :]
                t = lgt[:, 3, :]
                ch(v.tensor_scalar(t, e, 1.0, -1.0, ALU.add, ALU.add))
                ch(v.tensor_scalar(t, t, 1e-30, None, ALU.max))
                ch(v.reciprocal(t, t))
                ch(v.tensor_tensor(t, t, e, ALU.mult))
                ch(v.tensor_tensor(l1, l1, t, ALU.mult))
                ch(v.tensor_scalar(t, e, -0.5, 1.0, ALU.mult, ALU.add))
                ch(v.tensor_tensor(t, t, e, ALU.mult))
                ch(v.tensor_tensor(l1, l1, t, ALU.max))
                v.scalar_tensor_tensor(x, x, 0.0, l1, ALU.min, ALU.subtract).then_inc(s_lg.sem, 1)
                v.wait_ge(*s_lg.at(1))
                for l in range(LAYERS):
                    v.wait_ge(*s_modmm.at(24 * (l + 1)))
                    ch(v.tensor_tensor(modv[:, l, :, :], bank[2 + l][:, 0:48].rearrange("p (m c) -> p m c", c=2),
                                       bmod[:, l, :].unsqueeze(2).to_broadcast([P, 24, 2]), ALU.add))
                    v.tensor_scalar(modv[:, l, 8:16, :], modv[:, l, 8:16, :], 1.0, None, ALU.add).then_inc(s_mod.sem, 1)
                    v.wait_ge(*s_mod.at(l + 1))

            return dict(pool=pool, act=act, pe=pe, dve=dve, s_mod=s_mod, s_lg=s_lg)

        mod = mod_phase()
        phases.append(mod)

        s_h = [sem(f"h{l}") for l in range(LAYERS)]
        s_hhi = [sem(f"hhi{l}") for l in range(LAYERS)]
        s_xst = sem("xst")
        s_dt = [sem(f"dt{l}") for l in range(LAYERS)]

        def start_phase(l, s_ready, v_ready):
            s_tabd = sem("tabd", 1)
            segs = [(0, CTX, 1), (CTX, SEQ, 0)]

            def act(a):
                a.wait_ge(*mod["s_mod"].at(l + 1))
                a.wait_ge(*s_ready.at(v_ready))
                for k in range(KT):
                    for si, (t0, n, w) in enumerate(segs):
                        ins = a.activation(HH[:, 0, k, t0:t0 + n], Y[:, k, t0:t0 + n], ACT.Identity,
                                           scale=modv[:, l, 8 + k, w:w + 1], bias=modv[:, l, k, w:w + 1])
                        ins.then_inc(s_hhi[l].sem, 1)
                a.wait_ge(*s_tabd.at(1))
                a.activation(DT[:, :, :], DT[:, :, :], ACT.Exp).then_inc(s_dt[l].sem, 1)
                lp = LG[:, l, 12:18]
                for d, src in enumerate(("ip1", "rev")):
                    for p in range(PAIRS):
                        a.activation(WQ[:, d, p, :], k1(src), ACT.Exp, scale=LG[:, l, 12 + 3 * d + p:13 + 3 * d + p]).then_inc(s_dt[l].sem, 1)
                a.activation(WK[:, 0, :], LG[:, l, 0:6], ACT.Exp, scale=k1("jrev")).then_inc(s_dt[l].sem, 1)
                a.activation(WK[:, 1, :], LG[:, l, 6:12], ACT.Exp, scale=k1("j")).then_inc(s_dt[l].sem, 1)
                a.activation(G128[:, :], lp, ACT.Exp, scale=float(P)).then_inc(s_dt[l].sem, 1)
                if l == 0:
                    act_split(a, 0)
                    act_split(a, 1)

            def dve(v):
                ch = dve_chain(v)
                v.wait_ge(*mod["s_lg"].at(1))
                if l:
                    v.wait_ge(*s_unit.at(n_units_before))
                for h in range(6):
                    ch(v.tensor_scalar(DT[:, h, :], k1("fwd"), LG[:, l, h:h + 1], None, ALU.mult))
                    ins = v.scalar_tensor_tensor(DT[:, h, :], k1("bwd"), LG[:, l, 6 + h:7 + h], DT[:, h, :], ALU.mult, ALU.add)
                    if h < 5:
                        ch(ins)
                    else:
                        ins.then_inc(s_tabd.sem, 1)
                v.wait_ge(*mod["s_mod"].at(l + 1))
                v.wait_ge(*s_ready.at(v_ready))
                i = 0
                for k in range(KT):
                    for si, (t0, n, w) in enumerate(segs):
                        tt = PXs[0][:, 0:n]
                        ch(v.tensor_scalar(tt, Y[:, k, t0:t0 + n], modv[:, l, 8 + k, w:w + 1], modv[:, l, k, w:w + 1], ALU.mult, ALU.add))
                        i += 1
                        v.wait_ge(*s_hhi[l].at(i))
                        v.tensor_tensor(HH[:, 1, k, t0:t0 + n], tt, HH[:, 0, k, t0:t0 + n].bitcast(F32), ALU.subtract).then_inc(s_h[l].sem, 1)
                        v.wait_ge(*s_h[l].at(i))
                if l == 0:
                    dve_split(v, 0)
                    dve_split(v, 1)

            def pe(p):
                p.wait_ge(*s_h[l].at(2 * KT))

            n_units_before = n_units[0]
            return dict(act=act, dve=dve, pe=pe)

        NDT = 10

        def conv_unit(l, c):
            u = n_units[0]
            n_units[0] += 1
            chunks = CHUNKS if l == 0 else MAIN
            segs = ([(0, CTX)] if l == 0 else []) + [(CTX, T)]
            lo = segs[0][0]
            cols = [24 + c, 26 + c, 28 + c, 30 + c]
            blks = [block(I["win"][l, m], KT, chunks, rhs_hh) for m in cols]
            
            def pe(p):
                for blk in blks:
                    pe_block(p, blk)

            def act(a):
                a.wait_ge(*s_unit.at(u))
                if u == 0:
                    a.wait_ge(*s_h[0].at(2 * KT))
                for i, blk in enumerate(blks):
                    act_block(a, blk, lambda ci, t0, n, ps: a.activation(PXs[i][:, t0:t0 + n], ps, ACT.Silu if i == 3 else ACT.Copy))

            def dve(v):
                ch = dve_chain(v)
                for blk in blks:
                    dve_split(v, blk["b"] + SPLIT)
                h, bg, cg, z = PXs
                w = convp[:, l, c, :]
                tmp = arena[:, a0:a0 + T]
                v.wait_ge(*s_evac.at(out_done(blks[3])))
                ch(v.tensor_tensor(h[:, lo:], h[:, lo:], cg[:, lo:], ALU.mult))
                ch(v.tensor_scalar(tmp[:, lo:], h[:, lo:], w[:, 1:2], w[:, 3:4], ALU.mult, ALU.add))
                for a_, b_ in segs:
                    ch(v.scalar_tensor_tensor(tmp[:, a_ + 1:b_], h[:, a_:b_ - 1], w[:, 0:1], tmp[:, a_ + 1:b_], ALU.mult, ALU.add))
                    ch(v.scalar_tensor_tensor(tmp[:, a_:b_ - 1], h[:, a_ + 1:b_], w[:, 2:3], tmp[:, a_:b_ - 1], ALU.mult, ALU.add))
                ch(v.tensor_tensor(tmp[:, lo:], tmp[:, lo:], bg[:, lo:], ALU.mult))
                if l == 1:
                    v.wait_ge(*s_xst.at(16))
                v.tensor_tensor(Y[:, c, lo:], tmp[:, lo:], z[:, lo:], ALU.mult).then_inc(s_unit.sem, 1)
                v.wait_ge(*s_unit.at(u + 1))

            return dict(pe=pe, act=act, dve=dve)

        def ret_unit(l, p):
            u = n_units[0]
            n_units[0] += 1
            qch = CHUNKS if l == 0 else MAIN
            blks = [block(I["win"][l, p], KT, CHUNKS, rhs_hh), block(I["win"][l, 3 + p], KT, CHUNKS, rhs_hh),
                    block(I["win"][l, 12 + p], KT, qch, rhs_hh), block(I["win"][l, 15 + p], KT, qch, rhs_hh)]
            Kb, Vb, Qb, Gb = PXs
            KWF, KWB, VT = (Y[:, 5 + i, :] for i in range(3))
            QBK = Vb
            items = [(Kb, 0, ci, c) for ci, c in enumerate(CHUNKS)] + [(Qb, 2, ci, c) for ci, c in enumerate(qch)]
            n_rope = len(items)
            groups = ([[0, 1]] if l == 0 else []) + [[2, 3, 4, 5], [6, 7, 8, 9]]
            NG = len(groups)
            s_cs, s_rot, s_rope, s_qf = sem("cossin", 32), sem("rot", n_rope), sem("rope", n_rope), sem("qf", 1)
            s_tp, s_kw, s_vt, s_u, s_um, s_S = sem("tp", 6), sem("kw", 3), sem("vt", 3), sem("u", 6), sem("um", 6), sem("S", 1)
            s_s, s_sc, s_o, s_os, s_cen, s_sq, s_var, s_rs, s_yr = (
                sem(x, n * NG) for x, n in (("rs", 2), ("rsc", 2), ("ro", 1), ("ros", 1), ("rcen", 1), ("rsq", 1), ("rvar", 1), ("rrs", 1), ("ryr", 1)))
            s_ac = sem("reta", 2 * NG)
            fills = [range(0, 4), range(4, 8), range(8, 10)]
            ufills = [(0, [0, 1, 2, 3]), (0, [4, 5, 6, 7]), (0, [8]), (1, [1, 0, 9, 8]), (1, [7, 6, 5, 4]), (1, [3])]
            lo = qch[0][0]

            def pool(g):
                g.wait_ge(*s_unit.at(u))
                g.dma_start(COS, I["cos"]).then_inc(s_cs.sem, 16)
                g.dma_start(SIN, I["sin"]).then_inc(s_cs.sem, 16)

            def pe(pt):
                for blk in blks:
                    pe_block(pt, blk)
                pt.wait_ge(*s_unit.at(u))
                for i, (x, bi, ci, (t0, n)) in enumerate(items):
                    pt.wait_ge(*s_evac.at(out_done(blks[bi], ci)))
                    if i >= 2:
                        pt.wait_ge(*s_rope.at(i - 1))
                    pt.matmul(bank[2 + i % 2][:, 0:n], k1("rot"), x[:, t0:t0 + n], start=True, stop=True).then_inc(s_rot.sem, 1)
                pt.wait_ge(*s_evac.at(out_done(blks[1])))
                for f, ns in enumerate(fills):
                    if f == 2:
                        pt.wait_ge(*s_vt.at(1))
                    for m, n in enumerate(ns):
                        mm = pt.transpose(bank[4 + f % 2][:, m * P:(m + 1) * P], Vb[:, n * P:(n + 1) * P], k1("ident"))
                    mm.then_inc(s_tp.sem, 1)
                pt.wait_ge(*s_rope.at(3))
                for f, ns in enumerate(fills):
                    if f == 2:
                        pt.wait_ge(*s_kw.at(1))
                    for m, n in enumerate(ns):
                        mm = pt.transpose(bank[6 + f % 2][:, m * P:(m + 1) * P], Kb[:, n * P:(n + 1) * P], k1("ident"))
                    mm.then_inc(s_tp.sem, 1)
                pt.wait_ge(*s_vt.at(3))
                pt.wait_ge(*s_kw.at(3))
                for f, (d, ns) in enumerate(ufills):
                    if f >= 2:
                        pt.wait_ge(*s_um.at(f - 1))
                    for m, n in enumerate(ns):
                        mm = pt.matmul(bank[4 + f % 2][:, m * P:(m + 1) * P], (KWF, KWB)[d][:, n * P:(n + 1) * P],
                                       VT[:, n * P:(n + 1) * P], start=True, stop=True)
                    mm.then_inc(s_u.sem, 1)

                def scores(g):
                    if g == 0:
                        pt.wait_ge(*s_rope.at(n_rope))
                    else:
                        pt.wait_ge(*s_sc.at(2 * g))
                    for e in range(2):
                        for m, n in enumerate(groups[g]):
                            r = slice(64 * e, 64 * e + 64)
                            mm = pt.matmul(bank[2 + e][:, m * P:(m + 1) * P], Kb[r, n * P:(n + 1) * P], Qb[r, n * P:(n + 1) * P],
                                           start=True, stop=True)
                        mm.then_inc(s_s.sem, 1)

                def outs(g):
                    if g == 0:
                        pt.wait_ge(*s_S.at(1))
                        pt.wait_ge(*s_qf.at(1))
                    if g >= 2:
                        pt.wait_ge(*s_os.at(g - 1))
                    pt.wait_ge(*s_sc.at(2 * g + 2))
                    for m, n in enumerate(groups[g]):
                        o = bank[4 + g % 2][:, m * P:(m + 1) * P]
                        c = slice(n * P, (n + 1) * P)
                        pt.matmul(o, SF[:, c], QF[:, c], start=True, stop=False)
                        pt.matmul(o, SB[:, c], QBK[:, c], start=False, stop=False)
                        for e in range(2):
                            mm = pt.matmul(o[64 * e:64 * e + 64, :], VT[:, n * P + 64 * e:n * P + 64 * e + 64],
                                           SC[:, (m * 2 + e) * P:(m * 2 + e + 1) * P], start=False, stop=True)
                    mm.then_inc(s_o.sem, 1)

                def center(g):
                    w = len(groups[g]) * P
                    pt.wait_ge(*s_os.at(g + 1))
                    if g >= 1:
                        pt.wait_ge(*s_sq.at(g))
                    pt.matmul(bank[6][:, 0:w], k1("center"), UMo[:, 0:w], start=True, stop=True).then_inc(s_cen.sem, 1)

                def var(g):
                    w = len(groups[g]) * P
                    pt.wait_ge(*s_sq.at(g + 1))
                    if g >= 1:
                        pt.wait_ge(*s_rs.at(g))
                    pt.matmul(bank[7][:, 0:w], k1("headmean"), TMP[:, 0:w], start=True, stop=True).then_inc(s_var.sem, 1)

                for g in range(NG):
                    scores(g)
                    if g >= 1:
                        center(g - 1)
                    outs(g)
                    if g >= 1:
                        var(g - 1)
                center(NG - 1)
                var(NG - 1)

            UMo = UM

            def act(a):
                a.wait_ge(*s_unit.at(u))
                for i, blk in enumerate(blks):
                    func, scale = ((ACT.Copy, HD ** -0.5), (ACT.Copy, 1.0), (ACT.Copy, 1.0), (ACT.Silu, 1.0))[i]
                    act_block(a, blk, lambda ci, t0, n, ps: a.activation(PXs[i][:, t0:t0 + n], ps, func, scale=scale))
                for f, ns in enumerate(fills):
                    a.wait_ge(*s_tp.at(f + 1))
                    w = len(ns) * P
                    a.activation(VT[:, ns[0] * P:ns[0] * P + w], bank[4 + f % 2][:, 0:w], ACT.Copy).then_inc(s_vt.sem, 1)
                for g in range(NG):
                    w = len(groups[g]) * P
                    a.wait_ge(*s_o.at(g + 1))
                    if g == 0:
                        a.wait_ge(*s_S.at(1))
                    else:
                        a.wait_ge(*s_yr.at(g))
                    a.activation(UMo[:, 0:w], bank[4 + g % 2][:, 0:w], ACT.Copy).then_inc(s_os.sem, 1)
                    a.wait_ge(*s_cen.at(g + 1))
                    a.activation(UMo[:, 0:w], bank[6][:, 0:w], ACT.Copy).then_inc(s_ac.sem, 1)
                    if g == 0:
                        a.wait_ge(*s_rope.at(n_rope))
                    a.activation(TMP[:, 0:w], bank[6][:, 0:w], ACT.Square).then_inc(s_sq.sem, 1)
                    a.wait_ge(*s_var.at(g + 1))
                    a.activation(TMP[:, 0:w], bank[7][:, 0:w], ACT.Ln, bias=k1("eps")).then_inc(s_ac.sem, 1)
                    a.wait_ge(*s_ac.at(2 * g + 2))
                    a.activation(TMP[:, 0:w], TMP[:, 0:w], ACT.Exp, scale=-0.5).then_inc(s_rs.sem, 1)

            def dve(v):
                ch = dve_chain(v)
                for blk in blks:
                    dve_split(v, blk["b"] + SPLIT)
                v.wait_ge(*s_cs.at(32))
                for i, (x, bi, ci, (t0, n)) in enumerate(items):
                    v.wait_ge(*s_rot.at(i + 1))
                    ch(v.tensor_tensor(TMP[:, 0:n], bank[2 + i % 2][:, 0:n], SIN[:, t0:t0 + n], ALU.mult))
                    ch(v.tensor_tensor(x[:, t0:t0 + n], x[:, t0:t0 + n], COS[:, t0:t0 + n], ALU.mult))
                    v.tensor_tensor(x[:, t0:t0 + n], x[:, t0:t0 + n], TMP[:, 0:n], ALU.add).then_inc(s_rope.sem, 1)
                    v.wait_ge(*s_rope.at(i + 1))
                v.wait_ge(*s_dt[l].at(NDT))
                for f, ns in enumerate(fills):
                    v.wait_ge(*s_tp.at(3 + f + 1))
                    k = len(ns)
                    src = bank[6 + f % 2][:, 0:k * P].rearrange("q (n c) -> q n c", c=P)
                    for d, kw in enumerate((KWF, KWB)):
                        dst = kw[:, ns[0] * P:(ns[0] + k) * P].rearrange("q (n c) -> q n c", c=P)
                        for e in range(2):
                            h = 2 * p + e
                            ins = v.tensor_scalar(dst[:, :, 64 * e:64 * e + 64], src[:, :, 64 * e:64 * e + 64], WK[:, d, h:h + 1], None, ALU.mult)
                            if d == 1 and e == 1:
                                ins.then_inc(s_kw.sem, 1)
                            else:
                                ch(ins)
                v.wait_ge(*s_kw.at(3))
                m = T // P
                v.wait_ge(*s_vt.at(3))
                nq = (T - lo) // P
                wide = lambda x: x[:, lo:T].rearrange("q (n c) -> q n c", c=P)
                ch(v.tensor_tensor(wide(QF), wide(Qb), WQ[:, 0, p, :].unsqueeze(1).to_broadcast([P, nq, P]), ALU.mult))
                v.tensor_tensor(wide(QBK), wide(Qb), WQ[:, 1, p, :].unsqueeze(1).to_broadcast([P, nq, P]), ALU.mult).then_inc(s_qf.sem, 1)
                ch(v.memset(SF[:, 0:P], 0.0))
                ch(v.memset(SB[:, P:2 * P], 0.0))
                mask = k1("pairmask").unsqueeze(1)
                for f, (d, ns) in enumerate(ufills):
                    v.wait_ge(*s_u.at(f + 1))
                    k = len(ns)
                    v.tensor_tensor(UM[:, 0:k * P].rearrange("q (n c) -> q n c", c=P),
                                    bank[4 + f % 2][:, 0:k * P].rearrange("q (n c) -> q n c", c=P),
                                    mask.to_broadcast([P, k, P]), ALU.mult).then_inc(s_um.sem, 1)
                    v.wait_ge(*s_um.at(f + 1))
                    S = (SF, SB)[d]
                    for i, n in enumerate(ns):
                        nxt = n + 1 if d == 0 else (n - 1 if n != 0 else 9)
                        ins = v.scalar_tensor_tensor(S[:, nxt * P:(nxt + 1) * P], S[:, n * P:(n + 1) * P], G128[:, 3 * d + p:3 * d + p + 1],
                                                     UM[:, i * P:(i + 1) * P], ALU.mult, ALU.add)
                        if f == 5 and i == k - 1:
                            ins.then_inc(s_S.sem, 1)
                            v.wait_ge(*s_S.at(1))
                        else:
                            ch(ins)

                def decay(g):
                    k = len(groups[g])
                    for e in range(2):
                        v.wait_ge(*s_s.at(2 * g + e + 1))
                        if g >= 1:
                            v.wait_ge(*s_o.at(g))
                        v.tensor_tensor(SC[:, 0:k * 2 * P].rearrange("q (n f c) -> q n f c", f=2, c=P)[:, :, e, :],
                                        bank[2 + e][:, 0:k * P].rearrange("q (n c) -> q n c", c=P),
                                        DT[:, 2 * p + e, :].unsqueeze(1).to_broadcast([P, k, P]), ALU.mult).then_inc(s_sc.sem, 1)

                def gate(g):
                    w = len(groups[g]) * P
                    t0 = groups[g][0] * P
                    v.wait_ge(*s_rs.at(g + 1))
                    v.wait_ge(*s_ac.at(2 * g + 2))
                    v.tensor_tensor(Y[:, 2 + p, t0:t0 + w], UMo[:, 0:w], TMP[:, 0:w], ALU.mult).then_inc(s_yr.sem, 1)
                    v.wait_ge(*s_yr.at(g + 1))
                    v.wait_ge(*s_evac.at(out_done(blks[3])))
                    ins = v.tensor_tensor(Y[:, 2 + p, t0:t0 + w], Y[:, 2 + p, t0:t0 + w], Gb[:, t0:t0 + w], ALU.mult)
                    if g == NG - 1:
                        ins.then_inc(s_unit.sem, 1)
                        v.wait_ge(*s_unit.at(u + 1))
                    else:
                        ch(ins)

                decay(0)
                for g in range(NG):
                    if g + 1 < NG:
                        decay(g + 1)
                    gate(g)

            return dict(pe=pe, act=act, dve=dve, pool=pool)

        s_pad = [sem(f"pad{l}") for l in range(LAYERS)]

        def rpb_phase():
            st = SC[0:LAYERS * 45, 0:254].rearrange("q (a y) -> q a y", a=2)
            s_z, s_l = sem("padz"), sem("padl")

            def pool(g):
                g.memset(st[:, :, :], 0.0).then_inc(s_z.sem, 1)
                g.wait_ge(*s_z.at(1))
                g.dma_start(st[:, :, 48:48 + RPB_W], I["rpb"]).then_inc(s_l.sem, 16)
                g.wait_ge(*s_l.at(16))
                g.dma_start(scratch["rpb"].ap().rearrange("(r a) y -> r a y", a=2), st[:, :, :]).then_inc(s_pad[0].sem, 16)
                g.wait_ge(*s_pad[0].at(16))

            return dict(pool=pool)

        def na_unit(l, p):
            u = n_units[0]
            n_units[0] += 1
            qch = CHUNKS if l == 0 else MAIN
            blks = [block(I["win"][l, 6 + p], KT, CHUNKS, rhs_hh), block(I["win"][l, 9 + p], KT, CHUNKS, rhs_hh),
                    block(I["win"][l, 18 + p], KT, qch, rhs_hh), block(I["win"][l, 21 + p], KT, qch, rhs_hh)]
            Kb, Vb, X2, Gb = PXs
            VT, L0 = X2, None
            VS = vs_t
            PT, LL = pt_t, l_t
            rows = ([("ctx", r) for r in range(4)] if l == 0 else []) + [("grid", r) for r in range(GRID_H)]
            R = len(rows)
            fills = [("t", range(0, 4)), ("t", range(4, 8)), ("t", range(8, 10)), ("s", range(0, 4)), ("s", range(4, 7))]
            s_f, s_fl, s_nt, s_tp, s_vt = (sem(x, n) for x, n in (("nf", 32), ("nfl", 2), ("nt", 2), ("ntp", 5), ("nvt", 5)))
            s_s, s_m, s_e, s_pn, s_ta, s_tb, s_pa, s_pb, s_o, s_y = (
                sem(x, GRID_H if x == "nta" else R) for x in "ns nm ne npn nta ntb npa npb no ny".split())
            s_z = sem("nz", 1)

            def q0(row):
                return (row[1] * GRID_W) + (CTX if row[0] == "grid" else 0)

            def band(row):
                r = row[1]
                rs = min(max(r - WIN_H // 2, 0), GRID_H - WIN_H)
                return rs, rs - r + WIN_H - 1

            def pool(g):
                g.wait_ge(*s_unit.at(u))
                for e in range(2):
                    off = ((l * 6 + 2 * p + e) * RPB_H) * 127
                    g.dma_start(NF[64 * e:64 * e + 64, :].rearrange("q (d c) -> q d c", c=GRID_W),
                                bass.AP(tensor=scratch["rpb"], offset=off, ap=[[1, 64], [127, RPB_H], [1, GRID_W]])).then_inc(s_f.sem, 16)
                g.memset(QB, 0.0).then_inc(s_z.sem, 1)

            def pe(pt):
                for blk in blks:
                    pe_block(pt, blk)
                pt.wait_ge(*s_unit.at(u))
                pt.wait_ge(*s_f.at(32))
                for c, (a_, n) in enumerate(((0, 512), (512, 448))):
                    pt.matmul(bank[2 + c][:, 0:n], k1("flip64"), NF[:, a_:a_ + n], start=True, stop=True).then_inc(s_fl.sem, 1)
                pt.wait_ge(*s_evac.at(out_done(blks[1])))
                for f, (kind, ns) in enumerate(fills):
                    if f >= 2:
                        pt.wait_ge(*s_vt.at(f - 1))
                    for m, n in enumerate(ns):
                        t0 = n * P if kind == "t" else CTX + 64 + n * P
                        mm = pt.transpose(bank[5 + f % 2][:, m * P:(m + 1) * P], Vb[:, t0:t0 + P], k1("ident"))
                    mm.then_inc(s_tp.sem, 1)
                pt.wait_ge(*s_nt.at(2))
                pt.wait_ge(*s_vt.at(5))
                pt.wait_ge(*s_evac.at(out_done(blks[3])))

                def scores(i):
                    qb = QB[:, rows_at(i) * P:(rows_at(i) + 1) * P]
                    if rows[i][0] == "grid":
                        if i >= 2:
                            pt.wait_ge(*s_m.at(i - 1))
                        rs, _ = band(rows[i])
                        pt.matmul(bank[2 + i % 2][:, :], qb, Kb[:, CTX + rs * GRID_W:CTX + rs * GRID_W + 512], start=True, stop=True)
                    if i >= 1:
                        pt.wait_ge(*s_e.at(i))
                    pt.matmul(bank[4][:, 0:CTX], qb, Kb[:, 0:CTX], start=True, stop=True).then_inc(s_s.sem, 1)

                def turn(i):
                    pt.wait_ge(*s_pn.at(i + 1))
                    pr = PR[i % 2]
                    if i >= 1:
                        pt.wait_ge(*s_pa.at(i))
                        pt.wait_ge(*s_pb.at(i))
                    if rows[i][0] == "grid":
                        for m in range(4):
                            mm = pt.transpose(bank[5][:, m * P:(m + 1) * P], pr[:, m * P:(m + 1) * P], k1("ident"))
                        mm.then_inc(s_ta.sem, 1)
                    for m in range(2):
                        mm = pt.transpose(bank[6][:, m * P:(m + 1) * P], pr[:, (4 + m) * P:(5 + m) * P], k1("ident"))
                    mm.then_inc(s_tb.sem, 1)

                def values(i):
                    pt.wait_ge(*s_pa.at(i + 1))
                    pt.wait_ge(*s_pb.at(i + 1))
                    if i >= 1:
                        pt.wait_ge(*s_y.at(i))
                    rs, _ = band(rows[i])
                    parts = []
                    if rows[i][0] == "grid":
                        for m in range(4):
                            parts.append((m, VT[:, (2 + rs // 2 + m) * P:(3 + rs // 2 + m) * P] if rs % 2 == 0 else
                                          VS[:, (rs // 2 + m) * P:(rs // 2 + m + 1) * P]))
                    parts += [(4 + m, VT[:, m * P:(m + 1) * P]) for m in range(2)]
                    for j, (m, vv) in enumerate(parts):
                        for e in range(2):
                            mm = pt.matmul(bank[7][64 * e:64 * e + 64, 0:64], vv[:, 64 * e:64 * e + 64],
                                           PT[:, m * P + 64 * e:m * P + 64 * e + 64], start=j == 0, stop=j == len(parts) - 1)
                    mm.then_inc(s_o.sem, 1)

                scores(0)
                for i in range(R):
                    if i + 1 < R:
                        scores(i + 1)
                    turn(i)
                    values(i)

            def rows_at(i):
                return q0(rows[i]) // GRID_W

            def act(a):
                a.wait_ge(*s_unit.at(u))
                a.wait_ge(*s_z.at(1))
                for i, blk in enumerate(blks):
                    if i == 2:
                        def evac(ci, t0, n, ps):
                            q = QB[:, (t0 // GRID_W) * P:((t0 + n) // GRID_W) * P].rearrange("q (r c) -> q r c", c=P)
                            s = ps.rearrange("q (r c) -> q r c", c=GRID_W)
                            a.activation(q[0:64, :, 0:64], s[0:64], ACT.Copy, scale=HD ** -0.5)
                            return a.activation(q[64:128, :, 64:128], s[64:128], ACT.Copy, scale=HD ** -0.5)
                        act_block(a, blk, evac)
                    else:
                        act_block(a, blk, lambda ci, t0, n, ps: a.activation(PXs[i][:, t0:t0 + n], ps, ACT.Silu if i == 3 else ACT.Copy))
                for f, (kind, ns) in enumerate(fills):
                    a.wait_ge(*s_tp.at(f + 1))
                    dst = VT if kind == "t" else VS
                    a.activation(dst[:, ns[0] * P:(ns[-1] + 1) * P], bank[5 + f % 2][:, 0:len(ns) * P], ACT.Copy).then_inc(s_vt.sem, 1)

                def exps(i):
                    a.wait_ge(*s_m.at(i + 1))
                    if i >= 2:
                        a.wait_ge(*s_tb.at(i - 1))
                    sm = small[:, 8 * (i % 2):8 * (i % 2) + 8]
                    if rows[i][0] == "grid":
                        a.activation(PR[i % 2][:, 0:512], LL[:, (i % 2) * 512:(i % 2) * 512 + 512], ACT.Exp, bias=sm[:, 2:3],
                                     accum_out=sm[:, 3:4])
                    a.activation(PR[i % 2][:, 512:768], bank[4][:, 0:CTX], ACT.Exp, bias=sm[:, 2:3], accum_out=sm[:, 4:5]).then_inc(s_e.sem, 1)

                def evac_pt(i):
                    if i >= 1:
                        a.wait_ge(*s_o.at(i))
                    if rows[i][0] == "grid":
                        a.wait_ge(*s_ta.at(i + 1 - R + GRID_H))
                        a.activation(PT[:, 0:512], bank[5][:, :], ACT.Copy).then_inc(s_pa.sem, 1)
                    else:
                        a.sem_inc(s_pa.sem, 1)

                exps(0)
                for i in range(R):
                    if i + 1 < R:
                        exps(i + 1)
                    evac_pt(i)

            def dve(v):
                ch = dve_chain(v)
                for blk in blks:
                    dve_split(v, blk["b"] + SPLIT)
                for c, (a_, n) in enumerate(((0, 8), (8, 7))):
                    v.wait_ge(*s_fl.at(c + 1))
                    v.tensor_tensor(NT[:, a_ * 64:(a_ + n) * 64].rearrange("q (d c) -> q d c", c=GRID_W),
                                    bank[2 + c][:, 0:n * 64].rearrange("q (d c) -> q d c", c=GRID_W),
                                    k1("wincol").unsqueeze(1).to_broadcast([P, n, GRID_W]), ALU.add).then_inc(s_nt.sem, 1)
                v.wait_ge(*s_nt.at(2))
                v.wait_ge(*s_vt.at(5))

                def maxes(i):
                    v.wait_ge(*s_s.at(i + 1))
                    if i >= 2:
                        v.wait_ge(*s_e.at(i - 1))
                    sm = small[:, 8 * (i % 2):8 * (i % 2) + 8]
                    ch(v.tensor_reduce(sm[:, 1:2], bank[4][:, 0:CTX], AX_X, ALU.max))
                    if rows[i][0] == "grid":
                        _, dr = band(rows[i])
                        ch(v.tensor_tensor_reduce(out=LL[:, (i % 2) * 512:(i % 2) * 512 + 512], in0=bank[2 + i % 2][:, :],
                                                  in1=NT[:, dr * GRID_W:dr * GRID_W + 512], scale=1.0, scalar=-3.0e38,
                                                  op0=ALU.add, op1=ALU.max, accum_out=sm[:, 0:1]))
                        v.tensor_scalar(sm[:, 2:3], sm[:, 0:1], sm[:, 1:2], -1.0, ALU.max, ALU.mult).then_inc(s_m.sem, 1)
                    else:
                        v.tensor_scalar(sm[:, 2:3], sm[:, 1:2], -1.0, None, ALU.mult).then_inc(s_m.sem, 1)

                def norm(i):
                    v.wait_ge(*s_e.at(i + 1))
                    sm = small[:, 8 * (i % 2):8 * (i % 2) + 8]
                    if rows[i][0] == "grid":
                        ch(v.tensor_tensor(sm[:, 5:6], sm[:, 3:4], sm[:, 4:5], ALU.add))
                        ch(v.reciprocal(sm[:, 6:7], sm[:, 5:6]))
                        lo = 0
                    else:
                        ch(v.reciprocal(sm[:, 6:7], sm[:, 4:5]))
                        lo = 512
                    v.tensor_scalar(PR[i % 2][:, lo:768], PR[i % 2][:, lo:768], sm[:, 6:7], None, ALU.mult).then_inc(s_pn.sem, 1)

                maxes(0)
                for i in range(R):
                    norm(i)
                    if i + 1 < R:
                        maxes(i + 1)
                    v.wait_ge(*s_tb.at(i + 1))
                    if i >= 1:
                        v.wait_ge(*s_o.at(i))
                    v.tensor_copy(PT[:, 512:768], bank[6][:, 0:256]).then_inc(s_pb.sem, 1)
                    v.wait_ge(*s_o.at(i + 1))
                    t0 = q0(rows[i])
                    v.tensor_tensor(Y[:, 5 + p, t0:t0 + GRID_W], bank[7][:, 0:64], Gb[:, t0:t0 + GRID_W], ALU.mult).then_inc(s_y.sem, 1)
                v.wait_ge(*s_y.at(R))
                v.engine_nop().then_inc(s_unit.sem, 1)
                v.wait_ge(*s_unit.at(u + 1))

            return dict(pe=pe, act=act, dve=dve, pool=pool)

        vs_t = sb("VS", [P, 7 * P], F32, b1)
        pt_t = DT[:, :, :].rearrange("q h c -> q (h c)")
        l_t = sb("LL", [P, 1024], F32, b1)

        def out_phase(l):
            chunks = CHUNKS if l == 0 else MAIN
            lo = chunks[0][0]
            u = n_units[0]
            blks = [block(I["wout"][l, m], KT, chunks, rhs_hh) for m in range(KT)]
            NCK = len(chunks)
            s_xs = [sem(f"xs{i}", 8 * KT) for i in range(2)]
            s_hi, s_lo, s_res, s_a = (sem(x, n) for x, n in (("yhi", KT), ("ylo", KT), ("res", KT * NCK), ("lna", NCK)))
            s_mu, s_cen, s_sq, s_var, s_rs, s_n, s_fin = (
                sem(x, n * NCK) for x, n in (("mu", 1), ("cen", KT), ("sq", KT), ("var", KT), ("rstd", 1), ("nrm", KT), ("fin", KT)))
            XS = [PXs[0], PXs[1]]
            SQ = [PXs[2][:, 0:512], PXs[2][:, 512:1024]]
            RS = PXs[3][:, 0:512]
            NCK = len(chunks)

            def pool(g):
                src = I["xt"] if l == 0 else scratch["x1"].ap()
                g.wait_ge(*s_unit.at(u))
                for m in range(KT):
                    if m >= 2:
                        g.wait_ge(*s_res.at(NCK * (m - 1)))
                    g.dma_start(XS[m % 2], src[:, m, :]).then_inc(s_xs[m % 2].sem, 16)
                if True:
                    g.wait_ge(*s_fin.at(NCK * KT))
                    dst = scratch["x1"] if l == 0 else scratch["x2"]
                    g.dma_start(dst.ap(), Y[:, :, :] if l == 0 else Y[:, :, :]).then_inc(s_xst.sem, 16)

            def pe(pt):
                pt.wait_ge(*s_lo.at(KT))
                for blk in blks:
                    pe_block(pt, blk)
                for c, (t0, n) in enumerate(chunks):
                    pt.wait_ge(*s_res.at(NCK * KT))
                    for m in range(KT):
                        mm = pt.matmul(bank[2][:, 0:n], k1("mean"), Y[:, m, t0:t0 + n], start=m == 0, stop=m == KT - 1)
                    mm.then_inc(s_mu.sem, 1)
                    if c:
                        pt.wait_ge(*s_rs.at(c))
                    for m in range(KT):
                        pt.wait_ge(*s_sq.at(c * KT + m + 1))
                        mm = pt.matmul(bank[3][:, 0:n], k1("mean"), SQ[m % 2][:, 0:n], start=m == 0, stop=m == KT - 1)
                        if m == KT - 1:
                            mm.then_inc(s_var.sem, 1)
                        else:
                            mm.then_inc(s_var.sem, 1)

            def act(a):
                a.wait_ge(*s_unit.at(u))
                for k in range(KT):
                    a.activation(HH[:, 0, k, lo:], Y[:, k, lo:], ACT.Copy).then_inc(s_hi.sem, 1)
                a.wait_ge(*s_lo.at(KT))
                for m, blk in enumerate(blks):
                    def evac(ci, t0, n, ps):
                        w = 1 if t0 < CTX else 0
                        return a.activation(Y[:, m, t0:t0 + n], ps, ACT.Copy, scale=modv[:, l, 16 + m, w:w + 1])
                    act_block(a, blk, evac)
                for c, (t0, n) in enumerate(chunks):
                    for m in range(KT):
                        a.wait_ge(*s_cen.at(c * KT + m + 1))
                        i = c * KT + m
                        if i >= 2:
                            a.wait_ge(*s_var.at(i - 1))
                        a.activation(SQ[m % 2][:, 0:n], Y[:, m, t0:t0 + n], ACT.Square).then_inc(s_sq.sem, 1)
                    a.wait_ge(*s_var.at((c + 1) * KT))
                    if c:
                        a.wait_ge(*s_n.at(c * KT))
                    a.activation(RS[:, 0:n], bank[3][:, 0:n], ACT.Ln, bias=k1("eps")).then_inc(s_a.sem, 1)
                    a.wait_ge(*s_a.at(c + 1))
                    a.activation(RS[:, 0:n], RS[:, 0:n], ACT.Exp, scale=-0.5).then_inc(s_rs.sem, 1)
                    for m in range(KT):
                        a.wait_ge(*s_n.at(c * KT + m + 1))
                        a.activation(Y[:, m, t0:t0 + n], Y[:, m, t0:t0 + n], ACT.Identity, scale=lnp[:, l, 0, m:m + 1],
                                     bias=lnp[:, l, 1, m:m + 1]).then_inc(s_fin.sem, 1)

            def dve(v):
                ch = dve_chain(v)
                for k in range(KT):
                    v.wait_ge(*s_hi.at(k + 1))
                    v.tensor_tensor(HH[:, 1, k, lo:], Y[:, k, lo:], HH[:, 0, k, lo:].bitcast(F32), ALU.subtract).then_inc(s_lo.sem, 1)
                for m, blk in enumerate(blks):
                    dve_split(v, blk["b"] + SPLIT)
                    v.wait_ge(*s_xs[m % 2].at(16 * (m // 2 + 1)))
                    for ci, (t0, n) in enumerate(chunks):
                        v.wait_ge(*s_evac.at(out_done(blk, ci)))
                        v.scalar_tensor_tensor(Y[:, m, t0:t0 + n], XS[m % 2][:, t0:t0 + n], ALPHA, Y[:, m, t0:t0 + n],
                                               ALU.mult, ALU.add).then_inc(s_res.sem, 1)
                v.wait_ge(*s_res.at(NCK * KT))
                for c, (t0, n) in enumerate(chunks):
                    v.wait_ge(*s_mu.at(c + 1))
                    for m in range(KT):
                        v.tensor_tensor(Y[:, m, t0:t0 + n], Y[:, m, t0:t0 + n], bank[2][:, 0:n], ALU.subtract).then_inc(s_cen.sem, 1)
                    v.wait_ge(*s_cen.at((c + 1) * KT))
                    v.wait_ge(*s_rs.at(c + 1))
                    for m in range(KT):
                        v.tensor_tensor(Y[:, m, t0:t0 + n], Y[:, m, t0:t0 + n], RS[:, 0:n], ALU.mult).then_inc(s_n.sem, 1)

            return dict(pe=pe, act=act, dve=dve, pool=pool, s_fin=s_fin, n_fin=NCK * KT)

        if upto != "mod":
            phases.append(rpb_phase())
        ready = (s_x0, 16)
        for l in range(LAYERS):
            phases.append(start_phase(l, *ready))
            for c in range(2):
                phases.append(conv_unit(l, c))
            for p in range(PAIRS):
                phases.append(ret_unit(l, p))
            for p in range(PAIRS):
                phases.append(na_unit(l, p))
            if upto == f"branches{l}":
                break
            ph = out_phase(l)
            phases.append(ph)
            ready = (ph["s_fin"], ph["n_fin"])
            if upto == f"layer{l}":
                break
        debug = upto is not None and (upto.startswith("branches") or upto.startswith("layer"))

        if not debug:
            M2 = [(0, 512), (512, 512)]
            X = lambda m, t0, n: Y[:, m, CTX + t0:CTX + t0 + n]
            b1.close()
            b2 = top.enter_context(ExitStack())
            H2 = sb("H2", [P, 2, KT, SEQ], F32R, b2)
            c2 = sb("c2", [P, N2], F32, b2)
            ar2_n = 17536
            ar2 = sb("ar2", [P, ar2_n], F32, b2)
            wba = sb("wba", [P, KT, 8], F32, b2)
            wbas = sb("wbas", [P, 2, KT, 8], F32R, b2)
            cw2 = sb("cw2", [P, 12, 4], F32, b2)
            gsm = sb("gsm", [P, 16, 32], F32, b2)
            hrow = sb("hrow", [P, 9], F32, b2)
            rhs_h2 = lambda part, k, t0, n: H2[:, part, k, t0:t0 + n]

            def k2(name):
                a, n = C2[name]
                return c2[:, a:a + n]

            s_c2 = sem("const2")

            def consts2_phase():
                def pool(g):
                    g.wait_ge(*ready[0].at(ready[1]))
                    g.dma_start(c2[:, :], I["c2"]).then_inc(s_c2.sem, 16)
                    g.dma_start(gp2[:, :, :], I["gp2"]).then_inc(s_c2.sem, 16)
                    g.dma_start(wba[:, :, :], I["wba"]).then_inc(s_c2.sem, 16)
                    g.dma_start(cw2[:, :, :], I["cw2"]).then_inc(s_c2.sem, 16)
                    for i, nm in enumerate(("dtb_t", "alog_t")):
                        g.dma_start(hrow[:, 4 * i:4 * i + 4], bass.AP(tensor=I[nm], offset=0, ap=[[0, P], [1, 4]])).then_inc(s_c2.sem, 16)
                    g.dma_start(hrow[:, 8:9], I["onorm"]).then_inc(s_c2.sem, 16)
                return dict(pool=pool)

            NC = 7 * 16

            def rms_in(gi, chunks, dst, sq, rs, tt, mean, eps, s_from, first_bank):
                nk = len(chunks) * KT
                s_sq, s_var, s_rt, s_hi, s_lo = (sem(x, nk) for x in "r_sq r_var r_t r_hi r_lo".split())
                s_rs, s_ln = sem("r_rs", len(chunks)), sem("r_ln", len(chunks))

                def act(a):
                    a.wait_ge(*s_c2.at(NC))
                    a.wait_ge(*s_from)
                    i = 0
                    for c, (t0, n) in enumerate(chunks):
                        for m in range(KT):
                            if i >= 2:
                                a.wait_ge(*s_var.at(i - 1))
                            a.activation(sq[m % 2][:, 0:n], X(m, t0, n), ACT.Square).then_inc(s_sq.sem, 1)
                            i += 1
                        a.wait_ge(*s_var.at((c + 1) * KT))
                        if c:
                            a.wait_ge(*s_rt.at(c * KT))
                        a.activation(rs[:, 0:n], bank[first_bank][:, 0:n], ACT.Ln, bias=eps).then_inc(s_ln.sem, 1)
                        a.wait_ge(*s_ln.at(c + 1))
                        a.activation(rs[:, 0:n], rs[:, 0:n], ACT.Exp, scale=-0.5).then_inc(s_rs.sem, 1)
                        for m in range(KT):
                            a.wait_ge(*s_rt.at(c * KT + m + 1))
                            a.activation(dst(0, m, t0, n), tt[m % 2][:, 0:n], ACT.Copy).then_inc(s_hi.sem, 1)

                def pe(p):
                    p.wait_ge(*s_c2.at(NC))
                    for c, (t0, n) in enumerate(chunks):
                        if c:
                            p.wait_ge(*s_rs.at(c))
                        for m in range(KT):
                            p.wait_ge(*s_sq.at(c * KT + m + 1))
                            p.matmul(bank[first_bank][:, 0:n], mean, sq[m % 2][:, 0:n], start=m == 0, stop=m == KT - 1).then_inc(s_var.sem, 1)
                    p.wait_ge(*s_lo.at(nk))

                def dve(v):
                    i = 0
                    for c, (t0, n) in enumerate(chunks):
                        v.wait_ge(*s_rs.at(c + 1))
                        for m in range(KT):
                            if i >= 2:
                                v.wait_ge(*s_lo.at(i - 1))
                            v.scalar_tensor_tensor(tt[m % 2][:, 0:n], X(m, t0, n), gp2[:, gi, m:m + 1], rs[:, 0:n], ALU.mult, ALU.mult).then_inc(s_rt.sem, 1)
                            i += 1
                            v.wait_ge(*s_hi.at(i))
                            v.tensor_tensor(dst(1, m, t0, n), tt[m % 2][:, 0:n], dst(0, m, t0, n).bitcast(F32), ALU.subtract).then_inc(s_lo.sem, 1)

                return dict(act=act, pe=pe, dve=dve, s_sq=s_sq, n=nk, s_lo=s_lo)

            def rms_out(gi, chunks, src, add, sq, rs, mean, eps, s_from, s_add, first_bank):
                nk = len(chunks) * KT
                s_sq, s_var, s_t, s_x = (sem(x, nk) for x in "p_sq p_var p_t p_x".split())
                s_rs, s_ln = sem("p_rs", len(chunks)), sem("p_ln", len(chunks))

                def act(a):
                    a.wait_ge(*s_from)
                    i = 0
                    for c, (t0, n) in enumerate(chunks):
                        for m in range(KT):
                            if i >= 2:
                                a.wait_ge(*s_var.at(i - 1))
                            a.activation(sq[m % 2][:, 0:n], src(m, t0, n), ACT.Square).then_inc(s_sq.sem, 1)
                            i += 1
                        a.wait_ge(*s_var.at((c + 1) * KT))
                        if c:
                            a.wait_ge(*s_t.at(c * KT))
                        a.activation(rs[:, 0:n], bank[first_bank][:, 0:n], ACT.Ln, bias=eps).then_inc(s_ln.sem, 1)
                        a.wait_ge(*s_ln.at(c + 1))
                        a.activation(rs[:, 0:n], rs[:, 0:n], ACT.Exp, scale=-0.5).then_inc(s_rs.sem, 1)

                def pe(p):
                    for c, (t0, n) in enumerate(chunks):
                        if c:
                            p.wait_ge(*s_rs.at(c))
                        for m in range(KT):
                            p.wait_ge(*s_sq.at(c * KT + m + 1))
                            p.matmul(bank[first_bank][:, 0:n], mean, sq[m % 2][:, 0:n], start=m == 0, stop=m == KT - 1).then_inc(s_var.sem, 1)

                def dve(v):
                    for c, (t0, n) in enumerate(chunks):
                        v.wait_ge(*s_rs.at(c + 1))
                        for m in range(KT):
                            s = src(m, t0, n)
                            v.scalar_tensor_tensor(s, s, gp2[:, gi, m:m + 1], rs[:, 0:n], ALU.mult, ALU.mult).then_inc(s_t.sem, 1)
                            if s_add is not None:
                                v.wait_ge(*s_add(m))
                            v.wait_ge(*s_t.at(c * KT + m + 1))
                            v.tensor_tensor(X(m, t0, n), s, add(m, t0, n), ALU.add).then_inc(s_x.sem, 1)

                return dict(act=act, pe=pe, dve=dve, s_x=s_x, n=nk)

            phases.append(consts2_phase())
            A2 = lambda i, n=1: ar2[:, i * 1024:(i + n) * 1024]
            half2 = lambda t: [t[:, 0:512], t[:, 512:1024]]
            r1 = rms_in(0, M2, lambda part, m, t0, n: H2[:, part, m, t0:t0 + n], half2(A2(0)), A2(1)[:, 0:512], half2(A2(2)),
                        k2("mean"), k2("eps"), ready[0].at(ready[1]), 2)
            phases.append(r1)

            s_ba, s_bam, s_baa, s_bad, s_wb = sem("ba"), sem("bam"), sem("baa"), sem("bad"), sem("wb")
            v3 = lambda i: gsm[:, i, :].rearrange("q (n h) -> q n h", h=GH)
            LBA = gsm[:, 0:2, :].rearrange("q a c -> q (a c)").rearrange("q (n c) -> q n c", c=8)
            BETA, Z, EZ, SP, TT, GG, GC, EGC, BE = (v3(i) for i in range(2, 11))
            EA = gsm[:, 11, 0:4]

            def ba_phase():
                def act(a):
                    a.activation(wbas[:, 0, :, :], wba[:, :, :], ACT.Copy).then_inc(s_wb.sem, 1)
                    a.wait_ge(*s_bam.at(1))
                    a.activation(LBA, bank[3][:, 0:64].rearrange("q (n c) -> q n c", c=8), ACT.Copy).then_inc(s_baa.sem, 1)
                    a.wait_ge(*s_baa.at(1))
                    a.activation(BETA, LBA[:, :, 0:4], ACT.Sigmoid).then_inc(s_baa.sem, 1)
                    a.activation(EA, hrow[:, 4:8], ACT.Exp).then_inc(s_baa.sem, 1)
                    a.wait_ge(*s_bad.at(1))
                    a.activation(EZ, TT, ACT.Exp).then_inc(s_baa.sem, 1)
                    a.wait_ge(*s_baa.at(4))
                    a.activation(SP, EZ, ACT.Ln, bias=1.0).then_inc(s_baa.sem, 1)
                    a.wait_ge(*s_bam.at(2))
                    a.activation(GC, bank[4][:, 0:32].rearrange("q (n h) -> q n h", h=GH), ACT.Copy).then_inc(s_baa.sem, 1)
                    a.wait_ge(*s_baa.at(6))
                    a.activation(EGC, GC, ACT.Exp).then_inc(s_baa.sem, 1)

                def pe(p):
                    p.wait_ge(*s_ba.at(1))
                    for n in range(NC2):
                        for k in range(KT):
                            for part, (wp, xp) in enumerate(((0, 0), (0, 1), (1, 0))):
                                mm = p.matmul(bank[3][:, 8 * n:8 * n + 8], H2[:, xp, k, n * P:(n + 1) * P], wbas[:, wp, k, :],
                                              start=k == 0 and part == 0, stop=k == KT - 1 and part == 2)
                    mm.then_inc(s_bam.sem, 1)
                    p.wait_ge(*s_ba.at(2))
                    p.matmul(bank[4][:, 0:32], k2("upto"), gsm[:, 7, :], start=True, stop=True).then_inc(s_bam.sem, 1)

                def dve(v):
                    ch = dve_chain(v)
                    v.wait_ge(*s_wb.at(1))
                    v.tensor_tensor(wbas[:, 1, :, :], wba[:, :, :], wbas[:, 0, :, :].bitcast(F32), ALU.subtract).then_inc(s_ba.sem, 1)
                    v.wait_ge(*s_baa.at(1))
                    ch(v.tensor_tensor(Z, LBA[:, :, 4:8], hrow[:, 0:4].unsqueeze(1).to_broadcast([P, NC2, GH]), ALU.add))
                    v.scalar_tensor_tensor(TT, Z, -1.0, Z, ALU.mult, ALU.min).then_inc(s_bad.sem, 1)
                    v.wait_ge(*s_baa.at(5))
                    ch(v.tensor_scalar(TT, EZ, 1.0, -1.0, ALU.add, ALU.add))
                    ch(v.tensor_scalar(TT, TT, 1e-30, None, ALU.max))
                    ch(v.reciprocal(TT, TT))
                    ch(v.tensor_tensor(TT, TT, EZ, ALU.mult))
                    ch(v.tensor_tensor(SP, SP, TT, ALU.mult))
                    ch(v.tensor_scalar(TT, EZ, -0.5, 1.0, ALU.mult, ALU.add))
                    ch(v.tensor_tensor(TT, TT, EZ, ALU.mult))
                    ch(v.tensor_tensor(SP, SP, TT, ALU.max))
                    ch(v.scalar_tensor_tensor(SP, Z, 0.0, SP, ALU.max, ALU.add))
                    v.scalar_tensor_tensor(GG, SP, -1.0, EA.unsqueeze(1).to_broadcast([P, NC2, GH]), ALU.mult, ALU.mult).then_inc(s_ba.sem, 1)
                    v.wait_ge(*s_baa.at(7))
                    v.tensor_tensor(BE, BETA, EGC, ALU.mult).then_inc(s_ba.sem, 1)
                    v.wait_ge(*s_ba.at(3))

                return dict(act=act, pe=pe, dve=dve)

            phases.append(ba_phase())

            def gdn_unit(hd):
                u = n_units[0]
                n_units[0] += 1
                blks = [block(I["win2"][0, 4 * i + hd], KT, M2, rhs_h2) for i in range(4)]
                Q, K, V, TA, TB_, KBG, KD, VB, GB, EG, ATT, DD, AT, XX, XT, YT = (A2(i) for i in range(16))
                QD, OT, U, WT = EG, TB_, V, TA
                SS = ar2[:, 16 * 1024:16 * 1024 + 256]
                GE, KDC = gsm[:, 12, 0:8], gsm[:, 13, 0:8]
                w4 = lambda t, hf: t[:, 512 * hf:512 * hf + 512].rearrange("q (n c) -> q n c", c=P)
                ch_ = lambda t, n: t[:, n * P:(n + 1) * P]
                bk = lambda i: bank[i][:, :].rearrange("q (n c) -> q n c", c=P)
                tokcol = lambda t, hf: t[:, 4 * hf:4 * hf + 4, hd].unsqueeze(2).to_broadcast([P, 4, P])
                rowc = lambda nm: k2(nm).unsqueeze(1).to_broadcast([P, 4, P])
                LV = INV_LEVELS - 1
                names = dict(g_gb=2, g_gbc=2, g_eg=2, g_conv=3, g_silu=3, g_sq=2, g_ss=4, g_rs=4, g_n=2, g_kd=1, g_kdc=1, g_tp=4, g_tk=2, g_tv=2,
                             g_d=4, g_dx=4, g_qk=4, g_att=2, g_a=2, g_tat=2, g_at=2, g_ot=2 * LV, g_py=2 * LV, g_y=2 * LV, g_pz=2 * LV,
                             g_x=2 * LV + 2, g_uw=4, g_u=4, g_S=NC2, g_ws=NC2, g_vn=NC2, g_kv=NC2, g_o=NC2, g_os=2, g_ov=2, g_ol=4, g_or=2)
                s = {k: sem(k, n) for k, n in names.items()}

                def pe(p):
                    for blk in blks:
                        pe_block(p, blk)
                    p.wait_ge(*s_unit.at(u))
                    p.wait_ge(*s_ba.at(3))
                    for hf in range(2):
                        for j in range(4):
                            n = 4 * hf + j
                            mm = p.matmul(bank[2 + hf][:, j * P:(j + 1) * P], GG[:, n, hd:hd + 1].to_broadcast([P, P]), k2("upto"), start=True, stop=True)
                        mm.then_inc(s["g_gb"].sem, 1)
                    for i in range(2):
                        p.wait_ge(*s["g_sq"].at(i + 1))
                        for hf in range(2):
                            p.matmul(bank[4 + 2 * i + hf][:, :], k2("ones"), (TB_, TA)[i][:, 512 * hf:512 * hf + 512], start=True, stop=True).then_inc(s["g_ss"].sem, 1)
                    p.wait_ge(*s["g_gbc"].at(2))
                    p.wait_ge(*s["g_n"].at(2))
                    for hf in range(2):
                        for j in range(4):
                            mm = p.transpose(bank[2 + hf][:, j * P:(j + 1) * P], ch_(K, 4 * hf + j), k2("ident"))
                        mm.then_inc(s["g_tp"].sem, 1)
                    p.wait_ge(*s["g_silu"].at(3))
                    for hf in range(2):
                        for j in range(4):
                            mm = p.transpose(bank[4 + hf][:, j * P:(j + 1) * P], ch_(V, 4 * hf + j), k2("ident"))
                        mm.then_inc(s["g_tp"].sem, 1)
                    for hf in range(2):
                        for j in range(4):
                            n = 4 * hf + j
                            mm = p.matmul(bank[6 + hf][:, j * P:(j + 1) * P], ch_(K, n), ch_(Q, n), start=True, stop=True)
                        mm.then_inc(s["g_qk"].sem, 1)
                    for hf in range(2):
                        p.wait_ge(*s["g_tk"].at(hf + 1))
                        for j in range(4):
                            n = 4 * hf + j
                            mm = p.matmul(bank[2 + hf][:, j * P:(j + 1) * P], ch_(K, n), ch_(K, n), start=True, stop=True)
                        mm.then_inc(s["g_qk"].sem, 1)
                    for hf in range(2):
                        p.wait_ge(*s["g_tv"].at(hf + 1))
                        p.wait_ge(*s["g_a"].at(hf + 1))
                        for j in range(4):
                            mm = p.transpose(bank[4 + hf][:, j * P:(j + 1) * P], ch_(DD, 4 * hf + j), k2("ident"))
                        mm.then_inc(s["g_tat"].sem, 1)
                    for k in range(LV):
                        for hf in range(2):
                            p.wait_ge(*s["g_ot"].at(2 * k + hf + 1))
                            p.wait_ge(*s["g_x"].at(2 * k + hf + 1))
                            for j in range(4):
                                n = 4 * hf + j
                                mm = p.matmul(bank[2 + hf][:, j * P:(j + 1) * P], ch_(OT, n), ch_(XX, n), start=True, stop=True)
                            mm.then_inc(s["g_py"].sem, 1)
                        for hf in range(2):
                            p.wait_ge(*s["g_y"].at(2 * k + hf + 1))
                            for j in range(4):
                                n = 4 * hf + j
                                if k < LV - 1:
                                    p.matmul(bank[4 + hf][:, j * P:(j + 1) * P], ch_(XT, n), ch_(YT, n), start=True, stop=True)
                                mm = p.matmul(bank[6 + hf][:, j * P:(j + 1) * P], ch_(YT, n), ch_(XT, n), start=True, stop=True)
                            mm.then_inc(s["g_pz"].sem, 1)
                    for hf in range(2):
                        p.wait_ge(*s["g_x"].at(2 * LV + hf + 1))
                        for j in range(4):
                            n = 4 * hf + j
                            mm = p.matmul(bank[2 + hf][:, j * P:(j + 1) * P], ch_(XT, n), ch_(VB, n), start=True, stop=True)
                        mm.then_inc(s["g_uw"].sem, 1)
                        for j in range(4):
                            n = 4 * hf + j
                            mm = p.matmul(bank[4 + hf][:, j * P:(j + 1) * P], ch_(KBG, n), ch_(XT, n), start=True, stop=True)
                        mm.then_inc(s["g_uw"].sem, 1)
                    p.wait_ge(*s["g_u"].at(4))
                    for n in range(NC2):
                        S = SS[:, (n % 2) * P:(n % 2 + 1) * P]
                        p.wait_ge(*s["g_S"].at(n + 1))
                        p.matmul(bank[6 + n % 2][:, 0:P], ch_(WT, n), S, start=True, stop=True).then_inc(s["g_ws"].sem, 1)
                        p.wait_ge(*s["g_vn"].at(n + 1))
                        p.matmul(bank[2 + n % 2][:, 0:P], ch_(KD, n), ch_(U, n), start=True, stop=True).then_inc(s["g_kv"].sem, 1)
                        o = bank[4 + n // 4][:, (n % 4) * P:(n % 4 + 1) * P]
                        p.matmul(o, S, ch_(QD, n), start=True, stop=False)
                        p.matmul(o, ch_(U, n), ch_(ATT, n), start=False, stop=True).then_inc(s["g_o"].sem, 1)
                    for hf in range(2):
                        p.wait_ge(*s["g_os"].at(hf + 1))
                        p.matmul(bank[6 + hf][:, :], k2("headmean"), AT[:, 512 * hf:512 * hf + 512], start=True, stop=True).then_inc(s["g_ov"].sem, 1)

                def act(a):
                    a.wait_ge(*s_unit.at(u))
                    if hd == 0:
                        a.wait_ge(*s_xst.at(32))
                        a.wait_ge(*r1["s_lo"].at(r1["n"]))
                    dst = [Q, K, V]
                    for i, blk in enumerate(blks):
                        act_block(a, blk, lambda ci, t0, n, ps: a.activation(X(hd, t0, n) if i == 3 else dst[i][:, t0:t0 + n], ps, ACT.Silu if i == 3 else ACT.Copy))
                    for i, x in enumerate((Q, K, V)):
                        a.wait_ge(*s["g_conv"].at(i + 1))
                        a.activation(x, (TA, TB_, KBG)[i], ACT.Silu).then_inc(s["g_silu"].sem, 1)
                    for i, x in enumerate((Q, K)):
                        a.wait_ge(*s["g_silu"].at(3))
                        a.activation((TB_, TA)[i], x, ACT.Square).then_inc(s["g_sq"].sem, 1)
                    for hf in range(2):
                        a.wait_ge(*s["g_gb"].at(hf + 1))
                        a.activation(GB[:, 512 * hf:512 * hf + 512], bank[2 + hf][:, :], ACT.Copy).then_inc(s["g_gbc"].sem, 1)
                    a.wait_ge(*s["g_gbc"].at(2))
                    last = GB.rearrange("q (n c) -> q n c", c=P)[:, :, P - 1]
                    a.activation(GE, last, ACT.Exp).then_inc(s["g_eg"].sem, 1)
                    a.activation(EG, GB, ACT.Exp).then_inc(s["g_eg"].sem, 1)
                    a.wait_ge(*s["g_kd"].at(1))
                    a.activation(KDC, KDC, ACT.Exp).then_inc(s["g_kdc"].sem, 1)
                    for i in range(2):
                        for hf in range(2):
                            a.wait_ge(*s["g_ss"].at(2 * i + hf + 1))
                            t = (TB_, TA)[i][:, 512 * hf:512 * hf + 512]
                            a.activation(t, bank[4 + 2 * i + hf][:, :], ACT.Ln, bias=k2("eps")).then_inc(s_gln.sem, 1)
                            a.wait_ge(*s_gln.at(4 * hd + 2 * i + hf + 1))
                            a.activation(t, t, ACT.Exp, scale=-0.5).then_inc(s["g_rs"].sem, 1)
                    for i, t in enumerate((XX, DD)):
                        for hf in range(2):
                            a.wait_ge(*s["g_d"].at(2 * i + hf + 1))
                            a.activation(w4(t, hf), w4(t, hf), ACT.Exp).then_inc(s["g_dx"].sem, 1)
                    for hf in range(2):
                        a.wait_ge(*s["g_tat"].at(hf + 1))
                        a.activation(w4(AT, hf), bk(4 + hf), ACT.Copy).then_inc(s["g_at"].sem, 1)
                    for k in range(LV):
                        for hf in range(2):
                            a.wait_ge(*s["g_py"].at(2 * k + hf + 1))
                            a.activation(w4(YT, hf), bk(2 + hf), ACT.Copy).then_inc(s["g_y"].sem, 1)
                    for hf in range(2):
                        a.wait_ge(*s["g_uw"].at(2 * hf + 1))
                        a.activation(w4(U, hf), bk(2 + hf), ACT.Copy).then_inc(s["g_u"].sem, 1)
                        a.wait_ge(*s["g_uw"].at(2 * hf + 2))
                        a.activation(w4(WT, hf), bk(4 + hf), ACT.Copy).then_inc(s["g_u"].sem, 1)
                    for hf in range(2):
                        a.wait_ge(*s["g_o"].at(4 * hf + 4))
                        a.activation(w4(DD, hf), bk(4 + hf), ACT.Copy).then_inc(s["g_ol"].sem, 1)
                        a.activation(w4(AT, hf), bk(4 + hf), ACT.Square).then_inc(s["g_os"].sem, 1)
                    for hf in range(2):
                        a.wait_ge(*s["g_ov"].at(hf + 1))
                        a.activation(w4(AT, hf), bk(6 + hf), ACT.Ln, bias=k2("eps")).then_inc(s["g_ol"].sem, 1)
                        a.wait_ge(*s["g_ol"].at(2 + hf + 1))
                        a.activation(w4(AT, hf), w4(AT, hf), ACT.Exp, scale=-0.5).then_inc(s["g_or"].sem, 1)

                def dve(v):
                    ch = dve_chain(v)
                    for blk in blks:
                        dve_split(v, blk["b"] + SPLIT)
                    for i, x in enumerate((Q, K, V)):
                        v.wait_ge(*s_evac.at(out_done(blks[i])))
                        t = (TA, TB_, KBG)[i]
                        w = cw2[:, 4 * i + hd, :]
                        ch(v.tensor_scalar(t, x, w[:, 3:4], None, ALU.mult))
                        for j in range(1, 4):
                            ins = v.scalar_tensor_tensor(t[:, j:], x[:, 0:SEQ - j], w[:, 3 - j:4 - j], t[:, j:], ALU.mult, ALU.add)
                            if j == 3:
                                ins.then_inc(s["g_conv"].sem, 1)
                            else:
                                ch(ins)
                    v.wait_ge(*s["g_gbc"].at(2))
                    last = GB.rearrange("q (n c) -> q n c", c=P)[:, :, P - 1]
                    v.tensor_tensor(KDC, last, GC[:, :, hd], ALU.subtract).then_inc(s["g_kd"].sem, 1)
                    for hf in range(2):
                        ch(v.tensor_tensor(w4(XX, hf), w4(GB, hf), tokcol(GC, hf), ALU.subtract))
                        v.tensor_tensor(w4(XX, hf), w4(XX, hf), rowc("causalT"), ALU.add).then_inc(s["g_d"].sem, 1)
                    for hf in range(2):
                        ch(v.tensor_tensor(w4(DD, hf), tokcol(GC, hf), w4(GB, hf), ALU.subtract))
                        v.tensor_tensor(w4(DD, hf), w4(DD, hf), rowc("strict"), ALU.add).then_inc(s["g_d"].sem, 1)
                    v.wait_ge(*s["g_rs"].at(2))
                    v.scalar_tensor_tensor(Q, Q, float(P) ** -0.5, TB_, ALU.mult, ALU.mult).then_inc(s["g_n"].sem, 1)
                    v.wait_ge(*s["g_rs"].at(4))
                    v.tensor_tensor(K, K, TA, ALU.mult).then_inc(s["g_n"].sem, 1)
                    v.wait_ge(*s["g_eg"].at(2))
                    v.wait_ge(*s["g_n"].at(2))
                    ch(v.tensor_tensor(QD, EG, Q, ALU.mult))
                    v.wait_ge(*s["g_kdc"].at(1))
                    for hf in range(2):
                        v.wait_ge(*s["g_tp"].at(hf + 1))
                        ch(v.tensor_tensor(w4(KBG, hf), bk(2 + hf), tokcol(BE, hf), ALU.mult))
                        v.tensor_tensor(w4(KD, hf), bk(2 + hf), KDC[:, 4 * hf:4 * hf + 4].unsqueeze(2).to_broadcast([P, 4, P]), ALU.mult).then_inc(s["g_tk"].sem, 1)
                    for hf in range(2):
                        v.wait_ge(*s["g_tp"].at(2 + hf + 1))
                        v.tensor_tensor(w4(VB, hf), bk(4 + hf), tokcol(BETA, hf), ALU.mult).then_inc(s["g_tv"].sem, 1)
                    for hf in range(2):
                        v.wait_ge(*s["g_qk"].at(hf + 1))
                        v.wait_ge(*s["g_dx"].at(hf + 1))
                        v.tensor_tensor(w4(ATT, hf), bk(6 + hf), w4(XX, hf), ALU.mult).then_inc(s["g_att"].sem, 1)
                    for hf in range(2):
                        v.wait_ge(*s["g_dx"].at(2 + hf + 1))
                        ch(v.tensor_tensor(w4(DD, hf), w4(DD, hf), tokcol(BETA, hf), ALU.mult))
                        v.wait_ge(*s["g_qk"].at(2 + hf + 1))
                        v.tensor_tensor(w4(DD, hf), bk(2 + hf), w4(DD, hf), ALU.mult).then_inc(s["g_a"].sem, 1)
                    v.wait_ge(*s["g_att"].at(2))
                    v.wait_ge(*s["g_a"].at(2))
                    for hf in range(2):
                        ch(v.tensor_tensor(w4(XX, hf), w4(DD, hf), rowc("low0"), ALU.mult))
                        ch(v.tensor_tensor(w4(XX, hf), rowc("ident"), w4(XX, hf), ALU.subtract))
                        v.wait_ge(*s["g_at"].at(hf + 1))
                        ch(v.tensor_tensor(w4(XT, hf), w4(AT, hf), rowc("lowT0"), ALU.mult))
                        v.tensor_tensor(w4(XT, hf), rowc("ident"), w4(XT, hf), ALU.subtract).then_inc(s["g_x"].sem, 1)
                    for k in range(LV):
                        for hf in range(2):
                            if k:
                                v.wait_ge(*s["g_py"].at(2 * (k - 1) + hf + 1))
                            v.tensor_tensor(w4(OT, hf), w4(AT, hf), rowc(f"lowT{k + 1}"), ALU.mult).then_inc(s["g_ot"].sem, 1)
                        for hf in range(2):
                            v.wait_ge(*s["g_pz"].at(2 * k + hf + 1))
                            v.wait_ge(*s["g_x"].at(2 * k + hf + 1))
                            if k < LV - 1:
                                ch(v.tensor_tensor(w4(XX, hf), w4(XX, hf), bk(4 + hf), ALU.subtract))
                            v.tensor_tensor(w4(XT, hf), w4(XT, hf), bk(6 + hf), ALU.subtract).then_inc(s["g_x"].sem, 1)
                    v.memset(SS, 0.0).then_inc(s["g_S"].sem, 1)
                    v.wait_ge(*s["g_u"].at(4))
                    v.wait_ge(*s["g_S"].at(1))
                    for n in range(NC2):
                        v.wait_ge(*s["g_ws"].at(n + 1))
                        v.tensor_tensor(ch_(U, n), ch_(U, n), bank[6 + n % 2][:, 0:P], ALU.subtract).then_inc(s["g_vn"].sem, 1)
                        if n + 1 < NC2:
                            v.wait_ge(*s["g_kv"].at(n + 1))
                            v.wait_ge(*s["g_S"].at(n + 1))
                            v.scalar_tensor_tensor(SS[:, ((n + 1) % 2) * P:((n + 1) % 2 + 1) * P], SS[:, (n % 2) * P:(n % 2 + 1) * P], GE[:, n:n + 1],
                                                   bank[2 + n % 2][:, 0:P], ALU.mult, ALU.add).then_inc(s["g_S"].sem, 1)
                    v.wait_ge(*s_evac.at(out_done(blks[3])))
                    for hf in range(2):
                        v.wait_ge(*s["g_or"].at(hf + 1))
                        ch(v.scalar_tensor_tensor(w4(DD, hf), w4(DD, hf), hrow[:, 8:9], w4(AT, hf), ALU.mult, ALU.mult))
                        y = X(hd, 512 * hf, 512)
                        ins = v.tensor_tensor(y, DD[:, 512 * hf:512 * hf + 512], y, ALU.mult)
                        if hf:
                            ins.then_inc(s_unit.sem, 1)
                            v.wait_ge(*s_unit.at(u + 1))
                        else:
                            ch(ins)

                return dict(pe=pe, act=act, dve=dve)

            s_gln = sem("gln", 4 * GH)
            for hd in range(GH):
                phases.append(gdn_unit(hd))

            s_bias = sem("biasd")

            def bias_phase():
                u = n_units[0]
                s_bl, s_bm, s_bc = sem("bl"), sem("bm"), sem("bc")
                bk_, bt_, rb_ = ar2[0:33, 0:TB], ar2[0:8, TB:2 * TB], ar2[0:33, 2 * TB:2 * TB + 8]

                def pool(g):
                    g.wait_ge(*s_unit.at(u))
                    g.dma_start(bk_, I["buckets"]).then_inc(s_bl.sem, 16)
                    g.dma_start(rb_, I["relb"]).then_inc(s_bl.sem, 16)
                    g.wait_ge(*s_bc.at(3))
                    g.dma_start(scratch["bias"].ap(), bt_).then_inc(s_bias.sem, 16)
                    g.wait_ge(*s_bias.at(16))

                def pe(p):
                    p.wait_ge(*s_bl.at(32))
                    for i in range(3):
                        p.matmul(bank[2 + i][0:8, 0:384], rb_, bk_[:, 384 * i:384 * i + 384], start=True, stop=True).then_inc(s_bm.sem, 1)

                def act(a):
                    for i in range(3):
                        a.wait_ge(*s_bm.at(i + 1))
                        a.activation(bt_[:, 384 * i:384 * i + 384], bank[2 + i][0:8, 0:384], ACT.Copy).then_inc(s_bc.sem, 1)

                return dict(pool=pool, pe=pe, act=act)

            phases.append(bias_phase())

            def swa_unit(p):
                u = n_units[0]
                n_units[0] += 1
                blks = [block(I["win2"][0, 16 + 4 * i + p], KT, M2, rhs_h2) for i in range(3)]
                Q, K, V, VT, PT = (A2(i) for i in range(5))
                LL = [A2(5), A2(6)]
                PR = [A2(7), A2(8)]
                W = A2(9, 2).rearrange("q (e x) -> q e x", e=2)
                F = A2(11, 2).rearrange("q (e x) -> q e x", e=2)
                its = [(a_, e) for a_ in range(NC2) for e in range(2)]
                NI = len(its)
                halves = [[(h, 512 * h, min(512, P * (a_ + 1) - 512 * h)) for h in range((a_ + 4) // 4)] for a_, e in its]
                hfirst = [sum(len(x) for x in halves[:i]) for i in range(NI + 1)]
                NHF = hfirst[NI]
                even = lambda k: (k + 1) // 2
                s_f, s_fl, s_w, s_tp, s_vt = (sem(x, n) for x, n in (("sf", 32), ("sfl", 4), ("sw", 4), ("stp", 2), ("svt", 2)))
                s_s, s_tt = sem("ss", NHF), sem("stt", NHF)
                s_m, s_e, s_pn, s_o = (sem(x, NI) for x in "sm se spn so".split())
                s_ti, s_pa, s_pd, s_y = sem("sti", NHF), sem("spa", even(NHF)), sem("spd", NHF - even(NHF)), sem("sy", NC2)

                def pool(g):
                    g.wait_ge(*s_unit.at(u))
                    for e in range(2):
                        g.dma_start(F[:, e, :], bass.AP(tensor=scratch["bias"], offset=(2 * p + e) * TB, ap=[[1, P], [1, 1024]])).then_inc(s_f.sem, 16)

                def pe(pt):
                    for blk in blks:
                        pe_block(pt, blk)
                    pt.wait_ge(*s_unit.at(u))
                    pt.wait_ge(*s_f.at(32))
                    for i in range(4):
                        pt.matmul(bank[2 + i][:, :], k2("flip"), F[:, i // 2, (i % 2) * 512:(i % 2) * 512 + 512], start=True, stop=True).then_inc(s_fl.sem, 1)
                    pt.wait_ge(*s_evac.at(out_done(blks[2])))
                    for f in range(2):
                        for m in range(4):
                            mm = pt.transpose(bank[6 + f][:, m * P:(m + 1) * P], V[:, (4 * f + m) * P:(4 * f + m + 1) * P], k2("ident"))
                        mm.then_inc(s_tp.sem, 1)
                    pt.wait_ge(*s_w.at(4))
                    pt.wait_ge(*s_vt.at(2))

                    def scores(i):
                        a_, e = its[i]
                        r = slice(64 * e, 64 * e + 64)
                        for h, k0, n in halves[i]:
                            hi = hfirst[i] + h
                            if hi >= 3:
                                pt.wait_ge(*s_tt.at(hi - 2))
                            pt.matmul(bank[2 + hi % 3][:, 0:n], Q[r, a_ * P:(a_ + 1) * P], K[r, k0:k0 + n], start=True, stop=True).then_inc(s_s.sem, 1)

                    def turn(i):
                        pt.wait_ge(*s_pn.at(i + 1))
                        for h, k0, n in halves[i]:
                            fi = hfirst[i] + h
                            if fi >= 2:
                                pt.wait_ge(*(s_pa if fi % 2 == 0 else s_pd).at(fi // 2))
                            for m in range(n // P):
                                mm = pt.transpose(bank[5 + fi % 2][:, m * P:(m + 1) * P], PR[i % 2][:, k0 + m * P:k0 + (m + 1) * P], k2("ident"))
                            mm.then_inc(s_ti.sem, 1)

                    def values(i):
                        a_, e = its[i]
                        k = hfirst[i + 1]
                        pt.wait_ge(*s_pa.at(even(k)))
                        if k > 1:
                            pt.wait_ge(*s_pd.at(k - even(k)))
                        if e == 0 and a_:
                            pt.wait_ge(*s_y.at(a_))
                        for kb in range(a_ + 1):
                            mm = pt.matmul(bank[7][64 * e:64 * e + 64, 0:P], VT[:, kb * P + 64 * e:kb * P + 64 * e + 64], PT[:, kb * P:(kb + 1) * P],
                                           start=kb == 0, stop=kb == a_)
                        mm.then_inc(s_o.sem, 1)

                    scores(0)
                    for i in range(NI):
                        if i + 1 < NI:
                            scores(i + 1)
                        turn(i)
                        values(i)

                def act(a):
                    a.wait_ge(*s_unit.at(u))
                    if p == 0:
                        a.wait_ge(*s_bias.at(16))
                    dst = [Q, K, V]
                    for i, blk in enumerate(blks):
                        act_block(a, blk, lambda ci, t0, n, ps: a.activation(dst[i][:, t0:t0 + n], ps, ACT.Copy, scale=HD ** -0.5 if i == 0 else 1.0))
                    for i in range(4):
                        a.wait_ge(*s_fl.at(i + 1))
                        a.activation(W[:, i // 2, (i % 2) * 512:(i % 2) * 512 + 512], bank[2 + i][:, :], ACT.Copy).then_inc(s_w.sem, 1)
                    for f in range(2):
                        a.wait_ge(*s_tp.at(f + 1))
                        a.activation(VT[:, 512 * f:512 * f + 512], bank[6 + f][:, :], ACT.Copy).then_inc(s_vt.sem, 1)

                    def exps(i):
                        a_, e = its[i]
                        nk = P * (a_ + 1)
                        a.wait_ge(*s_m.at(i + 1))
                        if i >= 2:
                            a.wait_ge(*s_ti.at(hfirst[i - 1]))
                        sm = gsm[:, 14 + i % 2, :]
                        a.activation(PR[i % 2][:, 0:nk], LL[i % 2][:, 0:nk], ACT.Exp, bias=sm[:, 2:3], accum_out=sm[:, 3:4]).then_inc(s_e.sem, 1)

                    def evac(i):
                        for h, k0, n in halves[i]:
                            fi = hfirst[i] + h
                            if fi % 2 == 0:
                                a.wait_ge(*s_ti.at(fi + 1))
                                if i:
                                    a.wait_ge(*s_o.at(i))
                                a.activation(PT[:, k0:k0 + n], bank[5][:, 0:n], ACT.Copy).then_inc(s_pa.sem, 1)

                    exps(0)
                    for i in range(NI):
                        if i + 1 < NI:
                            exps(i + 1)
                        evac(i)

                def dve(v):
                    ch = dve_chain(v)
                    for blk in blks:
                        dve_split(v, blk["b"] + SPLIT)
                    v.wait_ge(*s_w.at(4))

                    def maxes(i):
                        a_, e = its[i]
                        sm = gsm[:, 14 + i % 2, :]
                        if i >= 2:
                            v.wait_ge(*s_e.at(i - 1))
                        for h, k0, n in halves[i]:
                            hi = hfirst[i] + h
                            v.wait_ge(*s_s.at(hi + 1))
                            x0 = 896 - P * a_ + k0
                            v.tensor_tensor_reduce(out=LL[i % 2][:, k0:k0 + n], in0=bank[2 + hi % 3][:, 0:n], in1=W[:, e, x0:x0 + n], scale=1.0,
                                                   scalar=-3.0e38, op0=ALU.add, op1=ALU.max, accum_out=sm[:, h:h + 1]).then_inc(s_tt.sem, 1)
                        v.wait_ge(*s_tt.at(hfirst[i + 1]))
                        if len(halves[i]) == 2:
                            v.tensor_scalar(sm[:, 2:3], sm[:, 0:1], sm[:, 1:2], -1.0, ALU.max, ALU.mult).then_inc(s_m.sem, 1)
                        else:
                            v.tensor_scalar(sm[:, 2:3], sm[:, 0:1], -1.0, None, ALU.mult).then_inc(s_m.sem, 1)

                    maxes(0)
                    for i in range(NI):
                        a_, e = its[i]
                        nk = P * (a_ + 1)
                        sm = gsm[:, 14 + i % 2, :]
                        v.wait_ge(*s_e.at(i + 1))
                        ch(v.reciprocal(sm[:, 4:5], sm[:, 3:4]))
                        v.tensor_scalar(PR[i % 2][:, 0:nk], PR[i % 2][:, 0:nk], sm[:, 4:5], None, ALU.mult).then_inc(s_pn.sem, 1)
                        if i + 1 < NI:
                            maxes(i + 1)
                        for h, k0, n in halves[i]:
                            fi = hfirst[i] + h
                            if fi % 2:
                                v.wait_ge(*s_ti.at(fi + 1))
                                if i:
                                    v.wait_ge(*s_o.at(i))
                                v.tensor_copy(PT[:, k0:k0 + n], bank[6][:, 0:n]).then_inc(s_pd.sem, 1)
                        if e == 1:
                            v.wait_ge(*s_o.at(i + 1))
                            ins = v.tensor_copy(X(4 + p, a_ * P, P), bank[7][:, 0:P]).then_inc(s_y.sem, 1)
                    v.wait_ge(*s_y.at(NC2))
                    v.engine_nop().then_inc(s_unit.sem, 1)
                    v.wait_ge(*s_unit.at(u + 1))

                return dict(pe=pe, act=act, dve=dve, pool=pool)

            for p in range(SWA_PAIRS):
                phases.append(swa_unit(p))

            def out2_phase():
                u = n_units[0]
                blks = [block(I["wout2"][0, m], KT, M2, rhs_h2) for m in range(KT)]
                s_hi, s_lo = sem("m_hi", KT), sem("m_lo", KT)

                def pool(g):
                    g.wait_ge(*s_unit.at(u))
                    for m in range(KT):
                        g.dma_start(A2(m), scratch["x2"].ap()[:, m, CTX:]).then_inc(s_xr[m].sem, 16)

                def pe(p):
                    p.wait_ge(*s_lo.at(KT))
                    for blk in blks:
                        pe_block(p, blk)

                def act(a):
                    a.wait_ge(*s_unit.at(u))
                    for k in range(KT):
                        a.activation(H2[:, 0, k, :], X(k, 0, SEQ), ACT.Copy).then_inc(s_hi.sem, 1)
                    a.wait_ge(*s_lo.at(KT))
                    for m, blk in enumerate(blks):
                        act_block(a, blk, lambda ci, t0, n, ps: a.activation(X(m, t0, n), ps, ACT.Copy))

                def dve(v):
                    for k in range(KT):
                        v.wait_ge(*s_hi.at(k + 1))
                        v.tensor_tensor(H2[:, 1, k, :], X(k, 0, SEQ), H2[:, 0, k, :].bitcast(F32), ALU.subtract).then_inc(s_lo.sem, 1)
                    for blk in blks:
                        dve_split(v, blk["b"] + SPLIT)

                return dict(pool=pool, pe=pe, act=act, dve=dve, done=s_evac.at(out_done(blks[-1])))

            s_xr = [sem(f"xr{m}") for m in range(KT)]
            o2 = out2_phase()
            phases.append(o2)
            ro = rms_out(1, M2, X, lambda m, t0, n: A2(m)[:, t0:t0 + n], half2(A2(8)), A2(9)[:, 0:512], k2("mean"), k2("eps"), o2["done"],
                         lambda m: s_xr[m].at(16), 2)
            phases.append(ro)
            x_ready = ro["s_x"].at(ro["n"])

            b2.close()
            b3 = top.enter_context(ExitStack())
            HF = sb("HF", [P, 2, KT, 512], F32R, b3)
            FF = sb("FF", [P, 2, FT, 512], F32R, b3)
            O3 = sb("O3", [P, KT, 512], F32, b3)
            c3 = sb("c3", [P, P + 1], F32, b3)
            sq3 = sb("sq3", [P, 2, 512], F32, b3)
            rs3 = sb("rs3", [P, 512], F32, b3)
            s_c3 = sem("const3")

            def consts3_phase():
                def pool(g):
                    g.wait_ge(*x_ready)
                    g.dma_start(c3[:, :], I["c2"][:, C2["mean"][0]:C2["mean"][0] + P + 1]).then_inc(s_c3.sem, 16)

                def wait(e):
                    e.wait_ge(*s_c3.at(16))
                return dict(pool=pool, act=wait, pe=wait)

            phases.append(consts3_phase())
            s_outd = sem("outd")
            tail = x_ready

            def ffn(c, s_from):
                t0c = 512 * c
                one = [(t0c, 512)]
                G1, U1, FP = ([O3[:, 2 * i, :], O3[:, 2 * i + 1, :]] for i in range(3))
                tt = [O3[:, 6, :], O3[:, 7, :]]
                rin = rms_in(2, one, lambda part, m, t0, n: HF[:, part, m, :], [sq3[:, 0, :], sq3[:, 1, :]], rs3[:, :], tt,
                             c3[:, 0:P], c3[:, P:P + 1], s_from, 2)
                rh = lambda part, k, t0, n: HF[:, part, k, :]
                rf = lambda part, k, t0, n: FF[:, part, k, :]
                up = []
                for j in range(FT):
                    up.append((block(I["wgate"][0, j], KT, one, rh), block(I["wup"][0, j], KT, one, rh)))
                down = []
                for m in range(KT):
                    ks = [(0, 8), (8, 8), (16, 6)]
                    down.append([block(I["wdown"][m, :, k0 * P:(k0 + n) * P], n, one, rf, k0, k0 == 0, k0 == 16) for k0, n in ks])
                s_fp, s_fhi, s_flo = sem("f_p", FT), sem("f_hi", FT), sem("f_lo", FT)

                def pe(p):
                    for g, w in up:
                        pe_block(p, g)
                        pe_block(p, w)
                    p.wait_ge(*s_flo.at(FT))
                    for bl in down:
                        for blk in bl:
                            pe_block(p, blk)

                def act(a):
                    def rounded(j):
                        a.wait_ge(*s_fp.at(j + 1))
                        a.activation(FF[:, 0, j, :], FP[j % 2], ACT.Copy).then_inc(s_fhi.sem, 1)

                    for j, (g, w) in enumerate(up):
                        if j >= 2:
                            a.wait_ge(*s_fp.at(j - 1))
                        act_block(a, g, lambda ci, t0, n, ps: a.activation(G1[j % 2], ps, ACT.Silu))
                        act_block(a, w, lambda ci, t0, n, ps: a.activation(U1[j % 2], ps, ACT.Copy))
                        if j:
                            rounded(j - 1)
                    rounded(FT - 1)
                    a.wait_ge(*s_flo.at(FT))
                    for m, bl in enumerate(down):
                        for blk in bl:
                            act_block(a, blk, lambda ci, t0, n, ps: a.activation(O3[:, m, :], ps, ACT.Copy))

                def dve(v):
                    for j, (g, w) in enumerate(up):
                        dve_split(v, g["b"] + SPLIT)
                        dve_split(v, w["b"] + SPLIT)
                        v.wait_ge(*s_evac.at(out_done(w)))
                        if j >= 2:
                            v.wait_ge(*s_flo.at(j - 1))
                        v.tensor_tensor(FP[j % 2], G1[j % 2], U1[j % 2], ALU.mult).then_inc(s_fp.sem, 1)
                        v.wait_ge(*s_fhi.at(j + 1))
                        v.tensor_tensor(FF[:, 1, j, :], FP[j % 2], FF[:, 0, j, :].bitcast(F32), ALU.subtract).then_inc(s_flo.sem, 1)
                    for bl in down:
                        for blk in bl:
                            dve_split(v, blk["b"] + SPLIT)

                rout = rms_out(3, one, lambda m, t0, n: O3[:, m, :], X, [sq3[:, 0, :], sq3[:, 1, :]], rs3[:, :], c3[:, 0:P], c3[:, P:P + 1],
                               s_evac.at(out_done(down[-1][-1])), None, 2)

                def store(g):
                    g.wait_ge(*rout["s_x"].at(KT))
                    g.dma_start(out[:, :, t0c:t0c + 512], Y[:, :, CTX + t0c:CTX + t0c + 512]).then_inc(s_outd.sem, 16)

                return [rin, dict(pe=pe, act=act, dve=dve), rout, dict(pool=store)], rout["s_x"].at(KT)

            for c in range(2):
                phs, tail = ffn(c, tail)
                phases.extend(phs)

            def end_phase():
                def pool(g):
                    g.wait_ge(*s_outd.at(32))
                return dict(pool=pool)

            phases.append(end_phase())

        s_out = sem("out")
        blk = top.enter_context(nc.Block())

        @blk.sync
        def _(sp):
            sp_weights(sp)
            for ph in phases:
                if "sp" in ph:
                    ph["sp"](sp)
            if debug:
                if upto.startswith("branches"):
                    sp.wait_ge(*s_unit.at(n_units[0]))
                else:
                    sp.wait_ge(*ready[0].at(ready[1]))
                sp.dma_start(out, Y[:, :, CTX:]).then_inc(s_out.sem, 16)
                sp.wait_ge(*s_out.at(16))

        @blk.gpsimd
        def _(pool):
            for ph in phases:
                if "pool" in ph:
                    ph["pool"](pool)

        @blk.scalar
        def _(act):
            for ph in phases:
                if "act" in ph:
                    ph["act"](act)

        @blk.tensor
        def _(pe):
            for ph in phases:
                if "pe" in ph:
                    ph["pe"](pe)

        @blk.vector
        def _(dve):
            for ph in phases:
                if "dve" in ph:
                    ph["dve"](dve)


def layout(inputs):
    f = np.float32
    a = {k: np.asarray(v) for k, v in inputs.items()}
    cols = lambda w: np.ascontiguousarray(w.reshape(w.shape[0], KT, P, -1, P).transpose(0, 3, 2, 1, 4).reshape(w.shape[0], -1, P, KT * P))
    feat = lambda v: np.ascontiguousarray(v.reshape(v.shape[0], -1, P).transpose(2, 0, 1))
    x = np.concatenate([a["ctx"][0], a["x"][0]], axis=0)
    put = {
        "xt": np.ascontiguousarray(x.T.reshape(KT, P, T).transpose(1, 0, 2)),
        "c2t": np.ascontiguousarray(np.stack([a["c"][0], a["c_ctx"]], axis=1).reshape(KT, P, 2).transpose(1, 0, 2)),
        "wmod": cols(a["w_mod"]), "bmod": feat(a["b_mod"]),
        "win": cols(a["w_in"]), "wout": cols(a["w_out"]),
        "convp": np.ascontiguousarray(np.concatenate([a["conv_w"], a["conv_b"][:, None]], axis=1).reshape(LAYERS, 4, 2, P).transpose(3, 0, 2, 1)),
        "decay": np.ascontiguousarray(a["ret_decay"].reshape(LAYERS * 12, 1)),
        "decayp": np.ascontiguousarray(a["ret_decay"].reshape(LAYERS, 2, PAIRS, 2).transpose(0, 3, 1, 2).reshape(LAYERS * 12, 1)),
        "rpb": np.ascontiguousarray(a["na_rpb"].reshape(LAYERS * 45, 2, RPB_W)),
        "lnp": np.ascontiguousarray(np.stack([a["ln_g"], a["ln_b"]], axis=1).reshape(LAYERS, 2, KT, P).transpose(3, 0, 1, 2)),
    }
    w2 = a["w_in_2"]
    small = GH * P * 4
    wide = np.concatenate([w2[:, :, :small], w2[:, :, small + 2 * GH:]], axis=2)
    put.update({
        "win2": cols(wide), "wba": np.ascontiguousarray(w2[0, :, small:small + 2 * GH].reshape(KT, P, 2 * GH).transpose(1, 0, 2)),
        "cw2": np.ascontiguousarray(a["conv_w_2"][0].reshape(4, 12, P).transpose(2, 1, 0)),
        "dtb": a["dt_bias_2"], "alog": a["a_log_2"], "onorm": np.ascontiguousarray(a["onorm_g_2"].reshape(P, 1)),
        "relb": np.concatenate([a["rel_bias_2"], np.ones((1, 8), f)], axis=0),
        "gp2": np.ascontiguousarray(np.concatenate([a["g_mix_pre_2"], a["g_mix_post_2"], a["g_ffn_pre_2"], a["g_ffn_post_2"]], axis=0)
                                    .reshape(4, KT, P).transpose(2, 0, 1)),
        "wout2": cols(a["w_out_2"]), "wgate": cols(a["w_gate_2"]), "wup": cols(a["w_up_2"]),
        "wdown": np.ascontiguousarray(a["w_down_2"][0].reshape(FT, P, KT, P).transpose(2, 1, 0, 3).reshape(KT, P, FT * P)),
    })
    put.update(constants())
    return put


def program(nc, put, upto=None):
    I = {}
    for name, v in put.items():
        t = nc.dram_tensor(f"in_{name}", v.shape, F32, kind="ExternalInput")
        I[name] = t.ap()
        I[name + "_t"] = t
    out = nc.dram_tensor("out_fm", [P, KT, SEQ], F32, kind="ExternalOutput").ap()
    scratch = {
        "x1": nc.dram_tensor("x1", [P, KT, T], F32, kind="Internal"),
        "x2": nc.dram_tensor("x2", [P, KT, T], F32, kind="Internal"),
        "rpb": nc.dram_tensor("rpbpad", [LAYERS * 6 * RPB_H, 127], F32, kind="Internal"),
        "bias": nc.dram_tensor("biasrow", [8, TB], F32, kind="Internal"),
    }
    build(nc, I, out, scratch, upto)


def kernel(**inputs):
    import concourse.bacc as bacc
    from concourse.bass_utils import run_bass_kernel_spmd as run

    put = layout(inputs)
    nc = bacc.Bacc("TRN2", target_bir_lowering=False, num_devices=1)
    program(nc, put)
    r = run(nc, [{f"in_{k}": v for k, v in put.items()}], core_ids=[0])
    fm = r.results[0]["out_fm"]
    return np.ascontiguousarray(fm.transpose(2, 1, 0).reshape(1, SEQ, D))
```

```python
from contextlib import ExitStack

import numpy as np

import concourse.bass as bass
from concourse import mybir

F32 = mybir.dt.float32
F32R = mybir.dt.float32r
ALU = mybir.AluOpType
ACT = mybir.ActivationFunctionType
AX_X = mybir.AxisListType.X

P = 128
D = 1024
KT = D // P
CTX, SEQ = 256, 1024
T = CTX + SEQ
LAYERS = 2
HD = 64
PAIRS = 3
NCH = T // P
GRID_W, GRID_H, WIN_H = 64, 16, 8
RPB_H, RPB_W = 15, 31
ALPHA = (2 * LAYERS) ** 0.25
GH = 4
NC2 = SEQ // P
SWA_PAIRS = 4
DFF = 2816
FT = DFF // P
BUCKETS = 32
TB = 1152
CHUNKS = [(0, CTX), (CTX, 512), (CTX + 512, 512)]
MAIN = CHUNKS[1:]
NEG = -1.0e30
INV_LEVELS = 7

C1 = {}
C2 = {}


def _place(table, names):
    at = 0
    for name, n in names:
        table[name] = (at, n)
        at += n
    return at


N1 = _place(C1, [("ident", P), ("rot", P), ("center", P), ("headmean", P), ("pairmask", P), ("flip64", P),
                 ("ip1", P), ("rev", P), ("fwd", P), ("bwd", P), ("mean", P), ("wincol", GRID_W),
                 ("jrev", 1), ("j", 1), ("eps", 1)])
N2 = _place(C2, [("ident", P), ("mean", P), ("eps", 1), ("ones", P), ("headmean", P), ("upto", P), ("causalT", P),
                 ("strict", P), ("flip", P), ("low0", P)] + [(f"lowT{k}", P) for k in range(INV_LEVELS)])


def constants():
    f = np.float32
    i = np.arange(P)
    eye = np.eye(P, dtype=f)
    half = (i[:, None] // HD == i[None, :] // HD).astype(f)
    rot = np.zeros((P, P), f)
    for b in range(0, P, 32):
        for k in range(16):
            rot[b + 16 + k, b + k] = -1.0
            rot[b + k, b + 16 + k] = 1.0
    flip64 = np.zeros((P, P), f)
    for b in (0, HD):
        for k in range(HD):
            flip64[b + k, b + HD - 1 - k] = 1.0
    c = np.arange(GRID_W)
    start = np.clip(c - 8, 0, GRID_W - 16)
    inside = (c[None, :] >= start[:, None]) & (c[None, :] < start[:, None] + 16)
    wincol = np.where(inside, 0.0, NEG).astype(f)
    row = lambda v: np.broadcast_to(np.asarray(v, f), (P, P))
    parts = {
        "ident": eye, "rot": rot, "center": eye - half / HD, "headmean": half / HD, "pairmask": half, "flip64": flip64,
        "ip1": row(i + 1), "rev": row(P - i), "fwd": np.maximum(i[None, :] - i[:, None], 0),
        "bwd": np.maximum(i[:, None] - i[None, :], 0), "mean": np.full((P, P), 1.0 / D),
        "wincol": np.concatenate([wincol, wincol]), "jrev": (P - 1 - i)[:, None], "j": i[:, None],
        "eps": np.full((P, 1), 1e-5),
    }
    c1 = np.concatenate([np.asarray(parts[n], f) for n in C1], axis=1)
    parts = {
        "ident": eye, "mean": np.full((P, P), 1.0 / D), "ones": np.ones((P, P)), "headmean": np.full((P, P), 1.0 / P),
        "upto": (i[:, None] <= i[None, :]), "causalT": np.where(i[None, :] >= i[:, None], 0.0, NEG),
        "strict": np.where(i[:, None] > i[None, :], 0.0, NEG), "flip": eye[::-1], "eps": np.full((P, 1), 1e-6),
    }
    for k in range(INV_LEVELS):
        b = i >> k
        low = ((b[:, None] % 2 == 1) & (b[None, :] == b[:, None] - 1)).astype(f)
        parts[f"lowT{k}"] = low.T
        if k == 0:
            parts["low0"] = low
    c2 = np.concatenate([np.asarray(parts[n], f) for n in C2], axis=1)
    nf = HD // 4
    inv = (f(10000.0) ** (-np.arange(nf, dtype=f) / f(nf))).astype(f)
    t = np.arange(SEQ)
    ang_r = (t // GRID_W).astype(f)[:, None] * inv
    ang_c = (t % GRID_W).astype(f)[:, None] * inv
    ang = np.concatenate([ang_r, ang_r, ang_c, ang_c], axis=1).T
    ang = np.concatenate([ang, ang], axis=0).astype(f)
    cos = np.concatenate([np.ones((P, CTX), f), np.cos(ang)], axis=1)
    sin = np.concatenate([np.zeros((P, CTX), f), np.sin(ang)], axis=1)
    dist = 1023 - np.arange(TB)
    d = np.maximum(dist, 1).astype(f)
    far = 16 + (np.log(d / f(16)) / f(np.log(2048 / 16)) * f(16)).astype(np.int32)
    bucket = np.where(dist < 16, dist, np.minimum(far, 31))
    times = ((dist <= 128).astype(int) + ((dist % 4 == 0) & (dist <= 512)) + ((dist % 16 == 0) & (dist <= 2048)))
    times = np.where(dist >= 0, times, 0)
    buckets = np.zeros((BUCKETS + 1, TB), f)
    for y in range(TB):
        if times[y] > 0:
            buckets[bucket[y], y] = 1.0
            buckets[BUCKETS, y] = np.log(f(times[y]))
        else:
            buckets[BUCKETS, y] = NEG
    return {"c1": c1, "c2": c2, "cos": cos, "sin": sin, "buckets": buckets}


SHARED = """
rot=g_gb tp=g_ss u=g_tp rs=g_qk ro=g_tat rcen=g_py rvar=g_pz nfl=g_uw ntp=g_ws ns=g_kv nta=g_o ntb=g_ov
no=stp mu=sfl var=r_var
rope=g_conv qf=g_n kw=g_kd um=g_tk S=g_S rsc=g_tv ryr=g_d nt=g_att nm=g_a npn=g_ot npb=g_x ny=g_vn
ylo=r_lo res=r_rt cen=p_t nrm=p_x
vt=g_gbc ros=g_eg rsq=g_silu rrs=g_sq reta=g_rs nvt=g_kdc ne=g_dx npa=g_at yhi=r_hi lna=g_y sq=r_sq rstd=r_rs fin=g_u
nf=sf
"""


class Count:

    def __init__(self, sem, base):
        self.sem, self.base = sem, base

    def at(self, n):
        return self.sem, self.base + n


class Chain:

    def __init__(self, eng, sem):
        self.eng, self.sem, self.n = eng, sem, 0

    def __call__(self, ins):
        self.n += 1
        ins.then_inc(self.sem, 1)
        self.eng.wait_ge(self.sem, self.n)


def build(nc, I, out, scratch):
    top = ExitStack()
    uid = [0]

    def sb(name, shape, dt=F32, stack=None):
        uid[0] += 1
        return (stack or top).enter_context(nc.sbuf_tensor(f"{name}_{uid[0]}", shape, dt))

    handles, raised = {}, {}
    signals = {}
    for a in SHARED.split():
        one, two = a.split("=")
        signals[one] = signals[two] = f"{one}_{two}"

    def sem(name, total=0):
        if name in signals:
            name = signals[name]
        if name not in handles:
            handles[name] = top.enter_context(nc.semaphore(name))
            raised[name] = 0
        raised[name] += total
        return Count(handles[name], raised[name] - total)

    with top:
        bank = [top.enter_context(nc.psum_tensor(f"bank{i}", [P, 512], F32)) for i in range(8)]

        RAW, SPLIT = 3, 2
        raw = sb("raw", [P, RAW, KT * P])
        ws = sb("ws", [P, SPLIT, 2, KT * P], F32R)
        s_raw = [sem(f"raw{i}") for i in range(RAW)]
        s_whi, s_wlo = sem("w_hi"), sem("w_lo")
        s_gemm = sem("gemm")
        s_evac = sem("evac")
        s_unit = sem("unit")

        dmas = []
        raw_free = []
        blocks = []
        n_piece, n_out, n_units = [0], [0], [0]

        def mod_block(src, out2, bias):
            dmas.append((src, KT * P))
            blk = dict(mod=True, r=len(dmas) - 1, piece=n_piece[0], out=n_out[0], chunks=[(0, 2)],
                       evac=lambda act, ci, t0, n, ps: act.activation(out2, ps, ACT.Identity, bias=bias))
            n_piece[0] += 1
            n_out[0] += 1
            raw_free.append(s_gemm.at(n_piece[0]))
            return blk

        def block(src, kts, chunks, rhs, k0=0, first=True, last=True, evac=None):
            b = len(blocks)
            dmas.append((src, kts * P))
            raw_free.append(s_wlo.at(b + 1))
            o0 = n_out[0]
            blocks.append(dict(mod=False, evac=evac, b=b, r=len(dmas) - 1, kts=kts, chunks=chunks, rhs=rhs, k0=k0, first=first, last=last,
                               piece=n_piece[0], out=o0))
            n_piece[0] += len(chunks)
            if last:
                n_out[0] += len(chunks)
            return blocks[-1]

        def sp_weights(sp):
            for r, (src, n) in enumerate(dmas):
                if r >= RAW:
                    sp.wait_ge(*raw_free[r - RAW])
                sp.dma_start(raw[:, r % RAW, 0:n], src).then_inc(s_raw[r % RAW].sem, 16)

        def act_split(act, b):
            if b >= len(blocks):
                return
            blk = blocks[b]
            n = blk["kts"] * P
            act.wait_ge(*s_raw[blk["r"] % RAW].at(16 * (blk["r"] // RAW + 1)))
            if b >= SPLIT:
                prev = blocks[b - SPLIT]
                act.wait_ge(*s_gemm.at(prev["piece"] + len(prev["chunks"])))
            act.activation(ws[:, b % SPLIT, 0, 0:n], raw[:, blk["r"] % RAW, 0:n], ACT.Copy).then_inc(s_whi.sem, 1)

        def dve_split(dve, b):
            if b >= len(blocks):
                return
            blk = blocks[b]
            n = blk["kts"] * P
            dve.wait_ge(*s_whi.at(b + 1))
            dve.tensor_tensor(ws[:, b % SPLIT, 1, 0:n], raw[:, blk["r"] % RAW, 0:n],
                              ws[:, b % SPLIT, 0, 0:n].bitcast(F32), ALU.subtract).then_inc(s_wlo.sem, 1)

        def pe_block(pe, blk, k_wait=None):
            if blk["mod"]:
                r = blk["r"]
                pe.wait_ge(*s_raw[r % RAW].at(16 * (r // RAW + 1)))
            else:
                b = blk["b"]
                pe.wait_ge(*s_wlo.at(b + 1))
            for ci, (t0, n) in enumerate(blk["chunks"]):
                o = blk["out"] + ci
                if (blk["mod"] or blk["first"]) and o >= 2:
                    pe.wait_ge(*s_evac.at(o - 1))
                if blk["mod"]:
                    for k in range(KT):
                        mm = pe.matmul(bank[o % 2][:, 0:n], raw[:, r % RAW, k * P:(k + 1) * P], cact[:, k, :], start=k == 0, stop=k == KT - 1)
                    yield
                else:
                    for k in range(blk["kts"]):
                        if k_wait is not None and ci == 0:
                            k_wait(k)
                        for part, (wp, xp) in enumerate(((0, 0), (0, 1), (1, 0))):
                            mm = pe.matmul(bank[o % 2][:, 0:n], ws[:, b % SPLIT, wp, k * P:(k + 1) * P],
                                           blk["rhs"](xp, blk["k0"] + k, t0, n),
                                           start=blk["first"] and k == 0 and part == 0,
                                           stop=blk["last"] and k == blk["kts"] - 1 and part == 2)
                        if k == blk["kts"] // 2 - 1:
                            yield
                mm.then_inc(s_gemm.sem, 1)
                yield

        def act_block(act, blk, evac=None):
            evac = evac or blk["evac"]
            for ci, (t0, n) in enumerate(blk["chunks"]):
                if blk["mod"] or blk["last"]:
                    act.wait_ge(*s_gemm.at(blk["piece"] + ci + 1))
                    evac(act, ci, t0, n, bank[(blk["out"] + ci) % 2][:, 0:n]).then_inc(s_evac.sem, 1)
                if not blk["mod"] and ci == len(blk["chunks"]) - 1:
                    act_split(act, blk["b"] + SPLIT)
                yield

        def dve_block(dve, blk):
            if not blk["mod"]:
                dve_split(dve, blk["b"] + SPLIT)

        def whole(steps):
            for _ in steps:
                pass

        class Fill:

            def __init__(self, steps, targets):
                self.steps, self.targets, self.done, self.at = steps, targets, 0, 0

            def to(self, n):
                while self.done < n:
                    next(self.steps)
                    self.done += 1

            def __call__(self):
                if self.targets is not None:
                    self.to(self.targets[self.at])
                self.at += 1

            def finish(self, points):
                assert self.at == points, (self.at, points)
                if self.targets is not None:
                    whole(self.steps)

        def targets(unit, points):
            ends = []
            for blk in unit["blks"]:
                ends.append((ends[-1] if ends else 0) + len(blk["chunks"]))
            pe_t = [-(-2 * ends[-1] * (i + 1) // points) for i in range(points)]
            act_t = [0] + [t // 2 for t in pe_t[:-1]]
            dve_t = [sum(e <= t for e in ends) for t in act_t]
            return pe_t, act_t, dve_t

        def project_pe(pe, unit):
            for blk in unit["blks"]:
                yield from pe_block(pe, blk)

        def project_act(act, unit):
            if unit["u"] >= 1:
                act.wait_ge(*s_unit.at(unit["u"] - 1))
            unit["act_first"](act)
            for blk in unit["blks"]:
                yield from act_block(act, blk)

        def project_dve(dve, unit):
            for blk in unit["blks"]:
                dve_block(dve, blk)
                yield

        def run_units(units):
            def program(which, project):
                def run(eng):
                    whole(project(eng, units[0]))
                    for i, un in enumerate(units):
                        nxt = units[i + 1] if i + 1 < len(units) else None
                        fill = Fill(project(eng, nxt) if nxt else None,
                                    targets(nxt, un["points"])[("pe", "act", "dve").index(which)] if nxt else None)
                        un[which](eng, fill)
                        fill.finish(un["points"])
                return run

            def pool(g):
                for i, un in enumerate(units):
                    if "pool" in un:
                        un["pool"](g)
                    if i and "stored" in units[i - 1]:
                        g.wait_ge(*units[i - 1]["stored"])
                    if "store" in un:
                        g.wait_ge(*s_unit.at(un["u"] + 1))
                        un["store"](g)

            return dict(pe=program("pe", project_pe), act=program("act", project_act), dve=program("dve", project_dve), pool=pool)

        def out_done(blk, ci=None):
            return blk["out"] + (len(blk["chunks"]) if ci is None else ci + 1)

        order = {}

        def dve_chain(v):
            if "dve" not in order:
                order["dve"] = Chain(v, sem("dve_order").sem)
            return order["dve"]

        Y = sb("Y", [P, KT, T])
        gp2 = sb("gp2", [P, 4, KT])
        s_const = sem("const")
        phases = []

        b1 = top.enter_context(ExitStack())
        HH = sb("HH", [P, 2, KT, T], F32R, b1)
        c1 = sb("c1", [P, N1], F32, b1)
        arena_n = 11008
        arena = sb("arena", [P, arena_n], F32, b1)
        modv = sb("modv", [P, LAYERS, 24, 2], F32, b1)
        cact = sb("cact", [P, KT, 2], F32, b1)
        bmod = sb("bmod", [P, LAYERS, 24], F32, b1)
        lnp = sb("lnp", [P, LAYERS, 2, KT], F32, b1)
        convp = sb("convp", [P, LAYERS, 2, 4], F32, b1)
        LG = sb("LG", [P, LAYERS, 18], F32, b1)
        DT = sb("DT", [P, 6, P], F32, b1)
        WQ = sb("WQ", [P, 2, PAIRS, P], F32, b1)
        WK = sb("WK", [P, 2, 6], F32, b1)
        G128 = sb("G128", [P, 6], F32, b1)
        small = sb("small", [P, 64], F32, b1)

        def k1(name):
            a, n = C1[name]
            return c1[:, a:a + n]

        arena_at = [0]

        def spot(n, at=None):
            at = arena_at[0] if at is None else at
            arena_at[0] = at + n
            assert at + n <= arena_n, at + n
            return arena[:, at:at + n]

        PXS = [[Y[:, 4 * i + j, :] for j in range(4)] for i in range(2)]
        TMP = spot(512)
        COS, SIN, QF = spot(T), spot(T), spot(T)
        UM, SC = spot(512), spot(1024)
        KWF, KWB, VTR, SF = spot(T), spot(T), spot(T), spot(T)
        SB = KWF
        QB = spot(20 * P, 0)
        NT = spot(RPB_H * GRID_W)
        PR = [spot(768), spot(768)]
        VT = spot(T)
        VS, LL, PT = spot(7 * P), spot(1024), spot(768)
        NF = arena[:, 2560 + RPB_H * GRID_W:2560 + 2 * RPB_H * GRID_W]
        ST = [spot(T, j * T) for j in range(7)]
        CT = spot(T)
        RS = spot(512)
        SQ = [ST[4][:, 0:512], ST[4][:, 512:1024]]
        lgt = UM[:, 0:4 * LAYERS * 18].rearrange("q (a c) -> q a c", a=4)
        HT = QF

        def rhs_hh(part, k, t0, n):
            return HH[:, part, k, t0:t0 + n]

        s_x0 = sem("x0")

        s_lg, s_bm1 = sem("lg"), sem("bm1")
        s_xst = sem("xst")
        s_h, s_hhi = sem("h", 2 * 16), sem("hhi", 2 * 16)
        s_dt = [sem(f"dt{l}") for l in range(LAYERS)]
        s_tabd = sem("tabd")
        s_cs = sem("cossin")
        modb = {}

        def mod_block_of(l, m):
            modb[l, m] = mod_block(I["wmod"][l, m], modv[:, l, m, :], bmod[:, l, m:m + 1])
            return modb[l, m]

        def mod_ready(l, m):
            return s_evac.at(out_done(modb[l, m]))

        def first_phase():
            for k in range(KT):
                mod_block_of(0, k)
                mod_block_of(0, 8 + k)
            s_achain, s_e = sem("modact"), sem("lge")
            NCONST = 5 + LAYERS * 3

            def pool(g):
                g.dma_start(cact[:, :, :], I["c2t"]).then_inc(s_const.sem, 16)
                g.dma_start(bmod[:, :, :], I["bmod"]).then_inc(s_const.sem, 16)
                rd = I["decay_t"]
                for l in range(LAYERS):
                    g.dma_start(LG[:, l, 0:12], bass.AP(tensor=rd, offset=l * 12, ap=[[0, P], [1, 12]])).then_inc(s_const.sem, 16)
                    for e in range(2):
                        g.dma_start(LG[64 * e:64 * e + 64, l, 12:18],
                                    bass.AP(tensor=I["decayp_t"], offset=(l * 2 + e) * 6, ap=[[0, 64], [1, 6]])).then_inc(s_const.sem, 16)
                g.dma_start(c1[:, :], I["c1"]).then_inc(s_const.sem, 16)
                g.dma_start(lnp[:, :, :, :], I["lnp"]).then_inc(s_const.sem, 16)
                g.dma_start(convp[:, :, :, :], I["convp"]).then_inc(s_const.sem, 16)
                g.dma_start(Y[:, :, :], I["xt"]).then_inc(s_x0.sem, 16)

            def act(a):
                a.wait_ge(*s_const.at(16 * NCONST))
                ch = Chain(a, s_achain.sem)
                ch(a.activation(cact[:, :, :], cact[:, :, :], ACT.Silu))
                a.wait_ge(*s_e.at(1))
                ch(a.activation(lgt[:, 1, :], lgt[:, 0, :], ACT.Exp))
                ch(a.activation(lgt[:, 2, :], lgt[:, 1, :], ACT.Ln, bias=1.0))

            def pe(p):
                p.wait_ge(*s_achain.at(1))

            def dve(v):
                ch = dve_chain(v)
                v.wait_ge(*s_const.at(16 * NCONST))
                v.tensor_scalar(bmod[:, :, 8:16], bmod[:, :, 8:16], 1.0, None, ALU.add).then_inc(s_bm1.sem, 1)
                x = LG[:, :, :].rearrange("p l c -> p (l c)")
                v.scalar_tensor_tensor(lgt[:, 0, :], x, -1.0, x, ALU.mult, ALU.min).then_inc(s_e.sem, 1)
                v.wait_ge(*s_achain.at(3))
                e, l1 = lgt[:, 1, :], lgt[:, 2, :]
                t = lgt[:, 3, :]
                ch(v.tensor_scalar(t, e, 1.0, -1.0, ALU.add, ALU.add))
                ch(v.tensor_scalar(t, t, 1e-30, None, ALU.max))
                ch(v.reciprocal(t, t))
                ch(v.tensor_tensor(t, t, e, ALU.mult))
                ch(v.tensor_tensor(l1, l1, t, ALU.mult))
                ch(v.tensor_scalar(t, e, -0.5, 1.0, ALU.mult, ALU.add))
                ch(v.tensor_tensor(t, t, e, ALU.mult))
                ch(v.tensor_tensor(l1, l1, t, ALU.max))
                v.scalar_tensor_tensor(x, x, 0.0, l1, ALU.min, ALU.subtract).then_inc(s_lg.sem, 1)
                v.wait_ge(*s_lg.at(1))

            return dict(pool=pool, act=act, pe=pe, dve=dve)

        def table_phase(l):
            u = n_units[0]

            def act(a):
                a.wait_ge(*s_tabd.at(l + 1))
                a.activation(DT[:, :, :], DT[:, :, :], ACT.Exp).then_inc(s_dt[l].sem, 1)
                lp = LG[:, l, 12:18]
                for d, src in enumerate(("ip1", "rev")):
                    for p in range(PAIRS):
                        a.activation(WQ[:, d, p, :], k1(src), ACT.Exp, scale=LG[:, l, 12 + 3 * d + p:13 + 3 * d + p]).then_inc(s_dt[l].sem, 1)
                a.activation(WK[:, 0, :], LG[:, l, 0:6], ACT.Exp, scale=k1("jrev")).then_inc(s_dt[l].sem, 1)
                a.activation(WK[:, 1, :], LG[:, l, 6:12], ACT.Exp, scale=k1("j")).then_inc(s_dt[l].sem, 1)
                a.activation(G128[:, :], lp, ACT.Exp, scale=float(P)).then_inc(s_dt[l].sem, 1)

            def dve(v):
                ch = dve_chain(v)
                v.wait_ge(*s_lg.at(1))
                if l:
                    v.wait_ge(*s_unit.at(u))
                for h in range(6):
                    ch(v.tensor_scalar(DT[:, h, :], k1("fwd"), LG[:, l, h:h + 1], None, ALU.mult))
                    ins = v.scalar_tensor_tensor(DT[:, h, :], k1("bwd"), LG[:, l, 6 + h:7 + h], DT[:, h, :], ALU.mult, ALU.add)
                    if h < 5:
                        ch(ins)
                    else:
                        ins.then_inc(s_tabd.sem, 1)
                        v.wait_ge(*s_tabd.at(l + 1))

            return dict(act=act, dve=dve)

        def start_phase(l, s_ready, v_ready):
            segs = [(0, CTX, 1), (CTX, SEQ, 0)]

            def pool(g):
                g.wait_ge(*s_ready.at(v_ready))
                g.dma_start(COS, I["cos"]).then_inc(s_cs.sem, 16)
                g.dma_start(SIN, I["sin"]).then_inc(s_cs.sem, 16)

            def act(a):
                if l == 0:
                    a.wait_ge(*s_bm1.at(1))
                a.wait_ge(*s_ready.at(v_ready))
                for k in range(KT):
                    if l == 0:
                        whole(act_block(a, modb[0, k]))
                        whole(act_block(a, modb[0, 8 + k]))
                    a.wait_ge(*mod_ready(l, 8 + k))
                    for si, (t0, n, w) in enumerate(segs):
                        ins = a.activation(HH[:, 0, k, t0:t0 + n], Y[:, k, t0:t0 + n], ACT.Identity,
                                           scale=modv[:, l, 8 + k, w:w + 1], bias=modv[:, l, k, w:w + 1])
                        ins.then_inc(s_hhi.sem, 1)
                if l == 0:
                    act_split(a, 0)
                    act_split(a, 1)

            def dve(v):
                ch = dve_chain(v)
                v.wait_ge(*s_ready.at(v_ready))
                i = 16 * l
                for k in range(KT):
                    v.wait_ge(*mod_ready(l, 8 + k))
                    for si, (t0, n, w) in enumerate(segs):
                        tt = HT[:, 0:n]
                        ch(v.tensor_scalar(tt, Y[:, k, t0:t0 + n], modv[:, l, 8 + k, w:w + 1], modv[:, l, k, w:w + 1], ALU.mult, ALU.add))
                        i += 1
                        v.wait_ge(*s_hhi.at(i))
                        v.tensor_tensor(HH[:, 1, k, t0:t0 + n], tt, HH[:, 0, k, t0:t0 + n].bitcast(F32), ALU.subtract).then_inc(s_h.sem, 1)
                        v.wait_ge(*s_h.at(i))
                if l == 0:
                    dve_split(v, 0)
                    dve_split(v, 1)

            def pe(p):
                if l == 0:
                    for k in range(KT):
                        whole(pe_block(p, modb[0, k]))
                        whole(pe_block(p, modb[0, 8 + k]))
                p.wait_ge(*s_h.at(16 * (l + 1)))

            return dict(act=act, dve=dve, pe=pe, pool=pool)

        mods_left = [(0, 16 + k) for k in range(KT)] + [(1, m) for m in range(24)]

        def projections(l, cols, chunks, evacs):
            out = []
            for c, ch, ev in zip(cols, chunks, evacs):
                out.append(block(I["win"][l, c], KT, ch, rhs_hh, evac=ev))
                if l == 0:
                    out.append(mod_block_of(*mods_left.pop(0)))
            return out

        def plain(dst, func=ACT.Copy, scale=1.0):
            return lambda act, ci, t0, n, ps: act.activation(dst[:, t0:t0 + n], ps, func, scale=scale)

        s_pad, s_bias, s_qz = sem("pad"), sem("biasd"), sem("qzero")
        s_brd = sem("branch")
        n_stored = [0]

        def store(unit, tile, lo):
            n_stored[0] += 1
            unit["stored"] = s_brd.at(16 * n_stored[0])
            unit["store"] = lambda g: g.dma_start(scratch["br"].ap()[:, tile, lo:], unit["result"][:, lo:]).then_inc(s_brd.sem, 16)

        def act_first(l, u):
            stored = n_stored[0] - 1

            def run(a):
                if u % 8 == 0:
                    a.wait_ge(*s_h.at(16 * (l + 1)))
                    if l:
                        a.wait_ge(*s_xst.at(16))
                elif stored > 0:
                    a.wait_ge(*s_brd.at(16 * stored))
            return run

        NDT = 10

        s_stg = sem("staged")
        s_conv = sem("convdone")

        def conv_unit(l, c):
            u = n_units[0]
            n_units[0] += 1
            chunks = CHUNKS if l == 0 else MAIN
            segs = ([(0, CTX)] if l == 0 else []) + [(CTX, T)]
            lo = segs[0][0]
            h, cg, bg, z = PXS[u % 2]
            blks = projections(l, [24 + c, 28 + c, 26 + c, 30 + c], [chunks] * 4, [plain(h), plain(cg), plain(bg), plain(z, ACT.Silu)])
            prods = [b for b in blks if not b["mod"]]
            unit = dict(u=u, blks=blks, points=3, act_first=act_first(l, u), result=z)

            def pool(g):
                g.wait_ge(*s_unit.at(u))
                g.wait_ge(*stored_before)
                if c == 0:
                    g.dma_start(arena[:, 0:6 * T].rearrange("q (m t) -> q m t", t=T)[:, :, lo:], scratch["br"].ap()[:, 2:8, lo:]).then_inc(s_stg.sem, 16)
                else:
                    g.wait_ge(*s_stg.at(32 * l + 16))
                    g.dma_start(ST[6][:, lo:], scratch["br"].ap()[:, 0, lo:]).then_inc(s_stg.sem, 16)

            def pe(p, fill):
                fill()
                fill()
                fill()

            def act(a, fill):
                fill()
                fill()
                fill()

            def dve(v, fill):
                ch = dve_chain(v)
                w = convp[:, l, c, :]
                v.wait_ge(*s_unit.at(u))
                v.wait_ge(*s_evac.at(out_done(prods[1])))
                ch(v.tensor_tensor(h[:, lo:], h[:, lo:], cg[:, lo:], ALU.mult))
                ch(v.tensor_scalar(CT[:, lo:], h[:, lo:], w[:, 1:2], w[:, 3:4], ALU.mult, ALU.add))
                fill()
                for a_, b_ in segs:
                    ch(v.scalar_tensor_tensor(CT[:, a_ + 1:b_], h[:, a_:b_ - 1], w[:, 0:1], CT[:, a_ + 1:b_], ALU.mult, ALU.add))
                    ch(v.scalar_tensor_tensor(CT[:, a_:b_ - 1], h[:, a_ + 1:b_], w[:, 2:3], CT[:, a_:b_ - 1], ALU.mult, ALU.add))
                fill()
                v.wait_ge(*s_evac.at(out_done(prods[2])))
                ch(v.tensor_tensor(CT[:, lo:], CT[:, lo:], bg[:, lo:], ALU.mult))
                v.wait_ge(*s_evac.at(out_done(prods[3])))
                v.tensor_tensor(z[:, lo:], CT[:, lo:], z[:, lo:], ALU.mult).then_inc(s_unit.sem, 1)
                v.wait_ge(*s_unit.at(u + 1))
                fill()

            stored_before = s_brd.at(16 * n_stored[0])
            unit.update(pe=pe, act=act, dve=dve, pool=pool)
            if c == 0:
                store(unit, c, lo)
            return unit

        def ret_unit(l, p):
            u = n_units[0]
            n_units[0] += 1
            qch = CHUNKS if l == 0 else MAIN
            Kb, Vb, Qb, Gb = PXS[u % 2]
            allb = projections(l, [p, 3 + p, 12 + p, 15 + p], [CHUNKS, CHUNKS, qch, qch],
                               [plain(Kb, scale=HD ** -0.5), plain(Vb), plain(Qb), plain(Gb, ACT.Silu)])
            blks = [b for b in allb if not b["mod"]]
            VT = VTR
            QBK = Vb
            items = [(Kb, 0, ci, c) for ci, c in enumerate(CHUNKS)] + [(Qb, 2, ci, c) for ci, c in enumerate(qch)]
            n_rope = len(items)
            groups = ([[0, 1]] if l == 0 else []) + [[2, 3, 4, 5], [6, 7, 8, 9]]
            NG = len(groups)
            s_rot, s_rope, s_qf = sem("rot", n_rope), sem("rope", n_rope), sem("qf", 1)
            s_tp, s_kw, s_vt, s_u, s_um, s_S = sem("tp", 6), sem("kw", 3), sem("vt", 3), sem("u", 6), sem("um", 6), sem("S", 1)
            s_s, s_sc, s_o, s_os, s_cen, s_sq, s_var, s_rs, s_yr = (
                sem(x, n * NG) for x, n in (("rs", 2), ("rsc", 2), ("ro", 1), ("ros", 1), ("rcen", 1), ("rsq", 1), ("rvar", 1), ("rrs", 1), ("ryr", 1)))
            s_ac, s_yg = sem("reta", 2 * NG), sem("ryg", NG)
            fills = [range(0, 4), range(4, 8), range(8, 10)]
            ufills = [(0, [0, 1, 2, 3]), (0, [4, 5, 6, 7]), (0, [8]), (1, [1, 0, 9, 8]), (1, [7, 6, 5, 4]), (1, [3])]
            lo = qch[0][0]

            def pe(pt, fill):
                pt.wait_ge(*s_unit.at(u))
                for i, (x, bi, ci, (t0, n)) in enumerate(items):
                    pt.wait_ge(*s_evac.at(out_done(blks[bi], ci)))
                    if i >= 2:
                        pt.wait_ge(*s_rope.at(i - 1))
                    pt.matmul(bank[2 + i % 2][:, 0:n], k1("rot"), x[:, t0:t0 + n], start=True, stop=True).then_inc(s_rot.sem, 1)
                    fill()
                pt.wait_ge(*s_evac.at(out_done(blks[1])))
                for f, ns in enumerate(fills):
                    if f == 2:
                        pt.wait_ge(*s_vt.at(1))
                    for m, n in enumerate(ns):
                        mm = pt.transpose(bank[4 + f % 2][:, m * P:(m + 1) * P], Vb[:, n * P:(n + 1) * P], k1("ident"))
                    mm.then_inc(s_tp.sem, 1)
                    fill()
                pt.wait_ge(*s_rope.at(3))
                for f, ns in enumerate(fills):
                    if f == 2:
                        pt.wait_ge(*s_kw.at(1))
                    for m, n in enumerate(ns):
                        mm = pt.transpose(bank[6 + f % 2][:, m * P:(m + 1) * P], Kb[:, n * P:(n + 1) * P], k1("ident"))
                    mm.then_inc(s_tp.sem, 1)
                    fill()
                pt.wait_ge(*s_vt.at(3))
                pt.wait_ge(*s_kw.at(3))
                for f, (d, ns) in enumerate(ufills):
                    if f >= 2:
                        pt.wait_ge(*s_um.at(f - 1))
                    for m, n in enumerate(ns):
                        mm = pt.matmul(bank[4 + f % 2][:, m * P:(m + 1) * P], (KWF, KWB)[d][:, n * P:(n + 1) * P],
                                       VT[:, n * P:(n + 1) * P], start=True, stop=True)
                    mm.then_inc(s_u.sem, 1)
                    fill()

                def scores(g):
                    if g == 0:
                        pt.wait_ge(*s_rope.at(n_rope))
                    else:
                        pt.wait_ge(*s_sc.at(2 * g))
                    for e in range(2):
                        for m, n in enumerate(groups[g]):
                            r = slice(64 * e, 64 * e + 64)
                            mm = pt.matmul(bank[2 + e][:, m * P:(m + 1) * P], Kb[r, n * P:(n + 1) * P], Qb[r, n * P:(n + 1) * P],
                                           start=True, stop=True)
                        mm.then_inc(s_s.sem, 1)

                def outs(g):
                    if g == 0:
                        pt.wait_ge(*s_S.at(1))
                        pt.wait_ge(*s_qf.at(1))
                    if g >= 2:
                        pt.wait_ge(*s_os.at(g - 1))
                    pt.wait_ge(*s_sc.at(2 * g + 2))
                    for m, n in enumerate(groups[g]):
                        o = bank[4 + g % 2][:, m * P:(m + 1) * P]
                        c = slice(n * P, (n + 1) * P)
                        pt.matmul(o, SF[:, c], QF[:, c], start=True, stop=False)
                        pt.matmul(o, SB[:, c], QBK[:, c], start=False, stop=False)
                        for e in range(2):
                            mm = pt.matmul(o[64 * e:64 * e + 64, :], VT[:, n * P + 64 * e:n * P + 64 * e + 64],
                                           SC[:, (m * 2 + e) * P:(m * 2 + e + 1) * P], start=False, stop=True)
                    mm.then_inc(s_o.sem, 1)

                def center(g):
                    w = len(groups[g]) * P
                    pt.wait_ge(*s_os.at(g + 1))
                    if g >= 1:
                        pt.wait_ge(*s_sq.at(g))
                    pt.matmul(bank[6][:, 0:w], k1("center"), UMo[:, 0:w], start=True, stop=True).then_inc(s_cen.sem, 1)

                def var(g):
                    w = len(groups[g]) * P
                    pt.wait_ge(*s_sq.at(g + 1))
                    if g >= 1:
                        pt.wait_ge(*s_rs.at(g))
                    pt.matmul(bank[7][:, 0:w], k1("headmean"), TMP[:, 0:w], start=True, stop=True).then_inc(s_var.sem, 1)

                for g in range(NG):
                    scores(g)
                    if g >= 1:
                        center(g - 1)
                    fill()
                    outs(g)
                    if g >= 1:
                        var(g - 1)
                    fill()
                center(NG - 1)
                fill()
                var(NG - 1)

            UMo = UM

            def act(a, fill):
                for _ in items:
                    fill()
                for f, ns in enumerate(fills):
                    a.wait_ge(*s_tp.at(f + 1))
                    w = len(ns) * P
                    a.activation(VT[:, ns[0] * P:ns[0] * P + w], bank[4 + f % 2][:, 0:w], ACT.Copy).then_inc(s_vt.sem, 1)
                    fill()
                for _ in range(3 + len(ufills)):
                    fill()
                for g in range(NG):
                    w = len(groups[g]) * P
                    a.wait_ge(*s_o.at(g + 1))
                    if g == 0:
                        a.wait_ge(*s_S.at(1))
                    else:
                        a.wait_ge(*s_yr.at(g))
                    fill()
                    a.activation(UMo[:, 0:w], bank[4 + g % 2][:, 0:w], ACT.Copy).then_inc(s_os.sem, 1)
                    fill()
                    a.wait_ge(*s_cen.at(g + 1))
                    a.activation(UMo[:, 0:w], bank[6][:, 0:w], ACT.Copy).then_inc(s_ac.sem, 1)
                    if g == 0:
                        a.wait_ge(*s_rope.at(n_rope))
                    a.activation(TMP[:, 0:w], bank[6][:, 0:w], ACT.Square).then_inc(s_sq.sem, 1)
                    a.wait_ge(*s_var.at(g + 1))
                    a.activation(TMP[:, 0:w], bank[7][:, 0:w], ACT.Ln, bias=k1("eps")).then_inc(s_ac.sem, 1)
                    a.wait_ge(*s_ac.at(2 * g + 2))
                    a.activation(TMP[:, 0:w], TMP[:, 0:w], ACT.Exp, scale=-0.5).then_inc(s_rs.sem, 1)
                fill()

            def dve(v, fill):
                ch = dve_chain(v)
                v.wait_ge(*s_cs.at(32 * (l + 1)))
                if u == 0:
                    v.wait_ge(*s_pad.at(16))
                    v.wait_ge(*s_bias.at(16))
                for i, (x, bi, ci, (t0, n)) in enumerate(items):
                    v.wait_ge(*s_rot.at(i + 1))
                    ch(v.tensor_tensor(TMP[:, 0:n], bank[2 + i % 2][:, 0:n], SIN[:, t0:t0 + n], ALU.mult))
                    ch(v.tensor_tensor(x[:, t0:t0 + n], x[:, t0:t0 + n], COS[:, t0:t0 + n], ALU.mult))
                    v.tensor_tensor(x[:, t0:t0 + n], x[:, t0:t0 + n], TMP[:, 0:n], ALU.add).then_inc(s_rope.sem, 1)
                    v.wait_ge(*s_rope.at(i + 1))
                    fill()
                v.wait_ge(*s_dt[l].at(NDT))
                for _ in fills:
                    fill()
                for f, ns in enumerate(fills):
                    v.wait_ge(*s_tp.at(3 + f + 1))
                    k = len(ns)
                    src = bank[6 + f % 2][:, 0:k * P].rearrange("q (n c) -> q n c", c=P)
                    for d, kw in enumerate((KWF, KWB)):
                        dst = kw[:, ns[0] * P:(ns[0] + k) * P].rearrange("q (n c) -> q n c", c=P)
                        for e in range(2):
                            h = 2 * p + e
                            ins = v.tensor_scalar(dst[:, :, 64 * e:64 * e + 64], src[:, :, 64 * e:64 * e + 64], WK[:, d, h:h + 1], None, ALU.mult)
                            if d == 1 and e == 1:
                                ins.then_inc(s_kw.sem, 1)
                            else:
                                ch(ins)
                    fill()
                v.wait_ge(*s_kw.at(3))
                m = T // P
                v.wait_ge(*s_vt.at(3))
                nq = (T - lo) // P
                wide = lambda x: x[:, lo:T].rearrange("q (n c) -> q n c", c=P)
                ch(v.tensor_tensor(wide(QF), wide(Qb), WQ[:, 0, p, :].unsqueeze(1).to_broadcast([P, nq, P]), ALU.mult))
                v.tensor_tensor(wide(QBK), wide(Qb), WQ[:, 1, p, :].unsqueeze(1).to_broadcast([P, nq, P]), ALU.mult).then_inc(s_qf.sem, 1)
                ch(v.memset(SF[:, 0:P], 0.0))
                mask = k1("pairmask").unsqueeze(1)
                for f, (d, ns) in enumerate(ufills):
                    v.wait_ge(*s_u.at(f + 1))
                    k = len(ns)
                    v.tensor_tensor(UM[:, 0:k * P].rearrange("q (n c) -> q n c", c=P),
                                    bank[4 + f % 2][:, 0:k * P].rearrange("q (n c) -> q n c", c=P),
                                    mask.to_broadcast([P, k, P]), ALU.mult).then_inc(s_um.sem, 1)
                    v.wait_ge(*s_um.at(f + 1))
                    S = (SF, SB)[d]
                    if f == 3:
                        ch(v.memset(SB[:, P:2 * P], 0.0))
                    for i, n in enumerate(ns):
                        nxt = n + 1 if d == 0 else (n - 1 if n != 0 else 9)
                        ins = v.scalar_tensor_tensor(S[:, nxt * P:(nxt + 1) * P], S[:, n * P:(n + 1) * P], G128[:, 3 * d + p:3 * d + p + 1],
                                                     UM[:, i * P:(i + 1) * P], ALU.mult, ALU.add)
                        if f == 5 and i == k - 1:
                            ins.then_inc(s_S.sem, 1)
                            v.wait_ge(*s_S.at(1))
                        else:
                            ch(ins)
                    fill()

                def decay(g):
                    k = len(groups[g])
                    for e in range(2):
                        v.wait_ge(*s_s.at(2 * g + e + 1))
                        if g >= 1:
                            v.wait_ge(*s_o.at(g))
                        v.tensor_tensor(SC[:, 0:k * 2 * P].rearrange("q (n f c) -> q n f c", f=2, c=P)[:, :, e, :],
                                        bank[2 + e][:, 0:k * P].rearrange("q (n c) -> q n c", c=P),
                                        DT[:, 2 * p + e, :].unsqueeze(1).to_broadcast([P, k, P]), ALU.mult).then_inc(s_sc.sem, 1)

                def gate(g):
                    w = len(groups[g]) * P
                    t0 = groups[g][0] * P
                    v.wait_ge(*s_rs.at(g + 1))
                    v.wait_ge(*s_ac.at(2 * g + 2))
                    v.wait_ge(*s_evac.at(out_done(blks[3])))
                    v.tensor_tensor(Gb[:, t0:t0 + w], Gb[:, t0:t0 + w], UMo[:, 0:w], ALU.mult).then_inc(s_yg.sem, 1)
                    v.wait_ge(*s_yg.at(g + 1))
                    ins = v.tensor_tensor(Gb[:, t0:t0 + w], Gb[:, t0:t0 + w], TMP[:, 0:w], ALU.mult)
                    ins.then_inc(s_yr.sem, 1)
                    v.wait_ge(*s_yr.at(g + 1))

                decay(0)
                for g in range(NG):
                    fill()
                    if g + 1 < NG:
                        decay(g + 1)
                    gate(g)
                    fill()
                v.engine_nop().then_inc(s_unit.sem, 1)
                v.wait_ge(*s_unit.at(u + 1))
                fill()

            unit = dict(u=u, blks=allb, points=n_rope + 6 + len(ufills) + 2 * NG + 1, act_first=act_first(l, u), result=Gb, pe=pe, act=act, dve=dve)
            store(unit, 2 + p, lo)
            return unit

        def rpb_phase():
            st = SC[0:LAYERS * 45, 0:254].rearrange("q (a y) -> q a y", a=2)
            s_z, s_l = sem("padz"), sem("padl")

            def pool(g):
                g.memset(st[:, :, :], 0.0).then_inc(s_z.sem, 1)
                g.wait_ge(*s_z.at(1))
                g.dma_start(st[:, :, 48:48 + RPB_W], I["rpb"]).then_inc(s_l.sem, 16)
                g.wait_ge(*s_l.at(16))
                g.dma_start(scratch["rpb"].ap().rearrange("(r a) y -> r a y", a=2), st[:, :, :]).then_inc(s_pad.sem, 16)
                g.wait_ge(*s_pad.at(16))

            return dict(pool=pool)

        def na_unit(l, p):
            u = n_units[0]
            n_units[0] += 1
            qch = CHUNKS if l == 0 else MAIN
            Kb, Vb, Qb, Gb = PXS[u % 2]
            allb = projections(l, [6 + p, 9 + p, 18 + p, 21 + p], [CHUNKS, CHUNKS, qch, qch],
                               [plain(Kb), plain(Vb), plain(Qb, scale=HD ** -0.5), plain(Gb, ACT.Silu)])
            blks = [b for b in allb if not b["mod"]]
            lo = qch[0][0]
            rows = ([("ctx", r) for r in range(4)] if l == 0 else []) + [("grid", r) for r in range(GRID_H)]
            R = len(rows)
            fills = [("t", range(0, 4)), ("t", range(4, 8)), ("t", range(8, 10)), ("s", range(0, 4)), ("s", range(4, 7))]
            s_f, s_fl, s_nt, s_tp, s_vt = (sem(x, n) for x, n in (("nf", 32), ("nfl", 2), ("nt", 2), ("ntp", 5), ("nvt", 5)))
            s_s, s_m, s_e, s_pn, s_ta, s_tb, s_pa, s_pb, s_o, s_y = (
                sem(x, GRID_H if x == "nta" else R) for x in "ns nm ne npn nta ntb npa npb no ny".split())
            s_qa, s_qd = sem("nqa", 1), sem("nqd", 1)

            def q0(row):
                return (row[1] * GRID_W) + (CTX if row[0] == "grid" else 0)

            def band(row):
                r = row[1]
                rs = min(max(r - WIN_H // 2, 0), GRID_H - WIN_H)
                return rs, rs - r + WIN_H - 1

            def pool(g):
                g.wait_ge(*s_unit.at(u))
                for e in range(2):
                    off = ((l * 6 + 2 * p + e) * RPB_H) * 127
                    g.dma_start(NF[64 * e:64 * e + 64, :].rearrange("q (d c) -> q d c", c=GRID_W),
                                bass.AP(tensor=scratch["rpb"], offset=off, ap=[[1, 64], [127, RPB_H], [1, GRID_W]])).then_inc(s_f.sem, 16)
                if p == 0:
                    g.memset(QB, 0.0).then_inc(s_qz.sem, 1)

            def pe(pt, fill):
                pt.wait_ge(*s_unit.at(u))
                pt.wait_ge(*s_f.at(32))
                for c, (a_, n) in enumerate(((0, 512), (512, 448))):
                    pt.matmul(bank[2 + c][:, 0:n], k1("flip64"), NF[:, a_:a_ + n], start=True, stop=True).then_inc(s_fl.sem, 1)
                pt.wait_ge(*s_evac.at(out_done(blks[1])))
                for f, (kind, ns) in enumerate(fills):
                    if f >= 2:
                        pt.wait_ge(*s_vt.at(f - 1))
                    for m, n in enumerate(ns):
                        t0 = n * P if kind == "t" else CTX + 64 + n * P
                        mm = pt.transpose(bank[5 + f % 2][:, m * P:(m + 1) * P], Vb[:, t0:t0 + P], k1("ident"))
                    mm.then_inc(s_tp.sem, 1)
                    fill()
                pt.wait_ge(*s_nt.at(2))
                pt.wait_ge(*s_vt.at(5))
                pt.wait_ge(*s_qa.at(1))
                pt.wait_ge(*s_qd.at(1))

                def scores(i):
                    qb = QB[:, rows_at(i) * P:(rows_at(i) + 1) * P]
                    if rows[i][0] == "grid":
                        if i >= 2:
                            pt.wait_ge(*s_m.at(i - 1))
                        rs, _ = band(rows[i])
                        pt.matmul(bank[2 + i % 2][:, :], qb, Kb[:, CTX + rs * GRID_W:CTX + rs * GRID_W + 512], start=True, stop=True)
                    if i >= 1:
                        pt.wait_ge(*s_e.at(i))
                    pt.matmul(bank[4][:, 0:CTX], qb, Kb[:, 0:CTX], start=True, stop=True).then_inc(s_s.sem, 1)

                def turn(i):
                    pt.wait_ge(*s_pn.at(i + 1))
                    pr = PR[i % 2]
                    if i >= 1:
                        pt.wait_ge(*s_pa.at(i))
                        pt.wait_ge(*s_pb.at(i))
                    if rows[i][0] == "grid":
                        for m in range(4):
                            mm = pt.transpose(bank[5][:, m * P:(m + 1) * P], pr[:, m * P:(m + 1) * P], k1("ident"))
                        mm.then_inc(s_ta.sem, 1)
                    for m in range(2):
                        mm = pt.transpose(bank[6][:, m * P:(m + 1) * P], pr[:, (4 + m) * P:(5 + m) * P], k1("ident"))
                    mm.then_inc(s_tb.sem, 1)

                def values(i):
                    pt.wait_ge(*s_pa.at(i + 1))
                    pt.wait_ge(*s_pb.at(i + 1))
                    if i >= 1:
                        pt.wait_ge(*s_y.at(i))
                    rs, _ = band(rows[i])
                    parts = []
                    if rows[i][0] == "grid":
                        for m in range(4):
                            parts.append((m, VT[:, (2 + rs // 2 + m) * P:(3 + rs // 2 + m) * P] if rs % 2 == 0 else
                                          VS[:, (rs // 2 + m) * P:(rs // 2 + m + 1) * P]))
                    parts += [(4 + m, VT[:, m * P:(m + 1) * P]) for m in range(2)]
                    for j, (m, vv) in enumerate(parts):
                        for e in range(2):
                            mm = pt.matmul(bank[7][64 * e:64 * e + 64, 0:64], vv[:, 64 * e:64 * e + 64],
                                           PT[:, m * P + 64 * e:m * P + 64 * e + 64], start=j == 0, stop=j == len(parts) - 1)
                    mm.then_inc(s_o.sem, 1)

                scores(0)
                for i in range(R):
                    if i + 1 < R:
                        scores(i + 1)
                    fill()
                    turn(i)
                    values(i)

            def rows_at(i):
                return q0(rows[i]) // GRID_W

            def spread(eng_copy, e):
                q = QB[64 * e:64 * e + 64, (lo // GRID_W) * P:].rearrange("q (r c) -> q r c", c=P)[:, :, 64 * e:64 * e + 64]
                return eng_copy(q, Qb[64 * e:64 * e + 64, lo:].rearrange("q (r c) -> q r c", c=GRID_W))

            def act(a, fill):
                a.wait_ge(*s_unit.at(u))
                a.wait_ge(*s_qz.at(l + 1))
                a.wait_ge(*s_evac.at(out_done(blks[2])))
                spread(lambda o, x: a.activation(o, x, ACT.Copy), 0).then_inc(s_qa.sem, 1)
                for f, (kind, ns) in enumerate(fills):
                    a.wait_ge(*s_tp.at(f + 1))
                    dst = VT if kind == "t" else VS
                    a.activation(dst[:, ns[0] * P:(ns[-1] + 1) * P], bank[5 + f % 2][:, 0:len(ns) * P], ACT.Copy).then_inc(s_vt.sem, 1)
                    fill()

                def exps(i):
                    a.wait_ge(*s_m.at(i + 1))
                    if i >= 2:
                        a.wait_ge(*s_tb.at(i - 1))
                    sm = small[:, 8 * (i % 2):8 * (i % 2) + 8]
                    if rows[i][0] == "grid":
                        a.activation(PR[i % 2][:, 0:512], LL[:, (i % 2) * 512:(i % 2) * 512 + 512], ACT.Exp, bias=sm[:, 2:3],
                                     accum_out=sm[:, 3:4])
                    a.activation(PR[i % 2][:, 512:768], bank[4][:, 0:CTX], ACT.Exp, bias=sm[:, 2:3], accum_out=sm[:, 4:5]).then_inc(s_e.sem, 1)

                def evac_pt(i):
                    if i >= 1:
                        a.wait_ge(*s_o.at(i))
                    if rows[i][0] == "grid":
                        a.wait_ge(*s_ta.at(i + 1 - R + GRID_H))
                        a.activation(PT[:, 0:512], bank[5][:, :], ACT.Copy).then_inc(s_pa.sem, 1)
                    else:
                        a.sem_inc(s_pa.sem, 1)

                exps(0)
                for i in range(R):
                    if i + 1 < R:
                        exps(i + 1)
                    evac_pt(i)
                    fill()

            def dve(v, fill):
                ch = dve_chain(v)
                v.wait_ge(*s_qz.at(l + 1))
                v.wait_ge(*s_evac.at(out_done(blks[2])))
                spread(v.tensor_copy, 1).then_inc(s_qd.sem, 1)
                for c, (a_, n) in enumerate(((0, 8), (8, 7))):
                    v.wait_ge(*s_fl.at(c + 1))
                    v.tensor_tensor(NT[:, a_ * 64:(a_ + n) * 64].rearrange("q (d c) -> q d c", c=GRID_W),
                                    bank[2 + c][:, 0:n * 64].rearrange("q (d c) -> q d c", c=GRID_W),
                                    k1("wincol").unsqueeze(1).to_broadcast([P, n, GRID_W]), ALU.add).then_inc(s_nt.sem, 1)
                v.wait_ge(*s_nt.at(2))
                for _ in fills:
                    fill()
                v.wait_ge(*s_vt.at(5))

                def maxes(i):
                    v.wait_ge(*s_s.at(i + 1))
                    if i >= 2:
                        v.wait_ge(*s_e.at(i - 1))
                    sm = small[:, 8 * (i % 2):8 * (i % 2) + 8]
                    ch(v.tensor_reduce(sm[:, 1:2], bank[4][:, 0:CTX], AX_X, ALU.max))
                    if rows[i][0] == "grid":
                        _, dr = band(rows[i])
                        ch(v.tensor_tensor_reduce(out=LL[:, (i % 2) * 512:(i % 2) * 512 + 512], in0=bank[2 + i % 2][:, :],
                                                  in1=NT[:, dr * GRID_W:dr * GRID_W + 512], scale=1.0, scalar=-3.0e38,
                                                  op0=ALU.add, op1=ALU.max, accum_out=sm[:, 0:1]))
                        v.tensor_scalar(sm[:, 2:3], sm[:, 0:1], sm[:, 1:2], -1.0, ALU.max, ALU.mult).then_inc(s_m.sem, 1)
                    else:
                        v.tensor_scalar(sm[:, 2:3], sm[:, 1:2], -1.0, None, ALU.mult).then_inc(s_m.sem, 1)

                def norm(i):
                    v.wait_ge(*s_e.at(i + 1))
                    sm = small[:, 8 * (i % 2):8 * (i % 2) + 8]
                    if rows[i][0] == "grid":
                        ch(v.tensor_tensor(sm[:, 5:6], sm[:, 3:4], sm[:, 4:5], ALU.add))
                        ch(v.reciprocal(sm[:, 6:7], sm[:, 5:6]))
                        lo = 0
                    else:
                        ch(v.reciprocal(sm[:, 6:7], sm[:, 4:5]))
                        lo = 512
                    v.tensor_scalar(PR[i % 2][:, lo:768], PR[i % 2][:, lo:768], sm[:, 6:7], None, ALU.mult).then_inc(s_pn.sem, 1)

                maxes(0)
                for i in range(R):
                    norm(i)
                    if i + 1 < R:
                        maxes(i + 1)
                    v.wait_ge(*s_tb.at(i + 1))
                    if i >= 1:
                        v.wait_ge(*s_o.at(i))
                    v.tensor_copy(PT[:, 512:768], bank[6][:, 0:256]).then_inc(s_pb.sem, 1)
                    fill()
                    v.wait_ge(*s_o.at(i + 1))
                    t0 = q0(rows[i])
                    if i == 0:
                        v.wait_ge(*s_evac.at(out_done(blks[3])))
                    v.tensor_tensor(Gb[:, t0:t0 + GRID_W], bank[7][:, 0:64], Gb[:, t0:t0 + GRID_W], ALU.mult).then_inc(s_y.sem, 1)
                v.wait_ge(*s_y.at(R))
                v.engine_nop().then_inc(s_unit.sem, 1)
                v.wait_ge(*s_unit.at(u + 1))

            unit = dict(u=u, blks=allb, points=len(fills) + R, act_first=act_first(l, u), result=Gb, pe=pe, act=act, dve=dve, pool=pool)
            store(unit, 5 + p, lo)
            return unit

        def bias_phase():
            s_bl, s_bm, s_bc = sem("bl"), sem("bm"), sem("bc")
            bk_, bt_, rb_ = KWF[0:33, 0:TB], KWB[0:8, 0:TB], VTR[0:33, 0:8]

            def pool(g):
                g.dma_start(bk_, I["buckets"]).then_inc(s_bl.sem, 16)
                g.dma_start(rb_, I["relb"]).then_inc(s_bl.sem, 16)
                g.wait_ge(*s_bc.at(3))
                g.dma_start(scratch["bias"].ap(), bt_).then_inc(s_bias.sem, 16)
                g.wait_ge(*s_bias.at(16))

            def pe(p):
                p.wait_ge(*s_bl.at(32))
                for i in range(3):
                    p.matmul(bank[2 + i][0:8, 0:384], rb_, bk_[:, 384 * i:384 * i + 384], start=True, stop=True).then_inc(s_bm.sem, 1)

            def act(a):
                for i in range(3):
                    a.wait_ge(*s_bm.at(i + 1))
                    a.activation(bt_[:, 384 * i:384 * i + 384], bank[2 + i][0:8, 0:384], ACT.Copy).then_inc(s_bc.sem, 1)

            return dict(pool=pool, pe=pe, act=act)

        def out_phase(l):
            chunks = CHUNKS if l == 0 else MAIN
            lo = chunks[0][0]
            u = n_units[0]
            blks = [block(I["wout"][l, m], KT, chunks, rhs_hh) for m in range(KT)]
            NCK = len(chunks)
            s_xs = [sem(f"xs{i}", 8 * KT) for i in range(2)]
            s_hi, s_lo, s_res, s_a = (sem(x, n) for x, n in (("yhi", KT), ("ylo", KT), ("res", KT * NCK), ("lna", NCK)))
            s_mu, s_cen, s_sq, s_var, s_rs, s_n, s_fin = (
                sem(x, n * NCK) for x, n in (("mu", 1), ("cen", KT), ("sq", KT), ("var", KT), ("rstd", 1), ("nrm", KT), ("fin", KT)))
            last = PXS[1][3]
            results = [last if k == 1 else ST[6] if k == 0 else ST[k - 2] for k in range(KT)]
            korder = [2, 3, 4, 5, 6, 7, 0, 1]
            XS = ST[0:2]

            def pool(g):
                src = I["xt"] if l == 0 else scratch["x1"].ap()
                g.wait_ge(*s_lo.at(KT))
                for m in range(KT):
                    if m >= 2:
                        g.wait_ge(*s_res.at(NCK * (m - 1)))
                    g.dma_start(XS[m % 2], src[:, m, :]).then_inc(s_xs[m % 2].sem, 16)
                g.wait_ge(*s_fin.at(NCK * KT))
                g.dma_start((scratch["x1"] if l == 0 else scratch["x2"]).ap(), Y[:, :, :]).then_inc(s_xst.sem, 16)

            def pe(pt):
                pt.wait_ge(*s_lo.at(KT))
                for blk in blks:
                    whole(pe_block(pt, blk))
                for c, (t0, n) in enumerate(chunks):
                    pt.wait_ge(*s_res.at(NCK * KT))
                    for m in range(KT):
                        mm = pt.matmul(bank[2][:, 0:n], k1("mean"), Y[:, m, t0:t0 + n], start=m == 0, stop=m == KT - 1)
                    mm.then_inc(s_mu.sem, 1)
                    if c:
                        pt.wait_ge(*s_rs.at(c))
                    for m in range(KT):
                        pt.wait_ge(*s_sq.at(c * KT + m + 1))
                        mm = pt.matmul(bank[3][:, 0:n], k1("mean"), SQ[m % 2][:, 0:n], start=m == 0, stop=m == KT - 1)
                        if m == KT - 1:
                            mm.then_inc(s_var.sem, 1)
                        else:
                            mm.then_inc(s_var.sem, 1)

            def act(a):
                a.wait_ge(*s_stg.at(32 * (l + 1)))
                a.wait_ge(*s_gemm.at(blks[0]["piece"]))
                for k in korder:
                    if k == 1:
                        a.wait_ge(*s_unit.at(u))
                    a.activation(HH[:, 0, k, lo:], results[k][:, lo:], ACT.Copy).then_inc(s_hi.sem, 1)
                a.wait_ge(*mod_ready(l, 23))
                a.wait_ge(*s_lo.at(KT))
                for m, blk in enumerate(blks):
                    def evac(a, ci, t0, n, ps):
                        w = 1 if t0 < CTX else 0
                        return a.activation(Y[:, m, t0:t0 + n], ps, ACT.Copy, scale=modv[:, l, 16 + m, w:w + 1])
                    whole(act_block(a, blk, evac))
                for c, (t0, n) in enumerate(chunks):
                    for m in range(KT):
                        a.wait_ge(*s_cen.at(c * KT + m + 1))
                        i = c * KT + m
                        if i >= 2:
                            a.wait_ge(*s_var.at(i - 1))
                        a.activation(SQ[m % 2][:, 0:n], Y[:, m, t0:t0 + n], ACT.Square).then_inc(s_sq.sem, 1)
                    a.wait_ge(*s_var.at((c + 1) * KT))
                    if c:
                        a.wait_ge(*s_n.at(c * KT))
                    a.activation(RS[:, 0:n], bank[3][:, 0:n], ACT.Ln, bias=k1("eps")).then_inc(s_a.sem, 1)
                    a.wait_ge(*s_a.at(c + 1))
                    a.activation(RS[:, 0:n], RS[:, 0:n], ACT.Exp, scale=-0.5).then_inc(s_rs.sem, 1)
                    for m in range(KT):
                        a.wait_ge(*s_n.at(c * KT + m + 1))
                        a.activation(Y[:, m, t0:t0 + n], Y[:, m, t0:t0 + n], ACT.Identity, scale=lnp[:, l, 0, m:m + 1],
                                     bias=lnp[:, l, 1, m:m + 1]).then_inc(s_fin.sem, 1)

            def dve(v):
                ch = dve_chain(v)
                for i, k in enumerate(korder):
                    v.wait_ge(*s_hi.at(i + 1))
                    v.tensor_tensor(HH[:, 1, k, lo:], results[k][:, lo:], HH[:, 0, k, lo:].bitcast(F32), ALU.subtract).then_inc(s_lo.sem, 1)
                for m, blk in enumerate(blks):
                    dve_split(v, blk["b"] + SPLIT)
                    v.wait_ge(*s_xs[m % 2].at(16 * (m // 2 + 1)))
                    for ci, (t0, n) in enumerate(chunks):
                        v.wait_ge(*s_evac.at(out_done(blk, ci)))
                        v.scalar_tensor_tensor(Y[:, m, t0:t0 + n], XS[m % 2][:, t0:t0 + n], ALPHA, Y[:, m, t0:t0 + n],
                                               ALU.mult, ALU.add).then_inc(s_res.sem, 1)
                v.wait_ge(*s_res.at(NCK * KT))
                for c, (t0, n) in enumerate(chunks):
                    v.wait_ge(*s_mu.at(c + 1))
                    for m in range(KT):
                        v.tensor_tensor(Y[:, m, t0:t0 + n], Y[:, m, t0:t0 + n], bank[2][:, 0:n], ALU.subtract).then_inc(s_cen.sem, 1)
                    v.wait_ge(*s_cen.at((c + 1) * KT))
                    v.wait_ge(*s_rs.at(c + 1))
                    for m in range(KT):
                        v.tensor_tensor(Y[:, m, t0:t0 + n], Y[:, m, t0:t0 + n], RS[:, 0:n], ALU.mult).then_inc(s_n.sem, 1)

            return dict(pe=pe, act=act, dve=dve, pool=pool, s_fin=s_fin, n_fin=NCK * KT)

        phases += [first_phase(), table_phase(0), rpb_phase(), bias_phase()]
        ready = (s_x0, 16)
        for l in range(LAYERS):
            phases.append(start_phase(l, *ready))
            units = [ret_unit(l, p) for p in range(PAIRS)] + [na_unit(l, p) for p in range(PAIRS)] + [conv_unit(l, c) for c in range(2)]
            phases.append(run_units(units))
            if l + 1 < LAYERS:
                phases.append(table_phase(l + 1))
            ph = out_phase(l)
            phases.append(ph)
            ready = (ph["s_fin"], ph["n_fin"])

        if True:
            M2 = [(0, 512), (512, 512)]
            X = lambda m, t0, n: Y[:, m, CTX + t0:CTX + t0 + n]
            b1.close()
            b2 = top.enter_context(ExitStack())
            H2 = sb("H2", [P, 2, KT, SEQ], F32R, b2)
            c2 = sb("c2", [P, N2], F32, b2)
            ar2_n = 16 * 1024
            ar2 = sb("ar2", [P, ar2_n], F32, b2)
            wba = sb("wba", [P, KT, 8], F32, b2)
            wbas = sb("wbas", [P, 2, KT, 8], F32R, b2)
            cw2 = sb("cw2", [P, 12, 4], F32, b2)
            gsm = sb("gsm", [P, 16, 32], F32, b2)
            hrow = sb("hrow", [P, 9], F32, b2)
            rhs_h2 = lambda part, k, t0, n: H2[:, part, k, t0:t0 + n]

            def k2(name):
                a, n = C2[name]
                return c2[:, a:a + n]

            s_c2 = sem("const2")

            def consts2_phase():
                def pool(g):
                    g.wait_ge(*ready[0].at(ready[1]))
                    g.dma_start(c2[:, :], I["c2"]).then_inc(s_c2.sem, 16)
                    g.dma_start(gp2[:, :, :], I["gp2"]).then_inc(s_c2.sem, 16)
                    g.dma_start(wba[:, :, :], I["wba"]).then_inc(s_c2.sem, 16)
                    g.dma_start(cw2[:, :, :], I["cw2"]).then_inc(s_c2.sem, 16)
                    for i, nm in enumerate(("dtb_t", "alog_t")):
                        g.dma_start(hrow[:, 4 * i:4 * i + 4], bass.AP(tensor=I[nm], offset=0, ap=[[0, P], [1, 4]])).then_inc(s_c2.sem, 16)
                    g.dma_start(hrow[:, 8:9], I["onorm"]).then_inc(s_c2.sem, 16)
                return dict(pool=pool)

            NC = 7 * 16

            def like(x, y):
                return x if len(y.shape) == 2 else x.rearrange("q (a c) -> q a c", a=y.shape[1])

            def rms_in(gi, chunks, dst, sq, rs, tt, mean, eps, s_from, first_bank):
                nk = len(chunks) * KT
                s_sq, s_var, s_rt, s_hi, s_lo = (sem(x, nk) for x in "r_sq r_var r_t r_hi r_lo".split())
                s_rs, s_ln = sem("r_rs", len(chunks)), sem("r_ln", len(chunks))

                def act(a):
                    a.wait_ge(*s_c2.at(NC))
                    a.wait_ge(*s_from)
                    i = 0
                    for c, (t0, n) in enumerate(chunks):
                        for m in range(KT):
                            if i >= 2:
                                a.wait_ge(*s_var.at(i - 1))
                            a.activation(sq[m % 2], like(X(m, t0, n), rs), ACT.Square).then_inc(s_sq.sem, 1)
                            i += 1
                        a.wait_ge(*s_var.at((c + 1) * KT))
                        if c:
                            a.wait_ge(*s_rt.at(c * KT))
                        a.activation(rs, like(bank[first_bank][:, 0:n], rs), ACT.Ln, bias=eps).then_inc(s_ln.sem, 1)
                        a.wait_ge(*s_ln.at(c + 1))
                        a.activation(rs, rs, ACT.Exp, scale=-0.5).then_inc(s_rs.sem, 1)
                        for m in range(KT):
                            a.wait_ge(*s_rt.at(c * KT + m + 1))
                            a.activation(dst(0, m, t0, n), tt[m % 2], ACT.Copy).then_inc(s_hi.sem, 1)

                def pe(p):
                    p.wait_ge(*s_c2.at(NC))
                    for c, (t0, n) in enumerate(chunks):
                        if c:
                            p.wait_ge(*s_rs.at(c))
                        for m in range(KT):
                            p.wait_ge(*s_sq.at(c * KT + m + 1))
                            p.matmul(bank[first_bank][:, 0:n], mean, sq[m % 2], start=m == 0, stop=m == KT - 1).then_inc(s_var.sem, 1)
                    p.wait_ge(*s_lo.at(nk))

                def dve(v):
                    i = 0
                    for c, (t0, n) in enumerate(chunks):
                        v.wait_ge(*s_rs.at(c + 1))
                        for m in range(KT):
                            if i >= 2:
                                v.wait_ge(*s_lo.at(i - 1))
                            v.scalar_tensor_tensor(tt[m % 2], like(X(m, t0, n), rs), gp2[:, gi, m:m + 1], rs, ALU.mult, ALU.mult).then_inc(s_rt.sem, 1)
                            i += 1
                            v.wait_ge(*s_hi.at(i))
                            v.tensor_tensor(dst(1, m, t0, n), tt[m % 2], dst(0, m, t0, n).bitcast(F32), ALU.subtract).then_inc(s_lo.sem, 1)

                return dict(act=act, pe=pe, dve=dve, s_sq=s_sq, n=nk, s_lo=s_lo)

            def rms_out(gi, chunks, src, add, sq, rs, mean, eps, s_from, s_add, first_bank):
                nk = len(chunks) * KT
                s_sq, s_var, s_t, s_x = (sem(x, nk) for x in "p_sq p_var p_t p_x".split())
                s_rs, s_ln = sem("p_rs", len(chunks)), sem("p_ln", len(chunks))

                def act(a):
                    a.wait_ge(*s_from)
                    i = 0
                    for c, (t0, n) in enumerate(chunks):
                        for m in range(KT):
                            if i >= 2:
                                a.wait_ge(*s_var.at(i - 1))
                            a.activation(sq[m % 2], like(src(m, t0, n), rs), ACT.Square).then_inc(s_sq.sem, 1)
                            i += 1
                        a.wait_ge(*s_var.at((c + 1) * KT))
                        if c:
                            a.wait_ge(*s_t.at(c * KT))
                        a.activation(rs, like(bank[first_bank][:, 0:n], rs), ACT.Ln, bias=eps).then_inc(s_ln.sem, 1)
                        a.wait_ge(*s_ln.at(c + 1))
                        a.activation(rs, rs, ACT.Exp, scale=-0.5).then_inc(s_rs.sem, 1)

                def pe(p):
                    for c, (t0, n) in enumerate(chunks):
                        if c:
                            p.wait_ge(*s_rs.at(c))
                        for m in range(KT):
                            p.wait_ge(*s_sq.at(c * KT + m + 1))
                            p.matmul(bank[first_bank][:, 0:n], mean, sq[m % 2], start=m == 0, stop=m == KT - 1).then_inc(s_var.sem, 1)

                def dve(v):
                    for c, (t0, n) in enumerate(chunks):
                        v.wait_ge(*s_rs.at(c + 1))
                        for m in range(KT):
                            s = src(m, t0, n)
                            v.scalar_tensor_tensor(like(s, rs), like(s, rs), gp2[:, gi, m:m + 1], rs, ALU.mult, ALU.mult).then_inc(s_t.sem, 1)
                            if s_add is not None:
                                v.wait_ge(*s_add(m))
                            v.wait_ge(*s_t.at(c * KT + m + 1))
                            v.tensor_tensor(X(m, t0, n), s, add(m, t0, n), ALU.add).then_inc(s_x.sem, 1)

                return dict(act=act, pe=pe, dve=dve, s_x=s_x, n=nk)

            phases.append(consts2_phase())
            A2 = lambda i, n=1: ar2[:, i * 1024:(i + n) * 1024]
            half2 = lambda t: [t[:, 0:512], t[:, 512:1024]]
            r1 = rms_in(0, M2, lambda part, m, t0, n: H2[:, part, m, t0:t0 + n], half2(A2(0)), A2(1)[:, 0:512], half2(A2(2)),
                        k2("mean"), k2("eps"), ready[0].at(ready[1]), 2)
            phases.append(r1)

            s_ba, s_bam, s_baa, s_bad, s_wb = sem("ba"), sem("bam"), sem("baa"), sem("bad"), sem("wb")
            v3 = lambda i: gsm[:, i, :].rearrange("q (n h) -> q n h", h=GH)
            LBA = gsm[:, 0:2, :].rearrange("q a c -> q (a c)").rearrange("q (n c) -> q n c", c=8)
            BETA, Z, EZ, SP, TT, GG, GC, EGC, BE = (v3(i) for i in range(2, 11))
            EA = gsm[:, 11, 0:4]

            def ba_phase():
                def act(a):
                    a.activation(wbas[:, 0, :, :], wba[:, :, :], ACT.Copy).then_inc(s_wb.sem, 1)
                    a.wait_ge(*s_bam.at(1))
                    a.activation(LBA, bank[3][:, 0:64].rearrange("q (n c) -> q n c", c=8), ACT.Copy).then_inc(s_baa.sem, 1)
                    a.wait_ge(*s_baa.at(1))
                    a.activation(BETA, LBA[:, :, 0:4], ACT.Sigmoid).then_inc(s_baa.sem, 1)
                    a.activation(EA, hrow[:, 4:8], ACT.Exp).then_inc(s_baa.sem, 1)
                    a.wait_ge(*s_bad.at(1))
                    a.activation(EZ, TT, ACT.Exp).then_inc(s_baa.sem, 1)
                    a.wait_ge(*s_baa.at(4))
                    a.activation(SP, EZ, ACT.Ln, bias=1.0).then_inc(s_baa.sem, 1)
                    a.wait_ge(*s_bam.at(2))
                    a.activation(GC, bank[4][:, 0:32].rearrange("q (n h) -> q n h", h=GH), ACT.Copy).then_inc(s_baa.sem, 1)
                    a.wait_ge(*s_baa.at(6))
                    a.activation(EGC, GC, ACT.Exp).then_inc(s_baa.sem, 1)

                def pe(p):
                    p.wait_ge(*s_ba.at(1))
                    for n in range(NC2):
                        for k in range(KT):
                            for part, (wp, xp) in enumerate(((0, 0), (0, 1), (1, 0))):
                                mm = p.matmul(bank[3][:, 8 * n:8 * n + 8], H2[:, xp, k, n * P:(n + 1) * P], wbas[:, wp, k, :],
                                              start=k == 0 and part == 0, stop=k == KT - 1 and part == 2)
                    mm.then_inc(s_bam.sem, 1)
                    p.wait_ge(*s_ba.at(2))
                    p.matmul(bank[4][:, 0:32], k2("upto"), gsm[:, 7, :], start=True, stop=True).then_inc(s_bam.sem, 1)

                def dve(v):
                    ch = dve_chain(v)
                    v.wait_ge(*s_wb.at(1))
                    v.tensor_tensor(wbas[:, 1, :, :], wba[:, :, :], wbas[:, 0, :, :].bitcast(F32), ALU.subtract).then_inc(s_ba.sem, 1)
                    v.wait_ge(*s_baa.at(1))
                    ch(v.tensor_tensor(Z, LBA[:, :, 4:8], hrow[:, 0:4].unsqueeze(1).to_broadcast([P, NC2, GH]), ALU.add))
                    v.scalar_tensor_tensor(TT, Z, -1.0, Z, ALU.mult, ALU.min).then_inc(s_bad.sem, 1)
                    v.wait_ge(*s_baa.at(5))
                    ch(v.tensor_scalar(TT, EZ, 1.0, -1.0, ALU.add, ALU.add))
                    ch(v.tensor_scalar(TT, TT, 1e-30, None, ALU.max))
                    ch(v.reciprocal(TT, TT))
                    ch(v.tensor_tensor(TT, TT, EZ, ALU.mult))
                    ch(v.tensor_tensor(SP, SP, TT, ALU.mult))
                    ch(v.tensor_scalar(TT, EZ, -0.5, 1.0, ALU.mult, ALU.add))
                    ch(v.tensor_tensor(TT, TT, EZ, ALU.mult))
                    ch(v.tensor_tensor(SP, SP, TT, ALU.max))
                    ch(v.scalar_tensor_tensor(SP, Z, 0.0, SP, ALU.max, ALU.add))
                    v.scalar_tensor_tensor(GG, SP, -1.0, EA.unsqueeze(1).to_broadcast([P, NC2, GH]), ALU.mult, ALU.mult).then_inc(s_ba.sem, 1)
                    v.wait_ge(*s_baa.at(7))
                    v.tensor_tensor(BE, BETA, EGC, ALU.mult).then_inc(s_ba.sem, 1)
                    v.wait_ge(*s_ba.at(3))

                return dict(act=act, pe=pe, dve=dve)

            phases.append(ba_phase())

            def gdn_unit(hd):
                u = n_units[0]
                n_units[0] += 1
                Q, K, V = [A2(i) if hd % 2 == 0 else X(4 + i, 0, SEQ) for i in range(3)]
                TA, TB_, KBG, KD, VB, GB, EG, ATT, DD, AT, XX, XT, YT = (A2(3 + i) for i in range(13))
                blks = [block(I["win2"][0, 4 * i + hd], KT, M2, rhs_h2, evac=plain(x, f))
                        for i, (x, f) in enumerate(((Q, ACT.Copy), (K, ACT.Copy), (V, ACT.Copy), (X(hd, 0, SEQ), ACT.Silu)))]
                QD, OT, U, WT = EG, TB_, V, TA
                SS = Y[:, 7, 0:2 * P]
                GE, KDC = gsm[:, 12, 0:8], gsm[:, 13, 0:8]
                w4 = lambda t, hf: t[:, 512 * hf:512 * hf + 512].rearrange("q (n c) -> q n c", c=P)
                ch_ = lambda t, n: t[:, n * P:(n + 1) * P]
                bk = lambda i: bank[i][:, :].rearrange("q (n c) -> q n c", c=P)
                tokcol = lambda t, hf: t[:, 4 * hf:4 * hf + 4, hd].unsqueeze(2).to_broadcast([P, 4, P])
                rowc = lambda nm: k2(nm).unsqueeze(1).to_broadcast([P, 4, P])
                LV = INV_LEVELS - 1
                names = dict(g_gb=2, g_gbc=2, g_eg=2, g_conv=3, g_silu=3, g_sq=2, g_ss=4, g_rs=4, g_n=2, g_kd=1, g_kdc=1, g_tp=4, g_tk=2, g_tv=2,
                             g_d=4, g_dx=4, g_qk=4, g_att=2, g_a=2, g_tat=2, g_at=2, g_ot=2 * LV, g_py=2 * LV, g_y=2 * LV, g_pz=2 * LV,
                             g_x=2 * LV + 2, g_uw=4, g_u=4, g_S=NC2, g_ws=NC2, g_vn=NC2, g_kv=NC2, g_o=NC2, g_os=2, g_ov=2, g_ol=4, g_or=2)
                s = {k: sem(k, n) for k, n in names.items()}

                def pe(p, fill):
                    p.wait_ge(*s_unit.at(u))
                    p.wait_ge(*s_ba.at(3))
                    for hf in range(2):
                        for j in range(4):
                            n = 4 * hf + j
                            mm = p.matmul(bank[2 + hf][:, j * P:(j + 1) * P], GG[:, n, hd:hd + 1].to_broadcast([P, P]), k2("upto"), start=True, stop=True)
                        mm.then_inc(s["g_gb"].sem, 1)
                    for _ in range(4):
                        fill()
                    for i in range(2):
                        p.wait_ge(*s["g_sq"].at(i + 1))
                        for hf in range(2):
                            p.matmul(bank[4 + 2 * i + hf][:, :], k2("ones"), (TB_, TA)[i][:, 512 * hf:512 * hf + 512], start=True, stop=True).then_inc(s["g_ss"].sem, 1)
                            fill()
                    p.wait_ge(*s["g_gbc"].at(2))
                    p.wait_ge(*s["g_n"].at(2))
                    for hf in range(2):
                        for j in range(4):
                            mm = p.transpose(bank[2 + hf][:, j * P:(j + 1) * P], ch_(K, 4 * hf + j), k2("ident"))
                        mm.then_inc(s["g_tp"].sem, 1)
                    p.wait_ge(*s["g_silu"].at(3))
                    for hf in range(2):
                        for j in range(4):
                            mm = p.transpose(bank[4 + hf][:, j * P:(j + 1) * P], ch_(V, 4 * hf + j), k2("ident"))
                        mm.then_inc(s["g_tp"].sem, 1)
                    fill()
                    for hf in range(2):
                        for j in range(4):
                            n = 4 * hf + j
                            mm = p.matmul(bank[6 + hf][:, j * P:(j + 1) * P], ch_(K, n), ch_(Q, n), start=True, stop=True)
                        mm.then_inc(s["g_qk"].sem, 1)
                    for hf in range(2):
                        p.wait_ge(*s["g_tk"].at(hf + 1))
                        for j in range(4):
                            n = 4 * hf + j
                            mm = p.matmul(bank[2 + hf][:, j * P:(j + 1) * P], ch_(K, n), ch_(K, n), start=True, stop=True)
                        mm.then_inc(s["g_qk"].sem, 1)
                    fill()
                    for hf in range(2):
                        p.wait_ge(*s["g_tv"].at(hf + 1))
                        p.wait_ge(*s["g_a"].at(hf + 1))
                        for j in range(4):
                            mm = p.transpose(bank[4 + hf][:, j * P:(j + 1) * P], ch_(DD, 4 * hf + j), k2("ident"))
                        mm.then_inc(s["g_tat"].sem, 1)
                    fill()
                    for k in range(LV):
                        for hf in range(2):
                            p.wait_ge(*s["g_ot"].at(2 * k + hf + 1))
                            p.wait_ge(*s["g_x"].at(2 * k + hf + 1))
                            for j in range(4):
                                n = 4 * hf + j
                                mm = p.matmul(bank[2 + hf][:, j * P:(j + 1) * P], ch_(OT, n), ch_(XX, n), start=True, stop=True)
                            mm.then_inc(s["g_py"].sem, 1)
                        fill()
                        for hf in range(2):
                            p.wait_ge(*s["g_y"].at(2 * k + hf + 1))
                            for j in range(4):
                                n = 4 * hf + j
                                if k < LV - 1:
                                    p.matmul(bank[4 + hf][:, j * P:(j + 1) * P], ch_(XT, n), ch_(YT, n), start=True, stop=True)
                                mm = p.matmul(bank[6 + hf][:, j * P:(j + 1) * P], ch_(YT, n), ch_(XT, n), start=True, stop=True)
                            mm.then_inc(s["g_pz"].sem, 1)
                        fill()
                    for hf in range(2):
                        p.wait_ge(*s["g_x"].at(2 * LV + hf + 1))
                        for j in range(4):
                            n = 4 * hf + j
                            mm = p.matmul(bank[2 + hf][:, j * P:(j + 1) * P], ch_(XT, n), ch_(VB, n), start=True, stop=True)
                        mm.then_inc(s["g_uw"].sem, 1)
                        for j in range(4):
                            n = 4 * hf + j
                            mm = p.matmul(bank[4 + hf][:, j * P:(j + 1) * P], ch_(KBG, n), ch_(XT, n), start=True, stop=True)
                        mm.then_inc(s["g_uw"].sem, 1)
                    p.wait_ge(*s["g_u"].at(4))
                    for n in range(NC2):
                        S = SS[:, (n % 2) * P:(n % 2 + 1) * P]
                        p.wait_ge(*s["g_S"].at(n + 1))
                        p.matmul(bank[6 + n % 2][:, 0:P], ch_(WT, n), S, start=True, stop=True).then_inc(s["g_ws"].sem, 1)
                        p.wait_ge(*s["g_vn"].at(n + 1))
                        p.matmul(bank[2 + n % 2][:, 0:P], ch_(KD, n), ch_(U, n), start=True, stop=True).then_inc(s["g_kv"].sem, 1)
                        o = bank[4 + n // 4][:, (n % 4) * P:(n % 4 + 1) * P]
                        p.matmul(o, S, ch_(QD, n), start=True, stop=False)
                        p.matmul(o, ch_(U, n), ch_(ATT, n), start=False, stop=True).then_inc(s["g_o"].sem, 1)
                        fill()
                    for hf in range(2):
                        p.wait_ge(*s["g_os"].at(hf + 1))
                        p.matmul(bank[6 + hf][:, :], k2("headmean"), AT[:, 512 * hf:512 * hf + 512], start=True, stop=True).then_inc(s["g_ov"].sem, 1)

                def act_first(a):
                    if hd == 0:
                        a.wait_ge(*s_xst.at(32))
                        a.wait_ge(*r1["s_lo"].at(r1["n"]))

                def act(a, fill):
                    for i, x in enumerate((Q, K, V)):
                        a.wait_ge(*s["g_conv"].at(i + 1))
                        a.activation(x, (TA, TB_, KBG)[i], ACT.Silu).then_inc(s["g_silu"].sem, 1)
                    for i, x in enumerate((Q, K)):
                        a.wait_ge(*s["g_silu"].at(3))
                        a.activation((TB_, TA)[i], x, ACT.Square).then_inc(s["g_sq"].sem, 1)
                    for _ in range(4):
                        fill()
                    for hf in range(2):
                        a.wait_ge(*s["g_gb"].at(hf + 1))
                        a.activation(GB[:, 512 * hf:512 * hf + 512], bank[2 + hf][:, :], ACT.Copy).then_inc(s["g_gbc"].sem, 1)
                    a.wait_ge(*s["g_gbc"].at(2))
                    last = GB.rearrange("q (n c) -> q n c", c=P)[:, :, P - 1]
                    a.activation(GE, last, ACT.Exp).then_inc(s["g_eg"].sem, 1)
                    a.activation(EG, GB, ACT.Exp).then_inc(s["g_eg"].sem, 1)
                    a.wait_ge(*s["g_kd"].at(1))
                    a.activation(KDC, KDC, ACT.Exp).then_inc(s["g_kdc"].sem, 1)
                    for i in range(2):
                        for hf in range(2):
                            a.wait_ge(*s["g_ss"].at(2 * i + hf + 1))
                            t = (TB_, TA)[i][:, 512 * hf:512 * hf + 512]
                            a.activation(t, bank[4 + 2 * i + hf][:, :], ACT.Ln, bias=k2("eps")).then_inc(s_gln.sem, 1)
                            a.wait_ge(*s_gln.at(4 * hd + 2 * i + hf + 1))
                            a.activation(t, t, ACT.Exp, scale=-0.5).then_inc(s["g_rs"].sem, 1)
                    for _ in range(4):
                        fill()
                    for i, t in enumerate((XX, DD)):
                        for hf in range(2):
                            a.wait_ge(*s["g_d"].at(2 * i + hf + 1))
                            a.activation(w4(t, hf), w4(t, hf), ACT.Exp).then_inc(s["g_dx"].sem, 1)
                    for _ in range(3):
                        fill()
                    for hf in range(2):
                        a.wait_ge(*s["g_tat"].at(hf + 1))
                        a.activation(w4(AT, hf), bk(4 + hf), ACT.Copy).then_inc(s["g_at"].sem, 1)
                    for k in range(LV):
                        for hf in range(2):
                            a.wait_ge(*s["g_py"].at(2 * k + hf + 1))
                            a.activation(w4(YT, hf), bk(2 + hf), ACT.Copy).then_inc(s["g_y"].sem, 1)
                        fill()
                        fill()
                    for hf in range(2):
                        a.wait_ge(*s["g_uw"].at(2 * hf + 1))
                        a.activation(w4(U, hf), bk(2 + hf), ACT.Copy).then_inc(s["g_u"].sem, 1)
                        a.wait_ge(*s["g_uw"].at(2 * hf + 2))
                        a.activation(w4(WT, hf), bk(4 + hf), ACT.Copy).then_inc(s["g_u"].sem, 1)
                    for _ in range(NC2):
                        fill()
                    for hf in range(2):
                        a.wait_ge(*s["g_o"].at(4 * hf + 4))
                        a.activation(w4(DD, hf), bk(4 + hf), ACT.Copy).then_inc(s["g_ol"].sem, 1)
                        a.activation(w4(AT, hf), bk(4 + hf), ACT.Square).then_inc(s["g_os"].sem, 1)
                    for hf in range(2):
                        a.wait_ge(*s["g_ov"].at(hf + 1))
                        a.activation(w4(AT, hf), bk(6 + hf), ACT.Ln, bias=k2("eps")).then_inc(s["g_ol"].sem, 1)
                        a.wait_ge(*s["g_ol"].at(2 + hf + 1))
                        a.activation(w4(AT, hf), w4(AT, hf), ACT.Exp, scale=-0.5).then_inc(s["g_or"].sem, 1)

                def dve(v, fill):
                    ch = dve_chain(v)
                    for i, x in enumerate((Q, K, V)):
                        v.wait_ge(*s_evac.at(out_done(blks[i])))
                        t = (TA, TB_, KBG)[i]
                        w = cw2[:, 4 * i + hd, :]
                        ch(v.tensor_scalar(t, x, w[:, 3:4], None, ALU.mult))
                        for j in range(1, 4):
                            ins = v.scalar_tensor_tensor(t[:, j:], x[:, 0:SEQ - j], w[:, 3 - j:4 - j], t[:, j:], ALU.mult, ALU.add)
                            if j == 3:
                                ins.then_inc(s["g_conv"].sem, 1)
                            else:
                                ch(ins)
                        fill()
                    fill()
                    v.wait_ge(*s["g_gbc"].at(2))
                    last = GB.rearrange("q (n c) -> q n c", c=P)[:, :, P - 1]
                    v.tensor_tensor(KDC, last, GC[:, :, hd], ALU.subtract).then_inc(s["g_kd"].sem, 1)
                    for hf in range(2):
                        ch(v.tensor_tensor(w4(XX, hf), w4(GB, hf), tokcol(GC, hf), ALU.subtract))
                        v.tensor_tensor(w4(XX, hf), w4(XX, hf), rowc("causalT"), ALU.add).then_inc(s["g_d"].sem, 1)
                    for hf in range(2):
                        ch(v.tensor_tensor(w4(DD, hf), tokcol(GC, hf), w4(GB, hf), ALU.subtract))
                        v.tensor_tensor(w4(DD, hf), w4(DD, hf), rowc("strict"), ALU.add).then_inc(s["g_d"].sem, 1)
                    v.wait_ge(*s["g_rs"].at(2))
                    v.scalar_tensor_tensor(Q, Q, float(P) ** -0.5, TB_, ALU.mult, ALU.mult).then_inc(s["g_n"].sem, 1)
                    fill()
                    fill()
                    v.wait_ge(*s["g_rs"].at(4))
                    fill()
                    fill()
                    v.tensor_tensor(K, K, TA, ALU.mult).then_inc(s["g_n"].sem, 1)
                    v.wait_ge(*s["g_eg"].at(2))
                    v.wait_ge(*s["g_n"].at(2))
                    ch(v.tensor_tensor(QD, EG, Q, ALU.mult))
                    v.wait_ge(*s["g_kdc"].at(1))
                    for hf in range(2):
                        v.wait_ge(*s["g_tp"].at(hf + 1))
                        ch(v.tensor_tensor(w4(KBG, hf), bk(2 + hf), tokcol(BE, hf), ALU.mult))
                        v.tensor_tensor(w4(KD, hf), bk(2 + hf), KDC[:, 4 * hf:4 * hf + 4].unsqueeze(2).to_broadcast([P, 4, P]), ALU.mult).then_inc(s["g_tk"].sem, 1)
                    fill()
                    for hf in range(2):
                        v.wait_ge(*s["g_tp"].at(2 + hf + 1))
                        v.tensor_tensor(w4(VB, hf), bk(4 + hf), tokcol(BETA, hf), ALU.mult).then_inc(s["g_tv"].sem, 1)
                    for hf in range(2):
                        v.wait_ge(*s["g_qk"].at(hf + 1))
                        v.wait_ge(*s["g_dx"].at(hf + 1))
                        v.tensor_tensor(w4(ATT, hf), bk(6 + hf), w4(XX, hf), ALU.mult).then_inc(s["g_att"].sem, 1)
                    fill()
                    for hf in range(2):
                        v.wait_ge(*s["g_dx"].at(2 + hf + 1))
                        ch(v.tensor_tensor(w4(DD, hf), w4(DD, hf), tokcol(BETA, hf), ALU.mult))
                        v.wait_ge(*s["g_qk"].at(2 + hf + 1))
                        v.tensor_tensor(w4(DD, hf), bk(2 + hf), w4(DD, hf), ALU.mult).then_inc(s["g_a"].sem, 1)
                    fill()
                    v.wait_ge(*s["g_att"].at(2))
                    v.wait_ge(*s["g_a"].at(2))
                    for hf in range(2):
                        ch(v.tensor_tensor(w4(XX, hf), w4(DD, hf), rowc("low0"), ALU.mult))
                        ch(v.tensor_tensor(w4(XX, hf), rowc("ident"), w4(XX, hf), ALU.subtract))
                        v.wait_ge(*s["g_at"].at(hf + 1))
                        ch(v.tensor_tensor(w4(XT, hf), w4(AT, hf), rowc("lowT0"), ALU.mult))
                        v.tensor_tensor(w4(XT, hf), rowc("ident"), w4(XT, hf), ALU.subtract).then_inc(s["g_x"].sem, 1)
                    for k in range(LV):
                        for hf in range(2):
                            if k:
                                v.wait_ge(*s["g_py"].at(2 * (k - 1) + hf + 1))
                            v.tensor_tensor(w4(OT, hf), w4(AT, hf), rowc(f"lowT{k + 1}"), ALU.mult).then_inc(s["g_ot"].sem, 1)
                        fill()
                        for hf in range(2):
                            v.wait_ge(*s["g_pz"].at(2 * k + hf + 1))
                            v.wait_ge(*s["g_x"].at(2 * k + hf + 1))
                            if k < LV - 1:
                                ch(v.tensor_tensor(w4(XX, hf), w4(XX, hf), bk(4 + hf), ALU.subtract))
                            v.tensor_tensor(w4(XT, hf), w4(XT, hf), bk(6 + hf), ALU.subtract).then_inc(s["g_x"].sem, 1)
                        fill()
                    v.memset(SS, 0.0).then_inc(s["g_S"].sem, 1)
                    v.wait_ge(*s["g_u"].at(4))
                    v.wait_ge(*s["g_S"].at(1))
                    for n in range(NC2):
                        v.wait_ge(*s["g_ws"].at(n + 1))
                        v.tensor_tensor(ch_(U, n), ch_(U, n), bank[6 + n % 2][:, 0:P], ALU.subtract).then_inc(s["g_vn"].sem, 1)
                        if n + 1 < NC2:
                            v.wait_ge(*s["g_kv"].at(n + 1))
                            v.wait_ge(*s["g_S"].at(n + 1))
                            v.scalar_tensor_tensor(SS[:, ((n + 1) % 2) * P:((n + 1) % 2 + 1) * P], SS[:, (n % 2) * P:(n % 2 + 1) * P], GE[:, n:n + 1],
                                                   bank[2 + n % 2][:, 0:P], ALU.mult, ALU.add).then_inc(s["g_S"].sem, 1)
                        fill()
                    v.wait_ge(*s_evac.at(out_done(blks[3])))
                    for hf in range(2):
                        v.wait_ge(*s["g_or"].at(hf + 1))
                        ch(v.scalar_tensor_tensor(w4(DD, hf), w4(DD, hf), hrow[:, 8:9], w4(AT, hf), ALU.mult, ALU.mult))
                        y = X(hd, 512 * hf, 512)
                        ins = v.tensor_tensor(y, DD[:, 512 * hf:512 * hf + 512], y, ALU.mult)
                        if hf:
                            ins.then_inc(s_unit.sem, 1)
                            v.wait_ge(*s_unit.at(u + 1))
                        else:
                            ch(ins)

                return dict(u=u, blks=blks, points=11 + 2 * LV + NC2, act_first=act_first, pe=pe, act=act, dve=dve)

            s_gln = sem("gln", 4 * GH)

            def swa_unit(p):
                u = n_units[0]
                n_units[0] += 1
                Q, K, V = (A2(i + 13 * (p % 2)) for i in range(3))
                VT, PT = A2(3), A2(4)
                blks = [block(I["win2"][0, 16 + 4 * i + p], KT, M2, rhs_h2, evac=plain(x, scale=HD ** -0.5 if i == 0 else 1.0))
                        for i, x in enumerate((Q, K, V))]
                LL = [A2(5), A2(6)]
                PR = [A2(7), A2(8)]
                W = A2(9, 2).rearrange("q (e x) -> q e x", e=2)
                F = A2(11, 2).rearrange("q (e x) -> q e x", e=2)
                its = [(a_, e) for a_ in range(NC2) for e in range(2)]
                NI = len(its)
                halves = [[(h, 512 * h, min(512, P * (a_ + 1) - 512 * h)) for h in range((a_ + 4) // 4)] for a_, e in its]
                hfirst = [sum(len(x) for x in halves[:i]) for i in range(NI + 1)]
                NHF = hfirst[NI]
                even = lambda k: (k + 1) // 2
                s_f, s_fl, s_w, s_tp, s_vt = (sem(x, n) for x, n in (("sf", 32), ("sfl", 4), ("sw", 4), ("stp", 2), ("svt", 2)))
                s_s, s_tt = sem("ss", NHF), sem("stt", NHF)
                s_m, s_e, s_pn, s_o = (sem(x, NI) for x in "sm se spn so".split())
                s_ti, s_pa, s_pd, s_y = sem("sti", NHF), sem("spa", even(NHF)), sem("spd", NHF - even(NHF)), sem("sy", NC2)

                def pool(g):
                    g.wait_ge(*s_unit.at(u))
                    for e in range(2):
                        g.dma_start(F[:, e, :], bass.AP(tensor=scratch["bias"], offset=(2 * p + e) * TB, ap=[[1, P], [1, 1024]])).then_inc(s_f.sem, 16)

                def pe(pt, fill):
                    pt.wait_ge(*s_unit.at(u))
                    pt.wait_ge(*s_f.at(32))
                    for i in range(4):
                        pt.matmul(bank[2 + i][:, :], k2("flip"), F[:, i // 2, (i % 2) * 512:(i % 2) * 512 + 512], start=True, stop=True).then_inc(s_fl.sem, 1)
                    pt.wait_ge(*s_evac.at(out_done(blks[2])))
                    for f in range(2):
                        for m in range(4):
                            mm = pt.transpose(bank[6 + f][:, m * P:(m + 1) * P], V[:, (4 * f + m) * P:(4 * f + m + 1) * P], k2("ident"))
                        mm.then_inc(s_tp.sem, 1)
                    pt.wait_ge(*s_w.at(4))
                    pt.wait_ge(*s_vt.at(2))

                    def scores(i):
                        a_, e = its[i]
                        r = slice(64 * e, 64 * e + 64)
                        for h, k0, n in halves[i]:
                            hi = hfirst[i] + h
                            if hi >= 3:
                                pt.wait_ge(*s_tt.at(hi - 2))
                            pt.matmul(bank[2 + hi % 3][:, 0:n], Q[r, a_ * P:(a_ + 1) * P], K[r, k0:k0 + n], start=True, stop=True).then_inc(s_s.sem, 1)

                    def turn(i):
                        pt.wait_ge(*s_pn.at(i + 1))
                        for h, k0, n in halves[i]:
                            fi = hfirst[i] + h
                            if fi >= 2:
                                pt.wait_ge(*(s_pa if fi % 2 == 0 else s_pd).at(fi // 2))
                            for m in range(n // P):
                                mm = pt.transpose(bank[5 + fi % 2][:, m * P:(m + 1) * P], PR[i % 2][:, k0 + m * P:k0 + (m + 1) * P], k2("ident"))
                            mm.then_inc(s_ti.sem, 1)

                    def values(i):
                        a_, e = its[i]
                        k = hfirst[i + 1]
                        pt.wait_ge(*s_pa.at(even(k)))
                        if k > 1:
                            pt.wait_ge(*s_pd.at(k - even(k)))
                        if e == 0 and a_:
                            pt.wait_ge(*s_y.at(a_))
                        for kb in range(a_ + 1):
                            mm = pt.matmul(bank[7][64 * e:64 * e + 64, 0:P], VT[:, kb * P + 64 * e:kb * P + 64 * e + 64], PT[:, kb * P:(kb + 1) * P],
                                           start=kb == 0, stop=kb == a_)
                        mm.then_inc(s_o.sem, 1)

                    scores(0)
                    for i in range(NI):
                        if i + 1 < NI:
                            scores(i + 1)
                        fill()
                        turn(i)
                        values(i)

                def act(a, fill):
                    for i in range(4):
                        a.wait_ge(*s_fl.at(i + 1))
                        a.activation(W[:, i // 2, (i % 2) * 512:(i % 2) * 512 + 512], bank[2 + i][:, :], ACT.Copy).then_inc(s_w.sem, 1)
                    for f in range(2):
                        a.wait_ge(*s_tp.at(f + 1))
                        a.activation(VT[:, 512 * f:512 * f + 512], bank[6 + f][:, :], ACT.Copy).then_inc(s_vt.sem, 1)

                    def exps(i):
                        a_, e = its[i]
                        nk = P * (a_ + 1)
                        a.wait_ge(*s_m.at(i + 1))
                        if i >= 2:
                            a.wait_ge(*s_ti.at(hfirst[i - 1]))
                        sm = gsm[:, 14 + i % 2, :]
                        a.activation(PR[i % 2][:, 0:nk], LL[i % 2][:, 0:nk], ACT.Exp, bias=sm[:, 2:3], accum_out=sm[:, 3:4]).then_inc(s_e.sem, 1)

                    def evac(i):
                        for h, k0, n in halves[i]:
                            fi = hfirst[i] + h
                            if fi % 2 == 0:
                                a.wait_ge(*s_ti.at(fi + 1))
                                if i:
                                    a.wait_ge(*s_o.at(i))
                                a.activation(PT[:, k0:k0 + n], bank[5][:, 0:n], ACT.Copy).then_inc(s_pa.sem, 1)

                    exps(0)
                    for i in range(NI):
                        if i + 1 < NI:
                            exps(i + 1)
                        evac(i)
                        fill()

                def dve(v, fill):
                    ch = dve_chain(v)
                    v.wait_ge(*s_w.at(4))

                    def maxes(i):
                        a_, e = its[i]
                        sm = gsm[:, 14 + i % 2, :]
                        if i >= 2:
                            v.wait_ge(*s_e.at(i - 1))
                        for h, k0, n in halves[i]:
                            hi = hfirst[i] + h
                            v.wait_ge(*s_s.at(hi + 1))
                            x0 = 896 - P * a_ + k0
                            v.tensor_tensor_reduce(out=LL[i % 2][:, k0:k0 + n], in0=bank[2 + hi % 3][:, 0:n], in1=W[:, e, x0:x0 + n], scale=1.0,
                                                   scalar=-3.0e38, op0=ALU.add, op1=ALU.max, accum_out=sm[:, h:h + 1]).then_inc(s_tt.sem, 1)
                        v.wait_ge(*s_tt.at(hfirst[i + 1]))
                        if len(halves[i]) == 2:
                            v.tensor_scalar(sm[:, 2:3], sm[:, 0:1], sm[:, 1:2], -1.0, ALU.max, ALU.mult).then_inc(s_m.sem, 1)
                        else:
                            v.tensor_scalar(sm[:, 2:3], sm[:, 0:1], -1.0, None, ALU.mult).then_inc(s_m.sem, 1)

                    maxes(0)
                    for i in range(NI):
                        a_, e = its[i]
                        nk = P * (a_ + 1)
                        sm = gsm[:, 14 + i % 2, :]
                        v.wait_ge(*s_e.at(i + 1))
                        ch(v.reciprocal(sm[:, 4:5], sm[:, 3:4]))
                        v.tensor_scalar(PR[i % 2][:, 0:nk], PR[i % 2][:, 0:nk], sm[:, 4:5], None, ALU.mult).then_inc(s_pn.sem, 1)
                        if i + 1 < NI:
                            maxes(i + 1)
                        fill()
                        for h, k0, n in halves[i]:
                            fi = hfirst[i] + h
                            if fi % 2:
                                v.wait_ge(*s_ti.at(fi + 1))
                                if i:
                                    v.wait_ge(*s_o.at(i))
                                v.tensor_copy(PT[:, k0:k0 + n], bank[6][:, 0:n]).then_inc(s_pd.sem, 1)
                        if e == 1:
                            v.wait_ge(*s_o.at(i + 1))
                            ins = v.tensor_copy(X(4 + p, a_ * P, P), bank[7][:, 0:P]).then_inc(s_y.sem, 1)
                    v.wait_ge(*s_y.at(NC2))
                    v.engine_nop().then_inc(s_unit.sem, 1)
                    v.wait_ge(*s_unit.at(u + 1))

                return dict(u=u, blks=blks, points=NI, act_first=lambda a: None, pe=pe, act=act, dve=dve, pool=pool)

            phases.append(run_units([gdn_unit(hd) for hd in range(GH)] + [swa_unit(p) for p in range(SWA_PAIRS)]))

            def out2_phase():
                u = n_units[0]
                blks = [block(I["wout2"][0, m], KT, M2, rhs_h2) for m in range(KT)]
                s_hi, s_lo = sem("m_hi", KT), sem("m_lo", KT)

                def pool(g):
                    g.wait_ge(*s_unit.at(u))
                    for m in range(KT):
                        g.dma_start(A2(m), scratch["x2"].ap()[:, m, CTX:]).then_inc(s_xr[m].sem, 16)

                def pe(p):
                    p.wait_ge(*s_lo.at(KT))
                    for blk in blks:
                        whole(pe_block(p, blk))

                def act(a):
                    a.wait_ge(*s_unit.at(u))
                    for k in range(KT):
                        a.activation(H2[:, 0, k, :], X(k, 0, SEQ), ACT.Copy).then_inc(s_hi.sem, 1)
                    a.wait_ge(*s_lo.at(KT))
                    for m, blk in enumerate(blks):
                        whole(act_block(a, blk, lambda a, ci, t0, n, ps: a.activation(X(m, t0, n), ps, ACT.Copy)))

                def dve(v):
                    for k in range(KT):
                        v.wait_ge(*s_hi.at(k + 1))
                        v.tensor_tensor(H2[:, 1, k, :], X(k, 0, SEQ), H2[:, 0, k, :].bitcast(F32), ALU.subtract).then_inc(s_lo.sem, 1)
                    for blk in blks:
                        dve_split(v, blk["b"] + SPLIT)

                return dict(pool=pool, pe=pe, act=act, dve=dve, done=s_evac.at(out_done(blks[-1])))

            s_xr = [sem(f"xr{m}") for m in range(KT)]
            o2 = out2_phase()
            phases.append(o2)
            ro = rms_out(1, M2, X, lambda m, t0, n: A2(m)[:, t0:t0 + n], half2(A2(8)), A2(9)[:, 0:512], k2("mean"), k2("eps"), o2["done"],
                         lambda m: s_xr[m].at(16), 2)
            phases.append(ro)
            x_ready = ro["s_x"].at(ro["n"])

            b2.close()
            b3 = top.enter_context(ExitStack())
            HF = sb("HF", [P, 2, KT, 512], F32R, b3)
            FF = sb("FF", [P, 2, FT, 512], F32R, b3)
            O3 = sb("O3", [P, KT, 512], F32, b3)
            c3 = sb("c3", [P, P + 1], F32, b3)
            SQ3 = [Y[:, 2 * i:2 * i + 2, 0:CTX] for i in range(2)]
            RS3 = Y[:, 4:6, 0:CTX]
            s_c3 = sem("const3")

            def consts3_phase():
                def pool(g):
                    g.wait_ge(*x_ready)
                    g.dma_start(c3[:, :], I["c2"][:, C2["mean"][0]:C2["mean"][0] + P + 1]).then_inc(s_c3.sem, 16)

                def wait(e):
                    e.wait_ge(*s_c3.at(16))
                return dict(pool=pool, act=wait, pe=wait)

            phases.append(consts3_phase())
            s_outd = sem("outd")
            tail = x_ready

            def ffn(c, s_from):
                t0c = 512 * c
                one = [(t0c, 512)]
                G1, U1, FP = ([O3[:, 2 * i, :], O3[:, 2 * i + 1, :]] for i in range(3))
                tt = [O3[:, 6, :], O3[:, 7, :]]
                rin = rms_in(2, one, lambda part, m, t0, n: HF[:, part, m, :], [O3[:, 0, :], O3[:, 1, :]], O3[:, 2, :], tt,
                             c3[:, 0:P], c3[:, P:P + 1], s_from, 2)
                rh = lambda part, k, t0, n: HF[:, part, k, :]
                rf = lambda part, k, t0, n: FF[:, part, k, :]
                up = []
                for j in range(FT):
                    up.append((block(I["wgate"][0, j], KT, one, rh), block(I["wup"][0, j], KT, one, rh)))
                down = []
                for m in range(KT):
                    ks = [(0, 8), (8, 8), (16, 6)]
                    down.append([block(I["wdown"][m, :, k0 * P:(k0 + n) * P], n, one, rf, k0, k0 == 0, k0 == 16) for k0, n in ks])
                s_fp, s_fhi, s_flo = sem("f_p", FT), sem("f_hi", FT), sem("f_lo", FT)

                def pe(p):
                    for g, w in up:
                        whole(pe_block(p, g))
                        whole(pe_block(p, w))
                    p.wait_ge(*s_flo.at(FT))
                    for bl in down:
                        for blk in bl:
                            whole(pe_block(p, blk))

                def act(a):
                    def rounded(j):
                        a.wait_ge(*s_fp.at(j + 1))
                        a.activation(FF[:, 0, j, :], FP[j % 2], ACT.Copy).then_inc(s_fhi.sem, 1)

                    for j, (g, w) in enumerate(up):
                        if j >= 2:
                            a.wait_ge(*s_fp.at(j - 1))
                        whole(act_block(a, g, lambda a, ci, t0, n, ps: a.activation(G1[j % 2], ps, ACT.Silu)))
                        if j:
                            rounded(j - 1)
                        whole(act_block(a, w, lambda a, ci, t0, n, ps: a.activation(U1[j % 2], ps, ACT.Copy)))
                    rounded(FT - 1)
                    a.wait_ge(*s_flo.at(FT))
                    for m, bl in enumerate(down):
                        for blk in bl:
                            whole(act_block(a, blk, lambda a, ci, t0, n, ps: a.activation(O3[:, m, :], ps, ACT.Copy)))

                def dve(v):
                    def rest(j):
                        v.wait_ge(*s_fhi.at(j + 1))
                        v.tensor_tensor(FF[:, 1, j, :], FP[j % 2], FF[:, 0, j, :].bitcast(F32), ALU.subtract).then_inc(s_flo.sem, 1)

                    for j, (g, w) in enumerate(up):
                        dve_split(v, g["b"] + SPLIT)
                        if j:
                            rest(j - 1)
                        v.wait_ge(*s_evac.at(out_done(w)))
                        if j >= 2:
                            v.wait_ge(*s_flo.at(j - 1))
                        v.tensor_tensor(FP[j % 2], G1[j % 2], U1[j % 2], ALU.mult).then_inc(s_fp.sem, 1)
                        dve_split(v, w["b"] + SPLIT)
                    rest(FT - 1)
                    for bl in down:
                        for blk in bl:
                            dve_split(v, blk["b"] + SPLIT)

                rout = rms_out(3, one, lambda m, t0, n: O3[:, m, :], X, SQ3, RS3, c3[:, 0:P], c3[:, P:P + 1],
                               s_evac.at(out_done(down[-1][-1])), None, 2)

                def store(g):
                    g.wait_ge(*rout["s_x"].at(KT))
                    g.dma_start(out[:, :, t0c:t0c + 512], Y[:, :, CTX + t0c:CTX + t0c + 512]).then_inc(s_outd.sem, 16)

                return [rin, dict(pe=pe, act=act, dve=dve), rout, dict(pool=store)], rout["s_x"].at(KT)

            for c in range(2):
                phs, tail = ffn(c, tail)
                phases.extend(phs)

            def end_phase():
                def pool(g):
                    g.wait_ge(*s_outd.at(32))
                return dict(pool=pool)

            phases.append(end_phase())

        blk = top.enter_context(nc.Block())

        @blk.sync
        def _(sp):
            sp_weights(sp)
            for ph in phases:
                if "sp" in ph:
                    ph["sp"](sp)

        @blk.gpsimd
        def _(pool):
            for ph in phases:
                if "pool" in ph:
                    ph["pool"](pool)

        @blk.scalar
        def _(act):
            for ph in phases:
                if "act" in ph:
                    ph["act"](act)

        @blk.tensor
        def _(pe):
            for ph in phases:
                if "pe" in ph:
                    ph["pe"](pe)

        @blk.vector
        def _(dve):
            for ph in phases:
                if "dve" in ph:
                    ph["dve"](dve)


def layout(inputs):
    f = np.float32
    a = {k: np.asarray(v) for k, v in inputs.items()}
    cols = lambda w: np.ascontiguousarray(w.reshape(w.shape[0], KT, P, -1, P).transpose(0, 3, 2, 1, 4).reshape(w.shape[0], -1, P, KT * P))
    feat = lambda v: np.ascontiguousarray(v.reshape(v.shape[0], -1, P).transpose(2, 0, 1))
    x = np.concatenate([a["ctx"][0], a["x"][0]], axis=0)
    put = {
        "xt": np.ascontiguousarray(x.T.reshape(KT, P, T).transpose(1, 0, 2)),
        "c2t": np.ascontiguousarray(np.stack([a["c"][0], a["c_ctx"]], axis=1).reshape(KT, P, 2).transpose(1, 0, 2)),
        "wmod": cols(a["w_mod"]), "bmod": feat(a["b_mod"]),
        "win": cols(a["w_in"]), "wout": cols(a["w_out"]),
        "convp": np.ascontiguousarray(np.concatenate([a["conv_w"], a["conv_b"][:, None]], axis=1).reshape(LAYERS, 4, 2, P).transpose(3, 0, 2, 1)),
        "decay": np.ascontiguousarray(a["ret_decay"].reshape(LAYERS * 12, 1)),
        "decayp": np.ascontiguousarray(a["ret_decay"].reshape(LAYERS, 2, PAIRS, 2).transpose(0, 3, 1, 2).reshape(LAYERS * 12, 1)),
        "rpb": np.ascontiguousarray(a["na_rpb"].reshape(LAYERS * 45, 2, RPB_W)),
        "lnp": np.ascontiguousarray(np.stack([a["ln_g"], a["ln_b"]], axis=1).reshape(LAYERS, 2, KT, P).transpose(3, 0, 1, 2)),
    }
    w2 = a["w_in_2"]
    small = GH * P * 4
    wide = np.concatenate([w2[:, :, :small], w2[:, :, small + 2 * GH:]], axis=2)
    put.update({
        "win2": cols(wide), "wba": np.ascontiguousarray(w2[0, :, small:small + 2 * GH].reshape(KT, P, 2 * GH).transpose(1, 0, 2)),
        "cw2": np.ascontiguousarray(a["conv_w_2"][0].reshape(4, 12, P).transpose(2, 1, 0)),
        "dtb": a["dt_bias_2"], "alog": a["a_log_2"], "onorm": np.ascontiguousarray(a["onorm_g_2"].reshape(P, 1)),
        "relb": np.concatenate([a["rel_bias_2"], np.ones((1, 8), f)], axis=0),
        "gp2": np.ascontiguousarray(np.concatenate([a["g_mix_pre_2"], a["g_mix_post_2"], a["g_ffn_pre_2"], a["g_ffn_post_2"]], axis=0)
                                    .reshape(4, KT, P).transpose(2, 0, 1)),
        "wout2": cols(a["w_out_2"]), "wgate": cols(a["w_gate_2"]), "wup": cols(a["w_up_2"]),
        "wdown": np.ascontiguousarray(a["w_down_2"][0].reshape(FT, P, KT, P).transpose(2, 1, 0, 3).reshape(KT, P, FT * P)),
    })
    put.update(constants())
    return put


def program(nc, put):
    I = {}
    for name, v in put.items():
        t = nc.dram_tensor(f"in_{name}", v.shape, F32, kind="ExternalInput")
        I[name] = t.ap()
        I[name + "_t"] = t
    out = nc.dram_tensor("out_fm", [P, KT, SEQ], F32, kind="ExternalOutput").ap()
    scratch = {
        "x1": nc.dram_tensor("x1", [P, KT, T], F32, kind="Internal"),
        "br": nc.dram_tensor("branches", [P, KT, T], F32, kind="Internal"),
        "x2": nc.dram_tensor("x2", [P, KT, T], F32, kind="Internal"),
        "rpb": nc.dram_tensor("rpbpad", [LAYERS * 6 * RPB_H, 127], F32, kind="Internal"),
        "bias": nc.dram_tensor("biasrow", [8, TB], F32, kind="Internal"),
    }
    build(nc, I, out, scratch)


def kernel(**inputs):
    import concourse.bacc as bacc
    from concourse.bass_utils import run_bass_kernel_spmd as run

    put = layout(inputs)
    nc = bacc.Bacc("TRN2", target_bir_lowering=False, num_devices=1)
    program(nc, put)
    r = run(nc, [{f"in_{k}": v for k, v in put.items()}], core_ids=[0])
    fm = r.results[0]["out_fm"]
    return np.ascontiguousarray(fm.transpose(2, 1, 0).reshape(1, SEQ, D))
```

```python
from contextlib import ExitStack

import numpy as np

import concourse.bass as bass
from concourse import mybir

F32 = mybir.dt.float32
F32R = mybir.dt.float32r
ALU = mybir.AluOpType
ACT = mybir.ActivationFunctionType
AX_X = mybir.AxisListType.X

P = 128
D = 1024
KT = D // P
CTX, SEQ = 256, 1024
T = CTX + SEQ
LAYERS = 2
HD = 64
PAIRS = 3
NCH = T // P
GRID_W, GRID_H, WIN_H = 64, 16, 8
RPB_H, RPB_W = 15, 31
ALPHA = (2 * LAYERS) ** 0.25
GH = 4
NC2 = SEQ // P
SWA_PAIRS = 4
DFF = 2816
FT = DFF // P
BUCKETS = 32
TB = 1152
CHUNKS = [(0, CTX), (CTX, 512), (CTX + 512, 512)]
MAIN = CHUNKS[1:]
NEG = -1.0e30
INV_LEVELS = 7

C1 = {}
C2 = {}


def _place(table, names):
    at = 0
    for name, n in names:
        table[name] = (at, n)
        at += n
    return at


N1 = _place(C1, [("ident", P), ("rot", P), ("center", P), ("headmean", P), ("pairmask", P), ("flip64", P),
                 ("ip1", P), ("rev", P), ("fwd", P), ("bwd", P), ("mean", P), ("wincol", GRID_W),
                 ("jrev", 1), ("j", 1), ("eps", 1), ("eps2", 1)])
N2 = _place(C2, [("ident", P), ("mean", P), ("eps", 1), ("ones", P), ("headmean", P), ("upto", P), ("causalT", P),
                 ("strict", P), ("flip", P), ("low0", P)] + [(f"lowT{k}", P) for k in range(INV_LEVELS)])


def constants():
    f = np.float32
    i = np.arange(P)
    eye = np.eye(P, dtype=f)
    half = (i[:, None] // HD == i[None, :] // HD).astype(f)
    rot = np.zeros((P, P), f)
    for b in range(0, P, 32):
        for k in range(16):
            rot[b + 16 + k, b + k] = -1.0
            rot[b + k, b + 16 + k] = 1.0
    flip64 = np.zeros((P, P), f)
    for b in (0, HD):
        for k in range(HD):
            flip64[b + k, b + HD - 1 - k] = 1.0
    c = np.arange(GRID_W)
    start = np.clip(c - 8, 0, GRID_W - 16)
    inside = (c[None, :] >= start[:, None]) & (c[None, :] < start[:, None] + 16)
    wincol = np.where(inside, 0.0, NEG).astype(f)
    row = lambda v: np.broadcast_to(np.asarray(v, f), (P, P))
    parts = {
        "ident": eye, "rot": rot, "center": eye - half / HD, "headmean": half / HD, "pairmask": half, "flip64": flip64,
        "ip1": row(i + 1), "rev": row(P - i), "fwd": np.maximum(i[None, :] - i[:, None], 0),
        "bwd": np.maximum(i[:, None] - i[None, :], 0), "mean": np.full((P, P), 1.0 / D),
        "wincol": np.concatenate([wincol, wincol]), "jrev": (P - 1 - i)[:, None], "j": i[:, None],
        "eps": np.full((P, 1), 1e-5), "eps2": np.full((P, 1), 1e-6),
    }
    c1 = np.concatenate([np.asarray(parts[n], f) for n in C1], axis=1)
    parts = {
        "ident": eye, "mean": np.full((P, P), 1.0 / D), "ones": np.ones((P, P)), "headmean": np.full((P, P), 1.0 / P),
        "upto": (i[:, None] <= i[None, :]), "causalT": np.where(i[None, :] >= i[:, None], 0.0, NEG),
        "strict": np.where(i[:, None] > i[None, :], 0.0, NEG), "flip": eye[::-1], "eps": np.full((P, 1), 1e-6),
    }
    for k in range(INV_LEVELS):
        b = i >> k
        low = ((b[:, None] % 2 == 1) & (b[None, :] == b[:, None] - 1)).astype(f)
        parts[f"lowT{k}"] = low.T
        if k == 0:
            parts["low0"] = low
    c2 = np.concatenate([np.asarray(parts[n], f) for n in C2], axis=1)
    nf = HD // 4
    inv = (f(10000.0) ** (-np.arange(nf, dtype=f) / f(nf))).astype(f)
    t = np.arange(SEQ)
    ang_r = (t // GRID_W).astype(f)[:, None] * inv
    ang_c = (t % GRID_W).astype(f)[:, None] * inv
    ang = np.concatenate([ang_r, ang_r, ang_c, ang_c], axis=1).T
    ang = np.concatenate([ang, ang], axis=0).astype(f)
    cos = np.concatenate([np.ones((P, CTX), f), np.cos(ang)], axis=1)
    sin = np.concatenate([np.zeros((P, CTX), f), np.sin(ang)], axis=1)
    dist = 1023 - np.arange(TB)
    d = np.maximum(dist, 1).astype(f)
    far = 16 + (np.log(d / f(16)) / f(np.log(2048 / 16)) * f(16)).astype(np.int32)
    bucket = np.where(dist < 16, dist, np.minimum(far, 31))
    times = ((dist <= 128).astype(int) + ((dist % 4 == 0) & (dist <= 512)) + ((dist % 16 == 0) & (dist <= 2048)))
    times = np.where(dist >= 0, times, 0)
    buckets = np.zeros((BUCKETS + 1, TB), f)
    for y in range(TB):
        if times[y] > 0:
            buckets[bucket[y], y] = 1.0
            buckets[BUCKETS, y] = np.log(f(times[y]))
        else:
            buckets[BUCKETS, y] = NEG
    return {"c1": c1, "c2": c2, "cos": cos, "sin": sin, "buckets": buckets}


SHARED = """
rot=g_gb tp=g_ss u=g_tp rs=g_qk ro=g_tat rcen=g_py rvar=g_pz nfl=g_uw ntp=g_ws ns=g_kv nta=g_o=r_var ntb=g_ov
no=stp mu=sfl
rope=g_conv qf=g_n kw=g_kd um=g_tk S=g_S rsc=g_tv ryr=g_d nt=g_att nm=g_a npn=g_ot=r_lo npb=g_x=r_rt ny=g_vn
cen=p_t nrm=p_x
vt=g_gbc ros=g_eg rsq=g_silu rrs=g_sq reta=g_rs nvt=g_kdc=r_hi ne=g_dx=r_sq npa=g_at=r_rs lna=g_y fin=g_u
"""


class Count:

    def __init__(self, sem, base):
        self.sem, self.base = sem, base

    def at(self, n):
        return self.sem, self.base + n


class Chain:

    def __init__(self, eng, sem):
        self.eng, self.sem, self.n = eng, sem, 0

    def __call__(self, ins):
        self.n += 1
        ins.then_inc(self.sem, 1)
        self.eng.wait_ge(self.sem, self.n)


def build(nc, I, out, scratch):
    top = ExitStack()
    uid = [0]

    def sb(name, shape, dt=F32, stack=None):
        uid[0] += 1
        return (stack or top).enter_context(nc.sbuf_tensor(f"{name}_{uid[0]}", shape, dt))

    handles, raised = {}, {}
    signals = {}
    for a in SHARED.split():
        for name in a.split("="):
            signals[name] = a.replace("=", "_")

    def sem(name, total=0):
        if name in signals:
            name = signals[name]
        if name not in handles:
            handles[name] = top.enter_context(nc.semaphore(name))
            raised[name] = 0
        raised[name] += total
        return Count(handles[name], raised[name] - total)

    with top:
        bank = [top.enter_context(nc.psum_tensor(f"bank{i}", [P, 512], F32)) for i in range(8)]

        RAW, SPLIT = 3, 2
        raw = sb("raw", [P, RAW, KT * P])
        ws = sb("ws", [P, SPLIT, 2, KT * P], F32R)
        s_raw = [sem(f"raw{i}") for i in range(RAW)]
        s_whi, s_wlo = sem("w_hi"), sem("w_lo")
        s_gemm = sem("gemm")
        s_evac = sem("evac")
        s_unit = sem("unit")

        dmas = []
        raw_free = []
        blocks = []
        n_piece, n_out, n_units = [0], [0], [0]

        def mod_block(src, out2, bias):
            dmas.append((src, KT * P))
            blk = dict(mod=True, pe_needs=(), act_needs=(), hook=None, r=len(dmas) - 1, piece=n_piece[0], out=n_out[0], chunks=[(0, 2)],
                       evac=lambda act, ci, t0, n, ps: act.activation(out2, ps, ACT.Identity, bias=bias))
            n_piece[0] += 1
            n_out[0] += 1
            raw_free.append(s_gemm.at(n_piece[0]))
            return blk

        def block(src, kts, chunks, rhs, k0=0, first=True, last=True, evac=None, korder=None, hook=None, pe_needs=(), act_needs=()):
            b = len(blocks)
            dmas.append((src, kts * P))
            raw_free.append(s_wlo.at(b + 1))
            o0 = n_out[0]
            blocks.append(dict(mod=False, pe_needs=pe_needs, act_needs=act_needs, evac=evac, korder=korder or list(range(kts)), hook=hook, b=b, r=len(dmas) - 1, kts=kts, chunks=chunks, rhs=rhs, k0=k0, first=first, last=last,
                               piece=n_piece[0], out=o0))
            n_piece[0] += len(chunks)
            if last:
                n_out[0] += len(chunks)
            return blocks[-1]

        def sp_weights(sp):
            for r, (src, n) in enumerate(dmas):
                if r >= RAW:
                    sp.wait_ge(*raw_free[r - RAW])
                sp.dma_start(raw[:, r % RAW, 0:n], src).then_inc(s_raw[r % RAW].sem, 16)

        def act_split(act, b):
            if b >= len(blocks):
                return
            blk = blocks[b]
            n = blk["kts"] * P
            act.wait_ge(*s_raw[blk["r"] % RAW].at(16 * (blk["r"] // RAW + 1)))
            if b >= SPLIT:
                prev = blocks[b - SPLIT]
                act.wait_ge(*s_gemm.at(prev["piece"] + len(prev["chunks"])))
            act.activation(ws[:, b % SPLIT, 0, 0:n], raw[:, blk["r"] % RAW, 0:n], ACT.Copy).then_inc(s_whi.sem, 1)

        def dve_split(dve, b):
            if b >= len(blocks):
                return
            blk = blocks[b]
            n = blk["kts"] * P
            dve.wait_ge(*s_whi.at(b + 1))
            dve.tensor_tensor(ws[:, b % SPLIT, 1, 0:n], raw[:, blk["r"] % RAW, 0:n],
                              ws[:, b % SPLIT, 0, 0:n].bitcast(F32), ALU.subtract).then_inc(s_wlo.sem, 1)

        def pe_block(pe, blk, k_wait=None):
            for need in blk["pe_needs"]:
                pe.wait_ge(*need)
            if blk["mod"]:
                r = blk["r"]
                pe.wait_ge(*s_raw[r % RAW].at(16 * (r // RAW + 1)))
            else:
                b = blk["b"]
                pe.wait_ge(*s_wlo.at(b + 1))
            for ci, (t0, n) in enumerate(blk["chunks"]):
                o = blk["out"] + ci
                if (blk["mod"] or blk["first"]) and o >= 2:
                    pe.wait_ge(*s_evac.at(o - 1))
                if blk["mod"]:
                    for k in range(KT):
                        mm = pe.matmul(bank[o % 2][:, 0:n], raw[:, r % RAW, k * P:(k + 1) * P], cact[:, k, :], start=k == 0, stop=k == KT - 1)
                    yield
                else:
                    for i, k in enumerate(blk["korder"]):
                        if k_wait is not None and ci == 0:
                            k_wait(i)
                        for part, (wp, xp) in enumerate(((0, 0), (0, 1), (1, 0))):
                            mm = pe.matmul(bank[o % 2][:, 0:n], ws[:, b % SPLIT, wp, k * P:(k + 1) * P],
                                           blk["rhs"](xp, blk["k0"] + k, t0, n),
                                           start=blk["first"] and i == 0 and part == 0,
                                           stop=blk["last"] and i == blk["kts"] - 1 and part == 2)
                        if i == blk["kts"] // 2 - 1:
                            yield
                mm.then_inc(s_gemm.sem, 1)
                yield

        def act_block(act, blk, evac=None):
            evac = evac or blk["evac"]
            for ci, (t0, n) in enumerate(blk["chunks"]):
                if blk["mod"] or blk["last"]:
                    for need in blk["act_needs"] if ci == 0 else []:
                        act.wait_ge(*need)
                    act.wait_ge(*s_gemm.at(blk["piece"] + ci + 1))
                    evac(act, ci, t0, n, bank[(blk["out"] + ci) % 2][:, 0:n]).then_inc(s_evac.sem, 1)
                for b in splits_after(blk, ci):
                    act_split(act, b)
                yield

        def dve_block(dve, blk):
            for ci in range(len(blk["chunks"])):
                for b in splits_after(blk, ci):
                    dve_split(dve, b)
                if ci == len(blk["chunks"]) - 1 and blk["hook"] is not None:
                    blk["hook"](dve)
                yield

        def splits_after(blk, ci):
            if blk["mod"]:
                return []
            b, n = blk["b"], len(blk["chunks"])
            single = b + 1 < len(blocks) and len(blocks[b + 1]["chunks"]) == 1
            return ([b + 1] if ci == 0 and n > 1 else []) + ([b + 2] if ci == n - 1 and single else [])

        def whole(steps):
            for _ in steps:
                pass

        class Fill:

            def __init__(self, steps, targets):
                self.steps, self.targets, self.done, self.at = steps, targets, 0, 0

            def to(self, n):
                while self.done < n:
                    next(self.steps)
                    self.done += 1

            def __call__(self):
                if self.targets is not None:
                    self.to(self.targets[self.at])
                self.at += 1

            def finish(self, points):
                assert self.at == points, (self.at, points)
                if self.targets is not None:
                    whole(self.steps)

        def targets(unit, points, tail, limit=None):
            n = limit or sum(len(blk["chunks"]) for blk in unit["blks"])
            early = points - tail
            pe_t = [min(-(-2 * n * (i + 1) // early), 2 * n) for i in range(points)]
            act_t = [0] + [t // 2 for t in pe_t[:-1]]
            return pe_t, act_t, act_t

        def project_pe(pe, unit):
            for blk in unit["blks"]:
                yield from pe_block(pe, blk)

        def project_act(act, unit):
            if unit["u"] >= 1:
                act.wait_ge(*s_unit.at(unit["u"] - 1))
            unit["act_first"](act)
            for blk in unit["blks"]:
                yield from act_block(act, blk)

        def project_dve(dve, unit):
            for blk in unit["blks"]:
                yield from dve_block(dve, blk)

        def run_units(units):
            def program(which, project):
                def run(eng):
                    whole(project(eng, units[0]))
                    for i, un in enumerate(units):
                        nxt = units[i + 1] if i + 1 < len(units) else None
                        fill = Fill(project(eng, nxt) if nxt else None,
                                    targets(nxt, un["points"], un.get("tail", 0), un.get("limit"))[("pe", "act", "dve").index(which)] if nxt else None)
                        un[which](eng, fill)
                        fill.finish(un["points"])
                return run

            def pool(g):
                for i, un in enumerate(units):
                    if "pool" in un:
                        un["pool"](g)
                    if i and "stored" in units[i - 1]:
                        g.wait_ge(*units[i - 1]["stored"])
                    if "store" in un:
                        g.wait_ge(*s_unit.at(un["u"] + 1))
                        un["store"](g)

            return dict(pe=program("pe", project_pe), act=program("act", project_act), dve=program("dve", project_dve), pool=pool)

        def out_done(blk, ci=None):
            return blk["out"] + (len(blk["chunks"]) if ci is None else ci + 1)

        order = {}

        def dve_chain(v):
            if "dve" not in order:
                order["dve"] = Chain(v, sem("dve_order").sem)
            return order["dve"]

        Y = sb("Y", [P, KT, T])
        gp2 = sb("gp2", [P, 4, KT])
        s_const, s_gp = sem("const"), sem("gains")
        phases = []

        M2 = [(0, 512), (512, 512)]

        def X(m, t0, n):
            return Y[:, m, CTX + t0:CTX + t0 + n]

        def like(x, y):
            return x if len(y.shape) == 2 else x.rearrange("q (a c) -> q a c", a=y.shape[1])

        class NormIn:

            def __init__(self, gi, chunks, dst, sq, rs, tt, mean, eps, bank0):
                self.gi, self.chunks, self.dst, self.sq, self.rs, self.tt = gi, chunks, dst, sq, rs, tt
                self.mean, self.eps, self.bank0 = mean, eps, bank0
                nk = len(chunks) * KT
                self.s_sq, self.s_var, self.s_rt, self.s_hi, self.s_lo = (sem(x, nk) for x in "r_sq r_var r_rt r_hi r_lo".split())
                self.s_rs, self.s_ln = sem("r_rs", len(chunks)), sem("r_ln", len(chunks))
                self.done = self.s_lo.at(nk)

            def act_squares(self, a, c, need=None):
                t0, n = self.chunks[c]
                for m in range(KT):
                    i = c * KT + m
                    if need is not None:
                        a.wait_ge(*need(m))
                    if i >= 2:
                        a.wait_ge(*self.s_var.at(i - 1))
                    sq = self.sq[i % 2]
                    a.activation(sq, like(X(m, t0, n), sq), ACT.Square).then_inc(self.s_sq.sem, 1)

            def pe_var(self, p, c):
                t0, n = self.chunks[c]
                for m in range(KT):
                    i = c * KT + m
                    p.wait_ge(*self.s_sq.at(i + 1))
                    p.matmul(bank[self.bank0 + c][:, 0:n], self.mean(), self.sq[i % 2], start=m == 0, stop=m == KT - 1).then_inc(self.s_var.sem, 1)

            def act_rstd(self, a, c):
                n = self.chunks[c][1]
                rs = self.rs[c]
                a.wait_ge(*self.s_var.at((c + 1) * KT))
                a.activation(rs, like(bank[self.bank0 + c][:, 0:n], rs), ACT.Ln, bias=self.eps()).then_inc(self.s_ln.sem, 1)
                a.wait_ge(*self.s_ln.at(c + 1))
                a.activation(rs, rs, ACT.Exp, scale=-0.5).then_inc(self.s_rs.sem, 1)

            def act_hi(self, a, c):
                t0, n = self.chunks[c]
                for m in range(KT):
                    i = c * KT + m
                    a.wait_ge(*self.s_rt.at(i + 1))
                    a.activation(self.dst(0, m, t0, n), self.tt[i % 2][:, 0:n], ACT.Copy).then_inc(self.s_hi.sem, 1)

            def dve_scale(self, v, c):
                t0, n = self.chunks[c]
                rs = self.rs[c]

                def scaled(m):
                    i = c * KT + m
                    tt = self.tt[i % 2][:, 0:n]
                    if i >= 2:
                        v.wait_ge(*self.s_lo.at(i - 1))
                    v.scalar_tensor_tensor(like(tt, rs), like(X(m, t0, n), rs), gp2[:, self.gi, m:m + 1], rs, ALU.mult, ALU.mult).then_inc(self.s_rt.sem, 1)

                v.wait_ge(*self.s_rs.at(c + 1))
                scaled(0)
                for m in range(KT):
                    i = c * KT + m
                    if m + 1 < KT:
                        scaled(m + 1)
                    v.wait_ge(*self.s_hi.at(i + 1))
                    v.tensor_tensor(self.dst(1, m, t0, n), self.tt[i % 2][:, 0:n], self.dst(0, m, t0, n).bitcast(F32), ALU.subtract).then_inc(self.s_lo.sem, 1)

        class NormOut:

            def __init__(self, gi, chunks, src, add, sq, rs, mean, eps, bank0):
                self.gi, self.chunks, self.src, self.add, self.sq, self.rs = gi, chunks, src, add, sq, rs
                self.mean, self.eps, self.bank0 = mean, eps, bank0
                nk = len(chunks) * KT
                self.s_sq, self.s_var, self.s_t, self.s_x = (sem(x, nk) for x in "p_sq p_var p_t p_x".split())
                self.s_rs, self.s_ln = sem("p_rs", len(chunks)), sem("p_ln", len(chunks))

            def x_done(self, c, m):
                return self.s_x.at(c * KT + m + 1)

            def act_square(self, a, c, m, need):
                t0, n = self.chunks[c]
                i = c * KT + m
                a.wait_ge(*need)
                if i >= 2:
                    a.wait_ge(*self.s_var.at(i - 1))
                sq = self.sq[i % 2]
                a.activation(sq, like(self.src(m, t0, n), sq), ACT.Square).then_inc(self.s_sq.sem, 1)

            def pe_var(self, p, c, m):
                t0, n = self.chunks[c]
                i = c * KT + m
                p.wait_ge(*self.s_sq.at(i + 1))
                p.matmul(bank[self.bank0 + c][:, 0:n], self.mean(), self.sq[i % 2], start=m == 0, stop=m == KT - 1).then_inc(self.s_var.sem, 1)

            def act_rstd(self, a, c):
                n = self.chunks[c][1]
                a.wait_ge(*self.s_var.at((c + 1) * KT))
                if c:
                    a.wait_ge(*self.s_t.at(c * KT))
                a.activation(self.rs, like(bank[self.bank0 + c][:, 0:n], self.rs), ACT.Ln, bias=self.eps()).then_inc(self.s_ln.sem, 1)
                a.wait_ge(*self.s_ln.at(c + 1))
                a.activation(self.rs, self.rs, ACT.Exp, scale=-0.5).then_inc(self.s_rs.sem, 1)

            def dve_add(self, v, c, tiles=range(KT)):
                t0, n = self.chunks[c]
                v.wait_ge(*self.s_rs.at(c + 1))
                for m in tiles:
                    x = self.src(m, t0, n)
                    v.scalar_tensor_tensor(like(x, self.rs), like(x, self.rs), gp2[:, self.gi, m:m + 1], self.rs, ALU.mult, ALU.mult).then_inc(self.s_t.sem, 1)
                for m in tiles:
                    v.wait_ge(*self.s_t.at(c * KT + m + 1))
                    v.tensor_tensor(X(m, t0, n), self.src(m, t0, n), self.add(m, t0, n), ALU.add).then_inc(self.s_x.sem, 1)

        b1 = top.enter_context(ExitStack())
        HH = sb("HH", [P, 2, KT, T], F32R, b1)
        c1 = sb("c1", [P, N1], F32, b1)
        arena_n = 11008
        arena = sb("arena", [P, arena_n], F32, b1)
        modv = sb("modv", [P, LAYERS, 24, 2], F32, b1)
        cact = sb("cact", [P, KT, 2], F32, b1)
        bmod = sb("bmod", [P, LAYERS, 24], F32, b1)
        lnp = sb("lnp", [P, LAYERS, 2, KT], F32, b1)
        convp = sb("convp", [P, LAYERS, 2, 4], F32, b1)
        LG = sb("LG", [P, LAYERS, 18], F32, b1)
        DT = sb("DT", [P, 6, P], F32, b1)
        WQ = sb("WQ", [P, 2, PAIRS, P], F32, b1)
        WK = sb("WK", [P, 2, 6], F32, b1)
        G128 = sb("G128", [P, 6], F32, b1)
        small = sb("small", [P, 16], F32, b1)
        NF = sb("NF", [P, RPB_H * GRID_W], F32, b1)

        def k1(name):
            a, n = C1[name]
            return c1[:, a:a + n]

        arena_at = [0]

        def spot(n, at=None):
            at = arena_at[0] if at is None else at
            arena_at[0] = at + n
            assert at + n <= arena_n, at + n
            return arena[:, at:at + n]

        PXS = [[Y[:, 4 * i + j, :] for j in range(4)] for i in range(2)]
        TMP = spot(512)
        COS, SIN, QF = spot(T), spot(T), spot(T)
        UM, SC = spot(512), spot(1024)
        KWF, KWB, VTR, SF = spot(T), spot(T), spot(T), spot(T)
        SB = KWF
        QB = spot(20 * P, 0)
        NT = spot(RPB_H * GRID_W)
        PR = [spot(768), spot(768)]
        VT = spot(T)
        VS, LL, PT = spot(7 * P), spot(1024), spot(768)
        ST = [spot(T, j * T) for j in range(7)]
        CT = spot(T)
        RS = [spot(512), ST[5][:, 0:512]]
        SQ = [ST[4][:, 0:512], ST[4][:, 512:1024]]
        lgt = UM[:, 0:4 * LAYERS * 18].rearrange("q (a c) -> q a c", a=4)
        HT = QF

        def rhs_hh(part, k, t0, n):
            return HH[:, part, k, t0:t0 + n]

        s_x0 = sem("x0")

        s_lg, s_bm1 = sem("lg"), sem("bm1")
        s_xst = sem("xst")
        s_h, s_hhi = sem("h"), sem("hhi")
        s_dt = [sem(f"dt{l}") for l in range(LAYERS)]
        s_tabd = sem("tabd")
        s_cs = sem("cossin")
        modb = {}

        def mod_block_of(l, m):
            modb[l, m] = mod_block(I["wmod"][l, m], modv[:, l, m, :], bmod[:, l, m:m + 1])
            return modb[l, m]

        def mod_ready(l, m):
            return s_evac.at(out_done(modb[l, m]))

        def first_phase():
            for k in range(KT):
                mod_block_of(0, k)
                mod_block_of(0, 8 + k)
            s_achain, s_e = sem("modact"), sem("lge")
            NCONST = 5 + LAYERS * 3

            def pool(g):
                g.dma_start(cact[:, :, :], I["c2t"]).then_inc(s_const.sem, 16)
                g.dma_start(bmod[:, :, :], I["bmod"]).then_inc(s_const.sem, 16)
                rd = I["decay_t"]
                for l in range(LAYERS):
                    g.dma_start(LG[:, l, 0:12], bass.AP(tensor=rd, offset=l * 12, ap=[[0, P], [1, 12]])).then_inc(s_const.sem, 16)
                    for e in range(2):
                        g.dma_start(LG[64 * e:64 * e + 64, l, 12:18],
                                    bass.AP(tensor=I["decayp_t"], offset=(l * 2 + e) * 6, ap=[[0, 64], [1, 6]])).then_inc(s_const.sem, 16)
                g.dma_start(c1[:, :], I["c1"]).then_inc(s_const.sem, 16)
                g.dma_start(lnp[:, :, :, :], I["lnp"]).then_inc(s_const.sem, 16)
                g.dma_start(convp[:, :, :, :], I["convp"]).then_inc(s_const.sem, 16)
                g.dma_start(Y[:, :, :], I["xt"]).then_inc(s_x0.sem, 16)
                g.dma_start(gp2[:, :, :], I["gp2"]).then_inc(s_gp.sem, 16)

            def act(a):
                a.wait_ge(*s_const.at(16 * NCONST))
                ch = Chain(a, s_achain.sem)
                ch(a.activation(cact[:, :, :], cact[:, :, :], ACT.Silu))
                a.wait_ge(*s_e.at(1))
                ch(a.activation(lgt[:, 1, :], lgt[:, 0, :], ACT.Exp))
                ch(a.activation(lgt[:, 2, :], lgt[:, 1, :], ACT.Ln, bias=1.0))

            def pe(p):
                p.wait_ge(*s_achain.at(1))

            def dve(v):
                ch = dve_chain(v)
                v.wait_ge(*s_const.at(16 * NCONST))
                v.tensor_scalar(bmod[:, :, 8:16], bmod[:, :, 8:16], 1.0, None, ALU.add).then_inc(s_bm1.sem, 1)
                x = LG[:, :, :].rearrange("p l c -> p (l c)")
                v.scalar_tensor_tensor(lgt[:, 0, :], x, -1.0, x, ALU.mult, ALU.min).then_inc(s_e.sem, 1)
                v.wait_ge(*s_achain.at(3))
                e, l1 = lgt[:, 1, :], lgt[:, 2, :]
                t = lgt[:, 3, :]
                ch(v.tensor_scalar(t, e, 1.0, -1.0, ALU.add, ALU.add))
                ch(v.tensor_scalar(t, t, 1e-30, None, ALU.max))
                ch(v.reciprocal(t, t))
                ch(v.tensor_tensor(t, t, e, ALU.mult))
                ch(v.tensor_tensor(l1, l1, t, ALU.mult))
                ch(v.tensor_scalar(t, e, -0.5, 1.0, ALU.mult, ALU.add))
                ch(v.tensor_tensor(t, t, e, ALU.mult))
                ch(v.tensor_tensor(l1, l1, t, ALU.max))
                v.scalar_tensor_tensor(x, x, 0.0, l1, ALU.min, ALU.subtract).then_inc(s_lg.sem, 1)
                v.wait_ge(*s_lg.at(1))

            return dict(pool=pool, act=act, pe=pe, dve=dve)

        def table_phase(l):
            u = n_units[0]

            def act(a):
                a.wait_ge(*s_tabd.at(l + 1))
                a.activation(DT[:, :, :], DT[:, :, :], ACT.Exp).then_inc(s_dt[l].sem, 1)
                lp = LG[:, l, 12:18]
                for d, src in enumerate(("ip1", "rev")):
                    for p in range(PAIRS):
                        a.activation(WQ[:, d, p, :], k1(src), ACT.Exp, scale=LG[:, l, 12 + 3 * d + p:13 + 3 * d + p]).then_inc(s_dt[l].sem, 1)
                a.activation(WK[:, 0, :], LG[:, l, 0:6], ACT.Exp, scale=k1("jrev")).then_inc(s_dt[l].sem, 1)
                a.activation(WK[:, 1, :], LG[:, l, 6:12], ACT.Exp, scale=k1("j")).then_inc(s_dt[l].sem, 1)
                a.activation(G128[:, :], lp, ACT.Exp, scale=float(P)).then_inc(s_dt[l].sem, 1)

            def dve(v):
                ch = dve_chain(v)
                v.wait_ge(*s_lg.at(1))
                if l:
                    v.wait_ge(*s_unit.at(u))
                for h in range(6):
                    ch(v.tensor_scalar(DT[:, h, :], k1("fwd"), LG[:, l, h:h + 1], None, ALU.mult))
                    ins = v.scalar_tensor_tensor(DT[:, h, :], k1("bwd"), LG[:, l, 6 + h:7 + h], DT[:, h, :], ALU.mult, ALU.add)
                    if h < 5:
                        ch(ins)
                    else:
                        ins.then_inc(s_tabd.sem, 1)
                        v.wait_ge(*s_tabd.at(l + 1))

            return dict(act=act, dve=dve)

        def start_phase():
            segs = [(0, CTX, 1), (CTX, SEQ, 0)]

            def pool(g):
                load_angles(g)

            def act(a):
                a.wait_ge(*s_bm1.at(1))
                a.wait_ge(*s_x0.at(16))
                for k in range(KT):
                    whole(act_block(a, modb[0, k]))
                    whole(act_block(a, modb[0, 8 + k]))
                    a.wait_ge(*mod_ready(0, 8 + k))
                    for si, (t0, n, w) in enumerate(segs):
                        ins = a.activation(HH[:, 0, k, t0:t0 + n], Y[:, k, t0:t0 + n], ACT.Identity,
                                           scale=modv[:, 0, 8 + k, w:w + 1], bias=modv[:, 0, k, w:w + 1])
                        ins.then_inc(s_hhi.sem, 1)
                act_split(a, 0)

            def dve(v):
                ch = dve_chain(v)
                v.wait_ge(*s_x0.at(16))
                i = 0
                for k in range(KT):
                    v.wait_ge(*mod_ready(0, 8 + k))
                    for si, (t0, n, w) in enumerate(segs):
                        tt = HT[:, 0:n]
                        ch(v.tensor_scalar(tt, Y[:, k, t0:t0 + n], modv[:, 0, 8 + k, w:w + 1], modv[:, 0, k, w:w + 1], ALU.mult, ALU.add))
                        i += 1
                        v.wait_ge(*s_hhi.at(i))
                        v.tensor_tensor(HH[:, 1, k, t0:t0 + n], tt, HH[:, 0, k, t0:t0 + n].bitcast(F32), ALU.subtract).then_inc(s_h.sem, 1)
                        v.wait_ge(*s_h.at(i))
                dve_split(v, 0)

            def pe(p):
                for k in range(KT):
                    whole(pe_block(p, modb[0, k]))
                    whole(pe_block(p, modb[0, 8 + k]))
                p.wait_ge(*s_h.at(16))

            return dict(act=act, dve=dve, pe=pe, pool=pool)

        def load_angles(g):
            g.dma_start(COS, I["cos"]).then_inc(s_cs.sem, 16)
            g.dma_start(SIN, I["sin"]).then_inc(s_cs.sem, 16)

        mods_left = [(0, 16 + k) for k in range(KT)] + [(1, m) for m in range(24)]

        def projections(l, cols, chunks, evacs):
            out, got = [], []
            apart = l > 0 and cols[0] == 0
            for c, ch, ev in zip(cols, chunks, evacs):
                first = ch[:-1] if apart else ch
                out.append(block(I["win"][l, c], KT, first, rhs_hh, evac=ev, pe_needs=[s_h.at(32)] if apart else (),
                                 act_needs=[s_h.at(32), s_xst.at(32)] if apart else ()))
                got.append([s_evac.at(out_done(out[-1], ci)) for ci in range(len(first))])
                if l == 0:
                    out.append(mod_block_of(*mods_left.pop(0)))
            if apart:
                for c, ch, ev, g in zip(cols, chunks, evacs, got):
                    out.append(block(I["win"][l, c], KT, ch[-1:], rhs_hh, evac=ev, pe_needs=[s_h.at(40)], act_needs=[s_h.at(40), s_xst.at(48)]))
                    g.append(s_evac.at(out_done(out[-1])))
            return out, got

        def plain(dst, func=ACT.Copy, scale=1.0):
            return lambda act, ci, t0, n, ps: act.activation(dst[:, t0:t0 + n], ps, func, scale=scale)

        s_pad, s_bias, s_qz = sem("pad"), sem("biasd"), sem("qzero")
        s_brd = sem("branch")
        n_stored = [0]

        def store(unit, tile, lo):
            n_stored[0] += 1
            unit["stored"] = s_brd.at(16 * n_stored[0])
            unit["store"] = lambda g: g.dma_start(scratch["br"].ap()[:, tile, lo:], unit["result"][:, lo:]).then_inc(s_brd.sem, 16)

        NDT = 10

        def act_first(l, u):
            def run(a):
                if u == 0:
                    a.wait_ge(*s_h.at(16))
            return run

        def gate_into(dst, l, u):
            stored = 6 * l + u % 8 - 1

            def evac(act, ci, t0, n, ps):
                if ci == 0 and u % 8 >= 2:
                    act.wait_ge(*s_brd.at(16 * stored))
                return act.activation(dst[:, t0:t0 + n], ps, ACT.Silu)
            return evac

        s_stg = sem("staged")

        def conv_unit(l, c):
            u = n_units[0]
            n_units[0] += 1
            chunks = CHUNKS if l == 0 else MAIN
            segs = ([(0, CTX)] if l == 0 else []) + [(CTX, T)]
            lo = segs[0][0]
            h, cg, bg, z = PXS[u % 2]
            blks, got = projections(l, [24 + c, 28 + c, 26 + c, 30 + c], [chunks] * 4, [plain(h), plain(cg), plain(bg), gate_into(z, l, u)])
            prods = [b for b in blks if not b["mod"]]
            tmp = (CT, ST[6])[c]
            w = convp[:, l, c, :]

            def pool(g):
                if c == 0:
                    g.wait_ge(*s_unit.at(u))
                    g.wait_ge(*stored_before)
                    g.dma_start(arena[:, 0:6 * T].rearrange("q (m t) -> q m t", t=T)[:, :, lo:], scratch["br"].ap()[:, 2:8, lo:]).then_inc(s_stg.sem, 16)

            def taps(v):
                ch = dve_chain(v)
                if c == 0:
                    v.wait_ge(*s_unit.at(u))
                v.wait_ge(*got[1][-1])
                ch(v.tensor_tensor(h[:, lo:], h[:, lo:], cg[:, lo:], ALU.mult))
                ch(v.tensor_scalar(tmp[:, lo:], h[:, lo:], w[:, 1:2], w[:, 3:4], ALU.mult, ALU.add))
                for a_, b_ in segs:
                    ch(v.scalar_tensor_tensor(tmp[:, a_ + 1:b_], h[:, a_:b_ - 1], w[:, 0:1], tmp[:, a_ + 1:b_], ALU.mult, ALU.add))
                    ch(v.scalar_tensor_tensor(tmp[:, a_:b_ - 1], h[:, a_ + 1:b_], w[:, 2:3], tmp[:, a_:b_ - 1], ALU.mult, ALU.add))

            def gate(v):
                ch = dve_chain(v)
                v.wait_ge(*got[2][-1])
                ch(v.tensor_tensor(tmp[:, lo:], tmp[:, lo:], bg[:, lo:], ALU.mult))

            if c == 1:
                prods[1]["hook"], prods[2]["hook"] = taps, gate

            def nothing(eng, fill):
                fill()

            def dve(v, fill):
                if c == 0:
                    taps(v)
                    gate(v)
                v.wait_ge(*got[3][-1])
                v.tensor_tensor(z[:, lo:], tmp[:, lo:], z[:, lo:], ALU.mult).then_inc(s_unit.sem, 1)
                v.wait_ge(*s_unit.at(u + 1))
                fill()

            stored_before = s_brd.at(16 * n_stored[0])
            return dict(u=u, blks=blks, points=1, act_first=act_first(l, u), pe=nothing, act=nothing, dve=dve, pool=pool)

        def ret_unit(l, p):
            u = n_units[0]
            n_units[0] += 1
            qch = CHUNKS if l == 0 else MAIN
            Kb, Vb, Qb, Gb = PXS[u % 2]
            allb, got = projections(l, [p, 3 + p, 12 + p, 15 + p], [CHUNKS, CHUNKS, qch, qch],
                               [plain(Kb, scale=HD ** -0.5), plain(Vb), plain(Qb), gate_into(Gb, l, u)])
            VT = VTR
            QBK = Vb
            items = [(Kb, 0, ci, c) for ci, c in enumerate(CHUNKS)] + [(Qb, 2, ci, c) for ci, c in enumerate(qch)]
            n_rope = len(items)
            groups = ([[0, 1]] if l == 0 else []) + [[2, 3, 4, 5], [6, 7, 8, 9]]
            NG = len(groups)
            s_rot, s_rope, s_qf = sem("rot", n_rope), sem("rope", n_rope), sem("qf", 1)
            s_tp, s_kw, s_vt, s_u, s_um, s_S = sem("tp", 6), sem("kw", 3), sem("vt", 3), sem("u", 6), sem("um", 6), sem("S", 1)
            s_s, s_sc, s_o, s_os, s_cen, s_sq, s_var, s_rs, s_yr = (
                sem(x, n * NG) for x, n in (("rs", 2), ("rsc", 2), ("ro", 1), ("ros", 1), ("rcen", 1), ("rsq", 1), ("rvar", 1), ("rrs", 1), ("ryr", 1)))
            s_ac, s_yg = sem("reta", 2 * NG), sem("ryg", NG)
            fills = [range(0, 4), range(4, 8), range(8, 10)]
            ufills = [(0, [0, 1, 2, 3]), (0, [4, 5, 6, 7]), (0, [8]), (1, [1, 0, 9, 8]), (1, [7, 6, 5, 4]), (1, [3])]
            lo = qch[0][0]

            def pe(pt, fill):
                pt.wait_ge(*s_unit.at(u))
                for i, (x, bi, ci, (t0, n)) in enumerate(items):
                    pt.wait_ge(*got[bi][ci])
                    if i >= 2:
                        pt.wait_ge(*s_rope.at(i - 1))
                    pt.matmul(bank[2 + i % 2][:, 0:n], k1("rot"), x[:, t0:t0 + n], start=True, stop=True).then_inc(s_rot.sem, 1)
                    fill()
                pt.wait_ge(*got[1][-1])
                for f, ns in enumerate(fills):
                    if f == 2:
                        pt.wait_ge(*s_vt.at(1))
                    for m, n in enumerate(ns):
                        mm = pt.transpose(bank[4 + f % 2][:, m * P:(m + 1) * P], Vb[:, n * P:(n + 1) * P], k1("ident"))
                    mm.then_inc(s_tp.sem, 1)
                    fill()
                pt.wait_ge(*s_rope.at(3))
                for f, ns in enumerate(fills):
                    if f == 2:
                        pt.wait_ge(*s_kw.at(1))
                    for m, n in enumerate(ns):
                        mm = pt.transpose(bank[6 + f % 2][:, m * P:(m + 1) * P], Kb[:, n * P:(n + 1) * P], k1("ident"))
                    mm.then_inc(s_tp.sem, 1)
                    fill()
                pt.wait_ge(*s_vt.at(3))
                pt.wait_ge(*s_kw.at(3))
                for f, (d, ns) in enumerate(ufills):
                    if f >= 2:
                        pt.wait_ge(*s_um.at(f - 1))
                    for m, n in enumerate(ns):
                        mm = pt.matmul(bank[4 + f % 2][:, m * P:(m + 1) * P], (KWF, KWB)[d][:, n * P:(n + 1) * P],
                                       VT[:, n * P:(n + 1) * P], start=True, stop=True)
                    mm.then_inc(s_u.sem, 1)
                    fill()

                def scores(g):
                    if g == 0:
                        pt.wait_ge(*s_rope.at(n_rope))
                    else:
                        pt.wait_ge(*s_sc.at(2 * g))
                    for e in range(2):
                        for m, n in enumerate(groups[g]):
                            r = slice(64 * e, 64 * e + 64)
                            mm = pt.matmul(bank[2 + e][:, m * P:(m + 1) * P], Kb[r, n * P:(n + 1) * P], Qb[r, n * P:(n + 1) * P],
                                           start=True, stop=True)
                        mm.then_inc(s_s.sem, 1)

                def outs(g):
                    if g == 0:
                        pt.wait_ge(*s_S.at(1))
                        pt.wait_ge(*s_qf.at(1))
                    if g >= 2:
                        pt.wait_ge(*s_os.at(g - 1))
                    pt.wait_ge(*s_sc.at(2 * g + 2))
                    for m, n in enumerate(groups[g]):
                        o = bank[4 + g % 2][:, m * P:(m + 1) * P]
                        c = slice(n * P, (n + 1) * P)
                        pt.matmul(o, SF[:, c], QF[:, c], start=True, stop=False)
                        pt.matmul(o, SB[:, c], QBK[:, c], start=False, stop=False)
                        for e in range(2):
                            mm = pt.matmul(o[64 * e:64 * e + 64, :], VT[:, n * P + 64 * e:n * P + 64 * e + 64],
                                           SC[:, (m * 2 + e) * P:(m * 2 + e + 1) * P], start=False, stop=True)
                    mm.then_inc(s_o.sem, 1)

                def center(g):
                    w = len(groups[g]) * P
                    pt.wait_ge(*s_os.at(g + 1))
                    if g >= 1:
                        pt.wait_ge(*s_sq.at(g))
                    pt.matmul(bank[6][:, 0:w], k1("center"), UMo[:, 0:w], start=True, stop=True).then_inc(s_cen.sem, 1)

                def var(g):
                    w = len(groups[g]) * P
                    pt.wait_ge(*s_sq.at(g + 1))
                    if g >= 1:
                        pt.wait_ge(*s_rs.at(g))
                    pt.matmul(bank[7][:, 0:w], k1("headmean"), TMP[:, 0:w], start=True, stop=True).then_inc(s_var.sem, 1)

                for g in range(NG):
                    scores(g)
                    if g >= 1:
                        center(g - 1)
                    fill()
                    outs(g)
                    if g >= 1:
                        var(g - 1)
                    fill()
                center(NG - 1)
                fill()
                var(NG - 1)

            UMo = UM

            def act(a, fill):
                for _ in items:
                    fill()
                for f, ns in enumerate(fills):
                    a.wait_ge(*s_tp.at(f + 1))
                    w = len(ns) * P
                    a.activation(VT[:, ns[0] * P:ns[0] * P + w], bank[4 + f % 2][:, 0:w], ACT.Copy).then_inc(s_vt.sem, 1)
                    fill()
                for _ in range(3 + len(ufills)):
                    fill()
                for g in range(NG):
                    w = len(groups[g]) * P
                    a.wait_ge(*s_o.at(g + 1))
                    if g == 0:
                        a.wait_ge(*s_S.at(1))
                    else:
                        a.wait_ge(*s_yr.at(g))
                    fill()
                    a.activation(UMo[:, 0:w], bank[4 + g % 2][:, 0:w], ACT.Copy).then_inc(s_os.sem, 1)
                    fill()
                    a.wait_ge(*s_cen.at(g + 1))
                    a.activation(UMo[:, 0:w], bank[6][:, 0:w], ACT.Copy).then_inc(s_ac.sem, 1)
                    if g == 0:
                        a.wait_ge(*s_rope.at(n_rope))
                    a.activation(TMP[:, 0:w], bank[6][:, 0:w], ACT.Square).then_inc(s_sq.sem, 1)
                    a.wait_ge(*s_var.at(g + 1))
                    a.activation(TMP[:, 0:w], bank[7][:, 0:w], ACT.Ln, bias=k1("eps")).then_inc(s_ac.sem, 1)
                    a.wait_ge(*s_ac.at(2 * g + 2))
                    a.activation(TMP[:, 0:w], TMP[:, 0:w], ACT.Exp, scale=-0.5).then_inc(s_rs.sem, 1)
                fill()

            def dve(v, fill):
                ch = dve_chain(v)
                v.wait_ge(*s_cs.at(32 * (l + 1)))
                if u == 0:
                    v.wait_ge(*s_pad.at(16))
                    v.wait_ge(*s_bias.at(16))
                for i, (x, bi, ci, (t0, n)) in enumerate(items):
                    v.wait_ge(*s_rot.at(i + 1))
                    ch(v.tensor_tensor(TMP[:, 0:n], bank[2 + i % 2][:, 0:n], SIN[:, t0:t0 + n], ALU.mult))
                    ch(v.tensor_tensor(x[:, t0:t0 + n], x[:, t0:t0 + n], COS[:, t0:t0 + n], ALU.mult))
                    v.tensor_tensor(x[:, t0:t0 + n], x[:, t0:t0 + n], TMP[:, 0:n], ALU.add).then_inc(s_rope.sem, 1)
                    v.wait_ge(*s_rope.at(i + 1))
                    fill()
                v.wait_ge(*s_dt[l].at(NDT))
                for _ in fills:
                    fill()
                for f, ns in enumerate(fills):
                    v.wait_ge(*s_tp.at(3 + f + 1))
                    k = len(ns)
                    src = bank[6 + f % 2][:, 0:k * P].rearrange("q (n c) -> q n c", c=P)
                    for d, kw in enumerate((KWF, KWB)):
                        dst = kw[:, ns[0] * P:(ns[0] + k) * P].rearrange("q (n c) -> q n c", c=P)
                        for e in range(2):
                            h = 2 * p + e
                            ins = v.tensor_scalar(dst[:, :, 64 * e:64 * e + 64], src[:, :, 64 * e:64 * e + 64], WK[:, d, h:h + 1], None, ALU.mult)
                            if d == 1 and e == 1:
                                ins.then_inc(s_kw.sem, 1)
                            else:
                                ch(ins)
                    fill()
                v.wait_ge(*s_kw.at(3))
                m = T // P
                v.wait_ge(*s_vt.at(3))
                nq = (T - lo) // P
                wide = lambda x: x[:, lo:T].rearrange("q (n c) -> q n c", c=P)
                ch(v.tensor_tensor(wide(QF), wide(Qb), WQ[:, 0, p, :].unsqueeze(1).to_broadcast([P, nq, P]), ALU.mult))
                v.tensor_tensor(wide(QBK), wide(Qb), WQ[:, 1, p, :].unsqueeze(1).to_broadcast([P, nq, P]), ALU.mult).then_inc(s_qf.sem, 1)
                ch(v.memset(SF[:, 0:P], 0.0))
                mask = k1("pairmask").unsqueeze(1)
                for f, (d, ns) in enumerate(ufills):
                    v.wait_ge(*s_u.at(f + 1))
                    k = len(ns)
                    v.tensor_tensor(UM[:, 0:k * P].rearrange("q (n c) -> q n c", c=P),
                                    bank[4 + f % 2][:, 0:k * P].rearrange("q (n c) -> q n c", c=P),
                                    mask.to_broadcast([P, k, P]), ALU.mult).then_inc(s_um.sem, 1)
                    v.wait_ge(*s_um.at(f + 1))
                    S = (SF, SB)[d]
                    if f == 3:
                        ch(v.memset(SB[:, P:2 * P], 0.0))
                    for i, n in enumerate(ns):
                        nxt = n + 1 if d == 0 else (n - 1 if n != 0 else 9)
                        ins = v.scalar_tensor_tensor(S[:, nxt * P:(nxt + 1) * P], S[:, n * P:(n + 1) * P], G128[:, 3 * d + p:3 * d + p + 1],
                                                     UM[:, i * P:(i + 1) * P], ALU.mult, ALU.add)
                        if f == 5 and i == k - 1:
                            ins.then_inc(s_S.sem, 1)
                            v.wait_ge(*s_S.at(1))
                        else:
                            ch(ins)
                    fill()

                def decay(g):
                    k = len(groups[g])
                    for e in range(2):
                        v.wait_ge(*s_s.at(2 * g + e + 1))
                        if g >= 1:
                            v.wait_ge(*s_o.at(g))
                        v.tensor_tensor(SC[:, 0:k * 2 * P].rearrange("q (n f c) -> q n f c", f=2, c=P)[:, :, e, :],
                                        bank[2 + e][:, 0:k * P].rearrange("q (n c) -> q n c", c=P),
                                        DT[:, 2 * p + e, :].unsqueeze(1).to_broadcast([P, k, P]), ALU.mult).then_inc(s_sc.sem, 1)

                def gate(g):
                    w = len(groups[g]) * P
                    t0 = groups[g][0] * P
                    v.wait_ge(*s_rs.at(g + 1))
                    v.wait_ge(*s_ac.at(2 * g + 2))
                    v.wait_ge(*got[3][-1])
                    v.tensor_tensor(Gb[:, t0:t0 + w], Gb[:, t0:t0 + w], UMo[:, 0:w], ALU.mult).then_inc(s_yg.sem, 1)
                    v.wait_ge(*s_yg.at(g + 1))
                    ins = v.tensor_tensor(Gb[:, t0:t0 + w], Gb[:, t0:t0 + w], TMP[:, 0:w], ALU.mult)
                    ins.then_inc(s_yr.sem, 1)
                    v.wait_ge(*s_yr.at(g + 1))

                decay(0)
                for g in range(NG):
                    fill()
                    if g + 1 < NG:
                        decay(g + 1)
                    gate(g)
                    fill()
                v.engine_nop().then_inc(s_unit.sem, 1)
                v.wait_ge(*s_unit.at(u + 1))
                fill()

            unit = dict(u=u, blks=allb, points=n_rope + 6 + len(ufills) + 2 * NG + 1, tail=5, act_first=act_first(l, u), result=Gb, pe=pe, act=act, dve=dve)
            store(unit, 2 + p, lo)
            return unit

        def rpb_phase():
            st = SC[0:LAYERS * 45, 0:254].rearrange("q (a y) -> q a y", a=2)
            s_z, s_l = sem("padz"), sem("padl")

            def pool(g):
                g.memset(st[:, :, :], 0.0).then_inc(s_z.sem, 1)
                g.wait_ge(*s_z.at(1))
                g.dma_start(st[:, :, 48:48 + RPB_W], I["rpb"]).then_inc(s_l.sem, 16)
                g.wait_ge(*s_l.at(16))
                g.dma_start(scratch["rpb"].ap().rearrange("(r a) y -> r a y", a=2), st[:, :, :]).then_inc(s_pad.sem, 16)
                g.wait_ge(*s_pad.at(16))
                load_rows(g, 0)

            return dict(pool=pool)

        def load_rows(g, i):
            for e in range(2):
                g.dma_start(NF[64 * e:64 * e + 64, :].rearrange("q (d c) -> q d c", c=GRID_W),
                            bass.AP(tensor=scratch["rpb"], offset=(2 * i + e) * RPB_H * 127, ap=[[1, 64], [127, RPB_H], [1, GRID_W]])).then_inc(s_nf.sem, 16)

        s_nf = sem("nf")

        def na_unit(l, p):
            u = n_units[0]
            n_units[0] += 1
            qch = CHUNKS if l == 0 else MAIN
            Kb, Vb, Qb, Gb = PXS[u % 2]
            allb, got = projections(l, [6 + p, 9 + p, 18 + p, 21 + p], [CHUNKS, CHUNKS, qch, qch],
                               [plain(Kb), plain(Vb), plain(Qb, scale=HD ** -0.5), gate_into(Gb, l, u)])
            lo = qch[0][0]
            rows = ([("ctx", r) for r in range(4)] if l == 0 else []) + [("grid", r) for r in range(GRID_H)]
            R = len(rows)
            fills = [("t", range(0, 4)), ("t", range(4, 8)), ("t", range(8, 10)), ("s", range(0, 4)), ("s", range(4, 7))]
            s_f, s_fl, s_nt, s_tp, s_vt = (sem(x, n) for x, n in (("nf", 32), ("nfl", 2), ("nt", 2), ("ntp", 5), ("nvt", 5)))
            s_s, s_m, s_e, s_pn, s_ta, s_tb, s_pa, s_pb, s_o, s_y = (
                sem(x, GRID_H if x == "nta" else R) for x in "ns nm ne npn nta ntb npa npb no ny".split())
            s_qa, s_qd = sem("nqa", 1), sem("nqd", 1)

            def q0(row):
                return (row[1] * GRID_W) + (CTX if row[0] == "grid" else 0)

            def band(row):
                r = row[1]
                rs = min(max(r - WIN_H // 2, 0), GRID_H - WIN_H)
                return rs, rs - r + WIN_H - 1

            def pool(g):
                if p == 0:
                    g.wait_ge(*s_unit.at(u))
                    g.memset(QB, 0.0).then_inc(s_qz.sem, 1)
                if (l, p) != (LAYERS - 1, PAIRS - 1):
                    g.wait_ge(*s_fl.at(2))
                    load_rows(g, PAIRS * l + p + 1)

            def pe(pt, fill):
                pt.wait_ge(*s_unit.at(u))
                pt.wait_ge(*s_f.at(32))
                for c, (a_, n) in enumerate(((0, 512), (512, 448))):
                    pt.matmul(bank[2 + c][:, 0:n], k1("flip64"), NF[:, a_:a_ + n], start=True, stop=True).then_inc(s_fl.sem, 1)
                pt.wait_ge(*got[1][-1])
                for f, (kind, ns) in enumerate(fills):
                    if f >= 2:
                        pt.wait_ge(*s_vt.at(f - 1))
                    for m, n in enumerate(ns):
                        t0 = n * P if kind == "t" else CTX + 64 + n * P
                        mm = pt.transpose(bank[5 + f % 2][:, m * P:(m + 1) * P], Vb[:, t0:t0 + P], k1("ident"))
                    mm.then_inc(s_tp.sem, 1)
                    fill()
                pt.wait_ge(*s_nt.at(2))
                pt.wait_ge(*s_vt.at(5))
                pt.wait_ge(*s_qa.at(1))
                pt.wait_ge(*s_qd.at(1))

                def scores(i):
                    qb = QB[:, rows_at(i) * P:(rows_at(i) + 1) * P]
                    if rows[i][0] == "grid":
                        if i >= 2:
                            pt.wait_ge(*s_m.at(i - 1))
                        rs, _ = band(rows[i])
                        pt.matmul(bank[2 + i % 2][:, :], qb, Kb[:, CTX + rs * GRID_W:CTX + rs * GRID_W + 512], start=True, stop=True)
                    if i >= 1:
                        pt.wait_ge(*s_e.at(i))
                    pt.matmul(bank[4][:, 0:CTX], qb, Kb[:, 0:CTX], start=True, stop=True).then_inc(s_s.sem, 1)

                def turn(i):
                    pt.wait_ge(*s_pn.at(i + 1))
                    pr = PR[i % 2]
                    if i >= 1:
                        pt.wait_ge(*s_pa.at(i))
                        pt.wait_ge(*s_pb.at(i))
                    if rows[i][0] == "grid":
                        for m in range(4):
                            mm = pt.transpose(bank[5][:, m * P:(m + 1) * P], pr[:, m * P:(m + 1) * P], k1("ident"))
                        mm.then_inc(s_ta.sem, 1)
                    for m in range(2):
                        mm = pt.transpose(bank[6][:, m * P:(m + 1) * P], pr[:, (4 + m) * P:(5 + m) * P], k1("ident"))
                    mm.then_inc(s_tb.sem, 1)

                def values(i):
                    pt.wait_ge(*s_pa.at(i + 1))
                    pt.wait_ge(*s_pb.at(i + 1))
                    if i >= 1:
                        pt.wait_ge(*s_y.at(i))
                    rs, _ = band(rows[i])
                    parts = []
                    if rows[i][0] == "grid":
                        for m in range(4):
                            parts.append((m, VT[:, (2 + rs // 2 + m) * P:(3 + rs // 2 + m) * P] if rs % 2 == 0 else
                                          VS[:, (rs // 2 + m) * P:(rs // 2 + m + 1) * P]))
                    parts += [(4 + m, VT[:, m * P:(m + 1) * P]) for m in range(2)]
                    for j, (m, vv) in enumerate(parts):
                        for e in range(2):
                            mm = pt.matmul(bank[7][64 * e:64 * e + 64, 0:64], vv[:, 64 * e:64 * e + 64],
                                           PT[:, m * P + 64 * e:m * P + 64 * e + 64], start=j == 0, stop=j == len(parts) - 1)
                    mm.then_inc(s_o.sem, 1)

                scores(0)
                for i in range(R):
                    if i + 1 < R:
                        scores(i + 1)
                    turn(i)
                    fill()
                    values(i)

            def rows_at(i):
                return q0(rows[i]) // GRID_W

            def spread(eng_copy, e):
                q = QB[64 * e:64 * e + 64, (lo // GRID_W) * P:].rearrange("q (r c) -> q r c", c=P)[:, :, 64 * e:64 * e + 64]
                return eng_copy(q, Qb[64 * e:64 * e + 64, lo:].rearrange("q (r c) -> q r c", c=GRID_W))

            def act(a, fill):
                a.wait_ge(*s_unit.at(u))
                a.wait_ge(*s_qz.at(l + 1))
                a.wait_ge(*got[2][-1])
                spread(lambda o, x: a.activation(o, x, ACT.Copy), 0).then_inc(s_qa.sem, 1)
                for f, (kind, ns) in enumerate(fills):
                    a.wait_ge(*s_tp.at(f + 1))
                    dst = VT if kind == "t" else VS
                    a.activation(dst[:, ns[0] * P:(ns[-1] + 1) * P], bank[5 + f % 2][:, 0:len(ns) * P], ACT.Copy).then_inc(s_vt.sem, 1)
                    fill()

                def exps(i):
                    a.wait_ge(*s_m.at(i + 1))
                    if i >= 2:
                        a.wait_ge(*s_tb.at(i - 1))
                    sm = small[:, 8 * (i % 2):8 * (i % 2) + 8]
                    if rows[i][0] == "grid":
                        a.activation(PR[i % 2][:, 0:512], LL[:, (i % 2) * 512:(i % 2) * 512 + 512], ACT.Exp, bias=sm[:, 2:3],
                                     accum_out=sm[:, 3:4])
                    a.activation(PR[i % 2][:, 512:768], bank[4][:, 0:CTX], ACT.Exp, bias=sm[:, 2:3], accum_out=sm[:, 4:5]).then_inc(s_e.sem, 1)

                def evac_pt(i):
                    if i >= 1:
                        a.wait_ge(*s_o.at(i))
                    if rows[i][0] == "grid":
                        a.wait_ge(*s_ta.at(i + 1 - R + GRID_H))
                        a.activation(PT[:, 0:512], bank[5][:, :], ACT.Copy).then_inc(s_pa.sem, 1)
                    else:
                        a.sem_inc(s_pa.sem, 1)

                exps(0)
                for i in range(R):
                    if i + 1 < R:
                        exps(i + 1)
                    evac_pt(i)
                    fill()

            def dve(v, fill):
                ch = dve_chain(v)
                v.wait_ge(*s_qz.at(l + 1))
                v.wait_ge(*got[2][-1])
                spread(v.tensor_copy, 1).then_inc(s_qd.sem, 1)
                for c, (a_, n) in enumerate(((0, 8), (8, 7))):
                    v.wait_ge(*s_fl.at(c + 1))
                    v.tensor_tensor(NT[:, a_ * 64:(a_ + n) * 64].rearrange("q (d c) -> q d c", c=GRID_W),
                                    bank[2 + c][:, 0:n * 64].rearrange("q (d c) -> q d c", c=GRID_W),
                                    k1("wincol").unsqueeze(1).to_broadcast([P, n, GRID_W]), ALU.add).then_inc(s_nt.sem, 1)
                v.wait_ge(*s_nt.at(2))
                for _ in fills:
                    fill()
                v.wait_ge(*s_vt.at(5))

                def maxes(i):
                    v.wait_ge(*s_s.at(i + 1))
                    if i >= 2:
                        v.wait_ge(*s_e.at(i - 1))
                    sm = small[:, 8 * (i % 2):8 * (i % 2) + 8]
                    ch(v.tensor_reduce(sm[:, 1:2], bank[4][:, 0:CTX], AX_X, ALU.max))
                    if rows[i][0] == "grid":
                        _, dr = band(rows[i])
                        ch(v.tensor_tensor_reduce(out=LL[:, (i % 2) * 512:(i % 2) * 512 + 512], in0=bank[2 + i % 2][:, :],
                                                  in1=NT[:, dr * GRID_W:dr * GRID_W + 512], scale=1.0, scalar=-3.0e38,
                                                  op0=ALU.add, op1=ALU.max, accum_out=sm[:, 0:1]))
                        v.tensor_scalar(sm[:, 2:3], sm[:, 0:1], sm[:, 1:2], -1.0, ALU.max, ALU.mult).then_inc(s_m.sem, 1)
                    else:
                        v.tensor_scalar(sm[:, 2:3], sm[:, 1:2], -1.0, None, ALU.mult).then_inc(s_m.sem, 1)

                def norm(i):
                    v.wait_ge(*s_e.at(i + 1))
                    sm = small[:, 8 * (i % 2):8 * (i % 2) + 8]
                    if rows[i][0] == "grid":
                        ch(v.tensor_tensor(sm[:, 5:6], sm[:, 3:4], sm[:, 4:5], ALU.add))
                        ch(v.reciprocal(sm[:, 6:7], sm[:, 5:6]))
                        lo = 0
                    else:
                        ch(v.reciprocal(sm[:, 6:7], sm[:, 4:5]))
                        lo = 512
                    v.tensor_scalar(PR[i % 2][:, lo:768], PR[i % 2][:, lo:768], sm[:, 6:7], None, ALU.mult).then_inc(s_pn.sem, 1)

                def result(i):
                    v.wait_ge(*s_o.at(i + 1))
                    t0 = q0(rows[i])
                    if i == 0:
                        v.wait_ge(*got[3][-1])
                    v.tensor_tensor(Gb[:, t0:t0 + GRID_W], bank[7][:, 0:64], Gb[:, t0:t0 + GRID_W], ALU.mult).then_inc(s_y.sem, 1)

                maxes(0)
                for i in range(R):
                    norm(i)
                    if i >= 1:
                        result(i - 1)
                    if i + 1 < R:
                        maxes(i + 1)
                    v.wait_ge(*s_tb.at(i + 1))
                    if i >= 1:
                        v.wait_ge(*s_o.at(i))
                    v.tensor_copy(PT[:, 512:768], bank[6][:, 0:256]).then_inc(s_pb.sem, 1)
                    fill()
                result(R - 1)
                v.wait_ge(*s_y.at(R))
                v.engine_nop().then_inc(s_unit.sem, 1)
                v.wait_ge(*s_unit.at(u + 1))

            unit = dict(u=u, blks=allb, points=len(fills) + R, act_first=act_first(l, u), result=Gb, pe=pe, act=act, dve=dve, pool=pool)
            store(unit, 5 + p, lo)
            return unit

        def bias_phase():
            s_bl, s_bm, s_bc = sem("bl"), sem("bm"), sem("bc")
            bk_, bt_, rb_ = KWF[0:33, 0:TB], KWB[0:8, 0:TB], VTR[0:33, 0:8]

            def pool(g):
                g.dma_start(bk_, I["buckets"]).then_inc(s_bl.sem, 16)
                g.dma_start(rb_, I["relb"]).then_inc(s_bl.sem, 16)
                g.wait_ge(*s_bc.at(3))
                g.dma_start(scratch["bias"].ap(), bt_).then_inc(s_bias.sem, 16)
                g.wait_ge(*s_bias.at(16))

            def pe(p):
                p.wait_ge(*s_bl.at(32))
                for i in range(3):
                    p.matmul(bank[2 + i][0:8, 0:384], rb_, bk_[:, 384 * i:384 * i + 384], start=True, stop=True).then_inc(s_bm.sem, 1)

            def act(a):
                for i in range(3):
                    a.wait_ge(*s_bm.at(i + 1))
                    a.activation(bt_[:, 384 * i:384 * i + 384], bank[2 + i][0:8, 0:384], ACT.Copy).then_inc(s_bc.sem, 1)

            return dict(pool=pool, pe=pe, act=act)

        def out_phases(l):
            chunks = CHUNKS if l == 0 else MAIN
            lo = chunks[0][0]
            u = n_units[0]
            NCK, NA = len(chunks), len(chunks) - 1
            LAST = NCK - 1
            korder = [2, 3, 4, 5, 6, 7, 0, 1]
            part_a = [block(I["wout"][l, m], KT, chunks[:NA], rhs_hh, korder=korder) for m in range(KT)]
            part_b = [block(I["wout"][l, m], KT, chunks[NA:], rhs_hh, korder=korder) for m in range(KT)]
            s_xs = [sem(f"xs{i}", 16 * KT) for i in range(2)]
            s_hi, s_lo, s_res, s_a = (sem(x, n) for x, n in (("yhi", KT), ("ylo", KT), ("res", KT * NCK), ("lna", NCK)))
            s_mu, s_cen, s_sq, s_var, s_rs, s_n, s_fin = (
                sem(x, n * NCK) for x, n in (("mu", 1), ("cen", KT), ("sq", KT), ("var", KT), ("rstd", 1), ("nrm", KT), ("fin", KT)))
            results = [PXS[k][3] if k < 2 else ST[k - 2] for k in range(KT)]
            XS = ST[0:2]
            dst = scratch["x1"] if l == 0 else scratch["x2"]
            xst0 = 48 * l
            h0 = 16
            rms = None
            if l + 1 == LAYERS:
                rms = NormIn(0, M2, lambda part, m, t0, n: H2[:, part, m, t0:t0 + n], [ST[6][:, 0:512], ST[6][:, 512:1024]],
                             [HT[:, 0:512], HT[:, 512:1024]], [CT[:, 0:512], CT[:, 512:1024]], lambda: k1("mean"), lambda: k1("eps2"), 6)

            def seg(c):
                return chunks[c][0], chunks[c][0] + chunks[c][1]

            def pe_mean(pt, c):
                a_, b_ = seg(c)
                pt.wait_ge(*s_res.at(KT * (NA if c < NA else NCK)))
                for m in range(KT):
                    mm = pt.matmul(bank[2 + 2 * c][:, 0:b_ - a_], k1("mean"), Y[:, m, a_:b_], start=m == 0, stop=m == KT - 1)
                mm.then_inc(s_mu.sem, 1)

            def dve_center(v, c):
                a_, b_ = seg(c)
                v.wait_ge(*s_mu.at(c + 1))
                for m in range(KT):
                    v.tensor_tensor(Y[:, m, a_:b_], Y[:, m, a_:b_], bank[2 + 2 * c][:, 0:b_ - a_], ALU.subtract).then_inc(s_cen.sem, 1)

            def act_squares(a, c):
                a_, b_ = seg(c)
                for m in range(KT):
                    i = c * KT + m
                    a.wait_ge(*s_cen.at(i + 1))
                    if i >= 2:
                        a.wait_ge(*s_var.at(i - 1))
                    a.activation(SQ[m % 2][:, 0:b_ - a_], Y[:, m, a_:b_], ACT.Square).then_inc(s_sq.sem, 1)

            def pe_var(pt, c):
                a_, b_ = seg(c)
                for m in range(KT):
                    pt.wait_ge(*s_sq.at(c * KT + m + 1))
                    pt.matmul(bank[3 + 2 * c][:, 0:b_ - a_], k1("mean"), SQ[m % 2][:, 0:b_ - a_], start=m == 0, stop=m == KT - 1).then_inc(s_var.sem, 1)

            def act_rstd(a, c):
                n = chunks[c][1]
                a.wait_ge(*s_var.at((c + 1) * KT))
                if c >= 2:
                    a.wait_ge(*s_n.at((c - 1) * KT))
                a.activation(RS[c % 2][:, 0:n], bank[3 + 2 * c][:, 0:n], ACT.Ln, bias=k1("eps")).then_inc(s_a.sem, 1)
                a.wait_ge(*s_a.at(c + 1))
                a.activation(RS[c % 2][:, 0:n], RS[c % 2][:, 0:n], ACT.Exp, scale=-0.5).then_inc(s_rs.sem, 1)

            def dve_scale(v, c):
                a_, b_ = seg(c)
                v.wait_ge(*s_cen.at((c + 1) * KT))
                v.wait_ge(*s_rs.at(c + 1))
                for m in range(KT):
                    v.tensor_tensor(Y[:, m, a_:b_], Y[:, m, a_:b_], RS[c % 2][:, 0:b_ - a_], ALU.mult).then_inc(s_n.sem, 1)

            def act_affine(a, c):
                a_, b_ = seg(c)
                for m in range(KT):
                    a.wait_ge(*s_n.at(c * KT + m + 1))
                    a.activation(Y[:, m, a_:b_], Y[:, m, a_:b_], ACT.Identity, scale=lnp[:, l, 0, m:m + 1],
                                 bias=lnp[:, l, 1, m:m + 1]).then_inc(s_fin.sem, 1)

            def act_input(a, c):
                if l + 1 == LAYERS:
                    return
                a_, b_ = seg(c)
                w = 1 if c == 0 else 0
                if c == 0:
                    a.wait_ge(*mod_ready(l + 1, 15))
                    a.wait_ge(*s_gemm.at(part_a[-1]["piece"] + NA))
                if c == LAST:
                    a.wait_ge(*s_gemm.at(part_b[-1]["piece"] + 1))
                for k in range(KT):
                    a.wait_ge(*s_fin.at(c * KT + k + 1))
                    a.activation(HH[:, 0, k, a_:b_], Y[:, k, a_:b_], ACT.Identity, scale=modv[:, l + 1, 8 + k, w:w + 1],
                                 bias=modv[:, l + 1, k, w:w + 1]).then_inc(s_hhi.sem, 1)

            def dve_input(v, c):
                if l + 1 == LAYERS:
                    return
                a_, b_ = seg(c)
                w = 1 if c == 0 else 0
                ch = dve_chain(v)
                for k in range(KT):
                    i = c * KT + k + 1
                    tt = HT[:, 0:b_ - a_]
                    v.wait_ge(*s_fin.at(i))
                    ch(v.tensor_scalar(tt, Y[:, k, a_:b_], modv[:, l + 1, 8 + k, w:w + 1], modv[:, l + 1, k, w:w + 1], ALU.mult, ALU.add))
                    v.wait_ge(*s_hhi.at(h0 + i))
                    v.tensor_tensor(HH[:, 1, k, a_:b_], tt, HH[:, 0, k, a_:b_].bitcast(F32), ALU.subtract).then_inc(s_h.sem, 1)
                    v.wait_ge(*s_h.at(h0 + i))

            def store_chunk(g, c):
                a_, b_ = seg(c)
                g.wait_ge(*s_fin.at((c + 1) * KT))
                g.dma_start(dst.ap()[:, :, a_:b_], Y[:, :, a_:b_]).then_inc(s_xst.sem, 16)
                g.wait_ge(*s_xst.at(xst0 + 16 * (c + 1)))

            def pool(g):
                src = I["xt"] if l == 0 else scratch["x1"].ap()
                g.wait_ge(*s_lo.at(KT))
                for i in range(2 * KT):
                    part, m = divmod(i, KT)
                    if i >= 2:
                        pt_, pm = divmod(i - 2, KT)
                        g.wait_ge(*s_res.at(NA * (pm + 1) if pt_ == 0 else NA * KT + pm + 1))
                    a_, b_ = (lo, chunks[NA][0]) if part == 0 else seg(LAST)
                    g.dma_start(XS[i % 2][:, a_:b_], src[:, m, a_:b_]).then_inc(s_xs[i % 2].sem, 16)
                for c in range(NA):
                    store_chunk(g, c)

            def pe(pt):
                for m, blk in enumerate(part_a):
                    whole(pe_block(pt, blk, (lambda i: pt.wait_ge(*s_lo.at(i + 1))) if m == 0 else None))
                for m, blk in enumerate(part_b):
                    whole(pe_block(pt, blk))
                    for c in range(NA):
                        if m == 1 + c:
                            pe_mean(pt, c)
                        if m == 3 + c:
                            pe_var(pt, c)
                if rms is not None:
                    rms.pe_var(pt, 0)

            def act(a):
                a.wait_ge(*s_stg.at(16 * (l + 1)))
                a.wait_ge(*s_gemm.at(part_a[0]["piece"]))
                for k in korder:
                    if k < 2:
                        a.wait_ge(*s_unit.at(u - 1 + k))
                    a.activation(HH[:, 0, k, lo:], results[k][:, lo:], ACT.Copy).then_inc(s_hi.sem, 1)
                a.wait_ge(*mod_ready(l, 23))
                a.wait_ge(*s_lo.at(KT))

                def gated(m):
                    def evac(a, ci, t0, n, ps):
                        w = 1 if t0 < CTX else 0
                        return a.activation(Y[:, m, t0:t0 + n], ps, ACT.Copy, scale=modv[:, l, 16 + m, w:w + 1])
                    return evac

                for m, blk in enumerate(part_a):
                    whole(act_block(a, blk, gated(m)))
                for m, blk in enumerate(part_b):
                    whole(act_block(a, blk, gated(m)))
                    for c in range(NA):
                        if m == 2 + c:
                            act_squares(a, c)
                        if m == 4 + c:
                            act_rstd(a, c)
                            act_affine(a, c)
                        if m == 6 + c:
                            act_input(a, c)
                if rms is not None:
                    rms.act_squares(a, 0)

            def dve(v):
                for i, k in enumerate(korder):
                    v.wait_ge(*s_hi.at(i + 1))
                    v.tensor_tensor(HH[:, 1, k, lo:], results[k][:, lo:], HH[:, 0, k, lo:].bitcast(F32), ALU.subtract).then_inc(s_lo.sem, 1)
                for i, blk in enumerate(part_a + part_b):
                    part, m = divmod(i, KT)
                    whole(dve_block(v, blk))
                    v.wait_ge(*s_xs[i % 2].at(16 * (i // 2 + 1)))
                    for ci, (t0, n) in enumerate(blk["chunks"]):
                        v.wait_ge(*s_evac.at(out_done(blk, ci)))
                        v.scalar_tensor_tensor(Y[:, m, t0:t0 + n], XS[i % 2][:, t0:t0 + n], ALPHA, Y[:, m, t0:t0 + n],
                                               ALU.mult, ALU.add).then_inc(s_res.sem, 1)
                    for c in range(NA if part else 0):
                        if m == 1 + c:
                            v.wait_ge(*s_res.at(KT * NA))
                            dve_center(v, c)
                        if m == 4 + c:
                            dve_scale(v, c)
                        if m == 6 + c:
                            dve_input(v, c)

            def tail_pool(g):
                store_chunk(g, LAST)
                if l + 1 < LAYERS:
                    load_angles(g)

            def tail_pe(pt, fill):
                pe_mean(pt, LAST)
                fill()
                fill()
                pe_var(pt, LAST)
                for _ in range(4):
                    fill()
                if rms is not None:
                    rms.pe_var(pt, 1)

            def tail_act(a, fill):
                if rms is not None:
                    rms.act_rstd(a, 0)
                fill()
                fill()
                act_squares(a, LAST)
                fill()
                act_rstd(a, LAST)
                fill()
                if rms is not None:
                    a.wait_ge(*s_gemm.at(part_b[-1]["piece"] + 1))
                    rms.act_hi(a, 0)
                act_affine(a, LAST)
                fill()
                act_input(a, LAST)
                fill()
                if rms is not None:
                    rms.act_squares(a, 1, lambda m: s_fin.at(LAST * KT + m + 1))
                    rms.act_rstd(a, 1)
                    rms.act_hi(a, 1)

            def tail_dve(v, fill):
                fill()
                v.wait_ge(*s_res.at(KT * NCK))
                dve_center(v, LAST)
                fill()
                fill()
                if rms is not None:
                    rms.dve_scale(v, 0)
                dve_scale(v, LAST)
                fill()
                dve_input(v, LAST)
                fill()
                fill()
                if rms is not None:
                    rms.dve_scale(v, 1)

            tail = dict(u=0, blks=[], points=6, limit=6, act_first=lambda a: None, pool=tail_pool, pe=tail_pe, act=tail_act, dve=tail_dve)
            return dict(pe=pe, act=act, dve=dve, pool=pool), tail, s_gemm.at(part_b[-1]["piece"] + 1), rms

        phases += [first_phase(), table_phase(0), rpb_phase(), bias_phase(), start_phase()]
        lead = []
        for l in range(LAYERS):
            units = [ret_unit(l, p) for p in range(PAIRS)] + [na_unit(l, p) for p in range(PAIRS)] + [conv_unit(l, c) for c in range(2)]
            phases.append(run_units(lead + units))
            if l + 1 < LAYERS:
                phases.append(table_phase(l + 1))
            ph, tail, products, r1 = out_phases(l)
            phases.append(ph)
            lead = [tail]
        phases.append(run_units(lead))

        if True:
            b1.close()
            b2 = top.enter_context(ExitStack())
            H2 = sb("H2", [P, 2, KT, SEQ], F32R, b2)
            c2 = sb("c2", [P, N2], F32, b2)
            cw2 = sb("cw2", [P, 12, 4], F32, b2)
            gsm = sb("gsm", [P, 16, 32], F32, b2)
            hrow = sb("hrow", [P, 9], F32, b2)
            ar2 = sb("ar2", [P, 16 * 1024], F32, b2)
            rhs_h2 = lambda part, k, t0, n: H2[:, part, k, t0:t0 + n]

            def k2(name):
                a, n = C2[name]
                return c2[:, a:a + n]

            s_c2 = sem("const2")

            def consts2_phase():
                def pool(g):
                    g.wait_ge(*products)
                    g.dma_start(c2[:, :], I["c2"]).then_inc(s_c2.sem, 16)
                    g.dma_start(cw2[:, :, :], I["cw2"]).then_inc(s_c2.sem, 16)
                    for i, nm in enumerate(("dtb_t", "alog_t")):
                        g.dma_start(hrow[:, 4 * i:4 * i + 4], bass.AP(tensor=I[nm], offset=0, ap=[[0, P], [1, 4]])).then_inc(s_c2.sem, 16)
                    g.dma_start(hrow[:, 8:9], I["onorm"]).then_inc(s_c2.sem, 16)
                return dict(pool=pool)

            NC = 5 * 16

            phases.append(consts2_phase())

            def wait_consts(e):
                e.wait_ge(*s_c2.at(NC))

            phases.append(dict(pe=wait_consts, act=wait_consts, dve=wait_consts))
            A2 = lambda i, n=1: ar2[:, i * 1024:(i + n) * 1024]
            half2 = lambda t: [t[:, 0:512], t[:, 512:1024]]
            s_ba, s_bam, s_baa, s_bad = sem("ba"), sem("bam"), sem("baa"), sem("bad")
            v3 = lambda i: gsm[:, i, :].rearrange("q (n h) -> q n h", h=GH)
            LBA = gsm[:, 0:2, :].rearrange("q a c -> q (a c)").rearrange("q (n c) -> q n c", c=8)
            BETA, Z, EZ, SP, TT, GG, GC, EGC, BE = (v3(i) for i in range(2, 11))
            EA = gsm[:, 11, 0:4]

            def ba_unit():
                u = n_units[0]
                n_units[0] += 1
                LT = Y[0:8, 0:4, 0:CTX]
                blks = [block(I["wba"], KT, [c], rhs_h2, pe_needs=[r1.s_lo.at(KT * (i + 1))],
                              evac=lambda act, ci, t0, n, ps: act.activation(LT[:, t0 // CTX:(t0 + n) // CTX, :], ps[0:8, :].rearrange("q (a c) -> q a c", c=CTX), ACT.Copy))
                        for i, c in enumerate(M2)]

                def act(a, fill):
                    fill()
                    fill()
                    a.wait_ge(*s_bam.at(1))
                    a.activation(LBA, bank[3][:, 0:64].rearrange("q (n c) -> q n c", c=8), ACT.Copy).then_inc(s_baa.sem, 1)
                    a.wait_ge(*s_baa.at(1))
                    a.activation(BETA, LBA[:, :, 0:4], ACT.Sigmoid).then_inc(s_baa.sem, 1)
                    a.activation(EA, hrow[:, 4:8], ACT.Exp).then_inc(s_baa.sem, 1)
                    fill()
                    fill()
                    a.wait_ge(*s_bad.at(1))
                    a.activation(EZ, TT, ACT.Exp).then_inc(s_baa.sem, 1)
                    a.wait_ge(*s_baa.at(4))
                    a.activation(SP, EZ, ACT.Ln, bias=1.0).then_inc(s_baa.sem, 1)
                    fill()
                    fill()
                    a.wait_ge(*s_bam.at(2))
                    a.activation(GC, bank[4][:, 0:32].rearrange("q (n h) -> q n h", h=GH), ACT.Copy).then_inc(s_baa.sem, 1)
                    a.wait_ge(*s_baa.at(6))
                    a.activation(EGC, GC, ACT.Exp).then_inc(s_baa.sem, 1)
                    fill()

                def pe(p, fill):
                    p.wait_ge(*s_unit.at(u))
                    p.wait_ge(*s_evac.at(out_done(blks[1])))
                    for n in range(NC2):
                        mm = p.transpose(bank[3][:, 8 * n:8 * n + 8], LT[:, n // 2, (n % 2) * P:(n % 2 + 1) * P], k2("ident")[0:8, 0:8])
                    mm.then_inc(s_bam.sem, 1)
                    for _ in range(6):
                        fill()
                    p.wait_ge(*s_ba.at(1))
                    p.matmul(bank[4][:, 0:32], k2("upto"), gsm[:, 7, :], start=True, stop=True).then_inc(s_bam.sem, 1)
                    fill()

                def dve(v, fill):
                    ch = dve_chain(v)
                    fill()
                    fill()
                    v.wait_ge(*s_baa.at(1))
                    ch(v.tensor_tensor(Z, LBA[:, :, 4:8], hrow[:, 0:4].unsqueeze(1).to_broadcast([P, NC2, GH]), ALU.add))
                    v.scalar_tensor_tensor(TT, Z, -1.0, Z, ALU.mult, ALU.min).then_inc(s_bad.sem, 1)
                    fill()
                    fill()
                    v.wait_ge(*s_baa.at(5))
                    ch(v.tensor_scalar(TT, EZ, 1.0, -1.0, ALU.add, ALU.add))
                    ch(v.tensor_scalar(TT, TT, 1e-30, None, ALU.max))
                    ch(v.reciprocal(TT, TT))
                    ch(v.tensor_tensor(TT, TT, EZ, ALU.mult))
                    ch(v.tensor_tensor(SP, SP, TT, ALU.mult))
                    ch(v.tensor_scalar(TT, EZ, -0.5, 1.0, ALU.mult, ALU.add))
                    ch(v.tensor_tensor(TT, TT, EZ, ALU.mult))
                    ch(v.tensor_tensor(SP, SP, TT, ALU.max))
                    ch(v.scalar_tensor_tensor(SP, Z, 0.0, SP, ALU.max, ALU.add))
                    v.scalar_tensor_tensor(GG, SP, -1.0, EA.unsqueeze(1).to_broadcast([P, NC2, GH]), ALU.mult, ALU.mult).then_inc(s_ba.sem, 1)
                    fill()
                    fill()
                    v.wait_ge(*s_baa.at(7))
                    v.tensor_tensor(BE, BETA, EGC, ALU.mult).then_inc(s_ba.sem, 1)
                    v.wait_ge(*s_ba.at(2))
                    v.engine_nop().then_inc(s_unit.sem, 1)
                    v.wait_ge(*s_unit.at(u + 1))
                    fill()

                return dict(u=u, blks=blks, points=7, act_first=lambda a: None, pe=pe, act=act, dve=dve)

            def gdn_unit(hd):
                u = n_units[0]
                n_units[0] += 1
                K, Q, V = [A2(i) if hd % 2 == 0 else X(4 + i, 0, SEQ) for i in range(3)]
                TA, TB_, KBG, KD, VB, GB, EG, ATT, DD, AT, XX, XT, YT = (A2(3 + i) for i in range(13))
                needs = [[r1.done], (), (), [s_xst.at(80)]] if hd == 0 else [()] * 4
                blks = [block(I["win2"][0, 4 * i + hd], KT, M2, rhs_h2, evac=plain(x, f), act_needs=needs[i])
                        for i, x, f in ((1, K, ACT.Copy), (0, Q, ACT.Copy), (2, V, ACT.Copy), (3, X(hd, 0, SEQ), ACT.Silu))]
                convolved = ((K, TB_, 1), (Q, TA, 0), (V, KBG, 2))
                QD, OT, U, WT = EG, TB_, V, TA
                SS = Y[:, 7, 0:2 * P]
                GE, KDC = gsm[:, 12, 0:8], gsm[:, 13, 0:8]
                w4 = lambda t, hf: t[:, 512 * hf:512 * hf + 512].rearrange("q (n c) -> q n c", c=P)
                ch_ = lambda t, n: t[:, n * P:(n + 1) * P]
                bk = lambda i: bank[i][:, :].rearrange("q (n c) -> q n c", c=P)
                tokcol = lambda t, hf: t[:, 4 * hf:4 * hf + 4, hd].unsqueeze(2).to_broadcast([P, 4, P])
                rowc = lambda nm: k2(nm).unsqueeze(1).to_broadcast([P, 4, P])
                LV = INV_LEVELS - 1
                names = dict(g_gb=2, g_gbc=2, g_eg=2, g_conv=3, g_silu=3, g_sq=2, g_ss=4, g_rs=4, g_n=2, g_kd=1, g_kdc=1, g_tp=4, g_tk=2, g_tv=2,
                             g_d=4, g_dx=4, g_qk=4, g_att=2, g_a=2, g_tat=2, g_at=2, g_ot=2 * LV, g_py=2 * LV, g_y=2 * LV, g_pz=2 * LV,
                             g_x=2 * LV + 2, g_uw=4, g_u=4, g_S=NC2, g_ws=NC2, g_vn=NC2, g_kv=NC2, g_o=NC2, g_os=2, g_ov=2, g_ol=4, g_or=2)
                s = {k: sem(k, n) for k, n in names.items()}

                def pe(p, fill):
                    p.wait_ge(*s_unit.at(u))
                    p.wait_ge(*s_ba.at(2))
                    for hf in range(2):
                        for j in range(4):
                            n = 4 * hf + j
                            mm = p.matmul(bank[2 + hf][:, j * P:(j + 1) * P], GG[:, n, hd:hd + 1].to_broadcast([P, P]), k2("upto"), start=True, stop=True)
                        mm.then_inc(s["g_gb"].sem, 1)
                    for _ in range(8):
                        fill()
                    for i in range(2):
                        p.wait_ge(*s["g_sq"].at(i + 1))
                        for hf in range(2):
                            p.matmul(bank[4 + 2 * i + hf][:, :], k2("ones"), (TB_, TA)[i][:, 512 * hf:512 * hf + 512], start=True, stop=True).then_inc(s["g_ss"].sem, 1)
                            fill()
                    p.wait_ge(*s["g_gbc"].at(2))
                    p.wait_ge(*s["g_n"].at(1))
                    for hf in range(2):
                        for j in range(4):
                            mm = p.transpose(bank[2 + hf][:, j * P:(j + 1) * P], ch_(K, 4 * hf + j), k2("ident"))
                        mm.then_inc(s["g_tp"].sem, 1)
                    p.wait_ge(*s["g_silu"].at(3))
                    for hf in range(2):
                        for j in range(4):
                            mm = p.transpose(bank[4 + hf][:, j * P:(j + 1) * P], ch_(V, 4 * hf + j), k2("ident"))
                        mm.then_inc(s["g_tp"].sem, 1)
                    fill()
                    p.wait_ge(*s["g_n"].at(2))
                    for hf in range(2):
                        for j in range(4):
                            n = 4 * hf + j
                            mm = p.matmul(bank[6 + hf][:, j * P:(j + 1) * P], ch_(K, n), ch_(Q, n), start=True, stop=True)
                        mm.then_inc(s["g_qk"].sem, 1)
                    for hf in range(2):
                        p.wait_ge(*s["g_tk"].at(hf + 1))
                        for j in range(4):
                            n = 4 * hf + j
                            mm = p.matmul(bank[2 + hf][:, j * P:(j + 1) * P], ch_(K, n), ch_(K, n), start=True, stop=True)
                        mm.then_inc(s["g_qk"].sem, 1)
                    fill()
                    for hf in range(2):
                        p.wait_ge(*s["g_tv"].at(hf + 1))
                        p.wait_ge(*s["g_a"].at(hf + 1))
                        for j in range(4):
                            mm = p.transpose(bank[4 + hf][:, j * P:(j + 1) * P], ch_(DD, 4 * hf + j), k2("ident"))
                        mm.then_inc(s["g_tat"].sem, 1)
                    fill()
                    for k in range(LV):
                        for hf in range(2):
                            p.wait_ge(*s["g_ot"].at(2 * k + hf + 1))
                            p.wait_ge(*s["g_x"].at(2 * k + hf + 1))
                            for j in range(4):
                                n = 4 * hf + j
                                mm = p.matmul(bank[2 + hf][:, j * P:(j + 1) * P], ch_(OT, n), ch_(XX, n), start=True, stop=True)
                            mm.then_inc(s["g_py"].sem, 1)
                        fill()
                        for hf in range(2):
                            p.wait_ge(*s["g_y"].at(2 * k + hf + 1))
                            for j in range(4):
                                n = 4 * hf + j
                                if k < LV - 1:
                                    p.matmul(bank[4 + hf][:, j * P:(j + 1) * P], ch_(XT, n), ch_(YT, n), start=True, stop=True)
                                mm = p.matmul(bank[6 + hf][:, j * P:(j + 1) * P], ch_(YT, n), ch_(XT, n), start=True, stop=True)
                            mm.then_inc(s["g_pz"].sem, 1)
                        fill()
                    for hf in range(2):
                        p.wait_ge(*s["g_x"].at(2 * LV + hf + 1))
                        for j in range(4):
                            n = 4 * hf + j
                            mm = p.matmul(bank[2 + hf][:, j * P:(j + 1) * P], ch_(XT, n), ch_(VB, n), start=True, stop=True)
                        mm.then_inc(s["g_uw"].sem, 1)
                        for j in range(4):
                            n = 4 * hf + j
                            mm = p.matmul(bank[4 + hf][:, j * P:(j + 1) * P], ch_(KBG, n), ch_(XT, n), start=True, stop=True)
                        mm.then_inc(s["g_uw"].sem, 1)
                    p.wait_ge(*s["g_u"].at(4))
                    for n in range(NC2):
                        S = SS[:, (n % 2) * P:(n % 2 + 1) * P]
                        p.wait_ge(*s["g_S"].at(n + 1))
                        p.matmul(bank[6 + n % 2][:, 0:P], ch_(WT, n), S, start=True, stop=True).then_inc(s["g_ws"].sem, 1)
                        p.wait_ge(*s["g_vn"].at(n + 1))
                        p.matmul(bank[2 + n % 2][:, 0:P], ch_(KD, n), ch_(U, n), start=True, stop=True).then_inc(s["g_kv"].sem, 1)
                        o = bank[4 + n // 4][:, (n % 4) * P:(n % 4 + 1) * P]
                        p.matmul(o, S, ch_(QD, n), start=True, stop=False)
                        p.matmul(o, ch_(U, n), ch_(ATT, n), start=False, stop=True).then_inc(s["g_o"].sem, 1)
                        fill()
                    fill()
                    fill()
                    for hf in range(2):
                        p.wait_ge(*s["g_os"].at(hf + 1))
                        p.matmul(bank[6 + hf][:, :], k2("headmean"), AT[:, 512 * hf:512 * hf + 512], start=True, stop=True).then_inc(s["g_ov"].sem, 1)

                def act(a, fill):
                    for i, (x, t, _) in enumerate(convolved):
                        fill()
                        fill()
                        a.wait_ge(*s["g_conv"].at(i + 1))
                        a.activation(x, t, ACT.Silu).then_inc(s["g_silu"].sem, 1)
                        if i < 2:
                            a.wait_ge(*s["g_silu"].at(i + 1))
                            a.activation(t, x, ACT.Square).then_inc(s["g_sq"].sem, 1)
                    fill()
                    fill()
                    for hf in range(2):
                        a.wait_ge(*s["g_gb"].at(hf + 1))
                        a.activation(GB[:, 512 * hf:512 * hf + 512], bank[2 + hf][:, :], ACT.Copy).then_inc(s["g_gbc"].sem, 1)
                    a.wait_ge(*s["g_gbc"].at(2))
                    last = GB.rearrange("q (n c) -> q n c", c=P)[:, :, P - 1]
                    a.activation(GE, last, ACT.Exp).then_inc(s["g_eg"].sem, 1)
                    a.activation(EG, GB, ACT.Exp).then_inc(s["g_eg"].sem, 1)
                    a.wait_ge(*s["g_kd"].at(1))
                    a.activation(KDC, KDC, ACT.Exp).then_inc(s["g_kdc"].sem, 1)
                    for i in range(2):
                        for hf in range(2):
                            a.wait_ge(*s["g_ss"].at(2 * i + hf + 1))
                            t = (TB_, TA)[i][:, 512 * hf:512 * hf + 512]
                            a.activation(t, bank[4 + 2 * i + hf][:, :], ACT.Ln, bias=k2("eps")).then_inc(s_gln.sem, 1)
                            a.wait_ge(*s_gln.at(4 * hd + 2 * i + hf + 1))
                            a.activation(t, t, ACT.Exp, scale=-0.5).then_inc(s["g_rs"].sem, 1)
                    for _ in range(4):
                        fill()
                    for i, t in enumerate((XX, DD)):
                        for hf in range(2):
                            a.wait_ge(*s["g_d"].at(2 * i + hf + 1))
                            a.activation(w4(t, hf), w4(t, hf), ACT.Exp).then_inc(s["g_dx"].sem, 1)
                    for _ in range(3):
                        fill()
                    for hf in range(2):
                        a.wait_ge(*s["g_tat"].at(hf + 1))
                        a.activation(w4(AT, hf), bk(4 + hf), ACT.Copy).then_inc(s["g_at"].sem, 1)
                    for k in range(LV):
                        for hf in range(2):
                            a.wait_ge(*s["g_py"].at(2 * k + hf + 1))
                            a.activation(w4(YT, hf), bk(2 + hf), ACT.Copy).then_inc(s["g_y"].sem, 1)
                        fill()
                        fill()
                    for hf in range(2):
                        a.wait_ge(*s["g_uw"].at(2 * hf + 1))
                        a.activation(w4(U, hf), bk(2 + hf), ACT.Copy).then_inc(s["g_u"].sem, 1)
                        a.wait_ge(*s["g_uw"].at(2 * hf + 2))
                        a.activation(w4(WT, hf), bk(4 + hf), ACT.Copy).then_inc(s["g_u"].sem, 1)
                    for _ in range(NC2):
                        fill()
                    for hf in range(2):
                        a.wait_ge(*s["g_o"].at(4 * hf + 4))
                        a.activation(w4(DD, hf), bk(4 + hf), ACT.Copy).then_inc(s["g_ol"].sem, 1)
                        a.activation(w4(AT, hf), bk(4 + hf), ACT.Square).then_inc(s["g_os"].sem, 1)
                    fill()
                    fill()
                    for hf in range(2):
                        a.wait_ge(*s["g_ov"].at(hf + 1))
                        a.activation(w4(AT, hf), bk(6 + hf), ACT.Ln, bias=k2("eps")).then_inc(s["g_ol"].sem, 1)
                        a.wait_ge(*s["g_ol"].at(2 + hf + 1))
                        a.activation(w4(AT, hf), w4(AT, hf), ACT.Exp, scale=-0.5).then_inc(s["g_or"].sem, 1)

                def dve(v, fill):
                    ch = dve_chain(v)
                    for i, (x, t, tap) in enumerate(convolved):
                        v.wait_ge(*s_evac.at(out_done(blks[i])))
                        w = cw2[:, 4 * tap + hd, :]
                        ch(v.tensor_scalar(t, x, w[:, 3:4], None, ALU.mult))
                        for j in range(1, 4):
                            ins = v.scalar_tensor_tensor(t[:, j:], x[:, 0:SEQ - j], w[:, 3 - j:4 - j], t[:, j:], ALU.mult, ALU.add)
                            if j == 3:
                                ins.then_inc(s["g_conv"].sem, 1)
                            else:
                                ch(ins)
                        fill()
                        fill()
                    fill()
                    fill()
                    v.wait_ge(*s["g_gbc"].at(2))
                    last = GB.rearrange("q (n c) -> q n c", c=P)[:, :, P - 1]
                    v.tensor_tensor(KDC, last, GC[:, :, hd], ALU.subtract).then_inc(s["g_kd"].sem, 1)
                    for hf in range(2):
                        ch(v.tensor_tensor(w4(XX, hf), w4(GB, hf), tokcol(GC, hf), ALU.subtract))
                        v.tensor_tensor(w4(XX, hf), w4(XX, hf), rowc("causalT"), ALU.add).then_inc(s["g_d"].sem, 1)
                    for hf in range(2):
                        ch(v.tensor_tensor(w4(DD, hf), tokcol(GC, hf), w4(GB, hf), ALU.subtract))
                        v.tensor_tensor(w4(DD, hf), w4(DD, hf), rowc("strict"), ALU.add).then_inc(s["g_d"].sem, 1)
                    v.wait_ge(*s["g_rs"].at(2))
                    v.tensor_tensor(K, K, TB_, ALU.mult).then_inc(s["g_n"].sem, 1)
                    fill()
                    fill()
                    v.wait_ge(*s["g_rs"].at(4))
                    fill()
                    fill()
                    v.scalar_tensor_tensor(Q, Q, float(P) ** -0.5, TA, ALU.mult, ALU.mult).then_inc(s["g_n"].sem, 1)
                    v.wait_ge(*s["g_eg"].at(2))
                    v.wait_ge(*s["g_n"].at(2))
                    ch(v.tensor_tensor(QD, EG, Q, ALU.mult))
                    v.wait_ge(*s["g_kdc"].at(1))
                    for hf in range(2):
                        v.wait_ge(*s["g_tp"].at(hf + 1))
                        ch(v.tensor_tensor(w4(KBG, hf), bk(2 + hf), tokcol(BE, hf), ALU.mult))
                        v.tensor_tensor(w4(KD, hf), bk(2 + hf), KDC[:, 4 * hf:4 * hf + 4].unsqueeze(2).to_broadcast([P, 4, P]), ALU.mult).then_inc(s["g_tk"].sem, 1)
                    fill()
                    for hf in range(2):
                        v.wait_ge(*s["g_tp"].at(2 + hf + 1))
                        v.tensor_tensor(w4(VB, hf), bk(4 + hf), tokcol(BETA, hf), ALU.mult).then_inc(s["g_tv"].sem, 1)
                    for hf in range(2):
                        v.wait_ge(*s["g_qk"].at(hf + 1))
                        v.wait_ge(*s["g_dx"].at(hf + 1))
                        v.tensor_tensor(w4(ATT, hf), bk(6 + hf), w4(XX, hf), ALU.mult).then_inc(s["g_att"].sem, 1)
                    fill()
                    for hf in range(2):
                        v.wait_ge(*s["g_dx"].at(2 + hf + 1))
                        ch(v.tensor_tensor(w4(DD, hf), w4(DD, hf), tokcol(BETA, hf), ALU.mult))
                        v.wait_ge(*s["g_qk"].at(2 + hf + 1))
                        v.tensor_tensor(w4(DD, hf), bk(2 + hf), w4(DD, hf), ALU.mult).then_inc(s["g_a"].sem, 1)
                    fill()
                    v.wait_ge(*s["g_att"].at(2))
                    v.wait_ge(*s["g_a"].at(2))
                    for hf in range(2):
                        ch(v.tensor_tensor(w4(XX, hf), w4(DD, hf), rowc("low0"), ALU.mult))
                        ch(v.tensor_tensor(w4(XX, hf), rowc("ident"), w4(XX, hf), ALU.subtract))
                        v.wait_ge(*s["g_at"].at(hf + 1))
                        ch(v.tensor_tensor(w4(XT, hf), w4(AT, hf), rowc("lowT0"), ALU.mult))
                        v.tensor_tensor(w4(XT, hf), rowc("ident"), w4(XT, hf), ALU.subtract).then_inc(s["g_x"].sem, 1)
                    for k in range(LV):
                        for hf in range(2):
                            if k:
                                v.wait_ge(*s["g_py"].at(2 * (k - 1) + hf + 1))
                            v.tensor_tensor(w4(OT, hf), w4(AT, hf), rowc(f"lowT{k + 1}"), ALU.mult).then_inc(s["g_ot"].sem, 1)
                        fill()
                        for hf in range(2):
                            v.wait_ge(*s["g_pz"].at(2 * k + hf + 1))
                            v.wait_ge(*s["g_x"].at(2 * k + hf + 1))
                            if k < LV - 1:
                                ch(v.tensor_tensor(w4(XX, hf), w4(XX, hf), bk(4 + hf), ALU.subtract))
                            v.tensor_tensor(w4(XT, hf), w4(XT, hf), bk(6 + hf), ALU.subtract).then_inc(s["g_x"].sem, 1)
                        fill()
                    v.memset(SS, 0.0).then_inc(s["g_S"].sem, 1)
                    v.wait_ge(*s["g_u"].at(4))
                    v.wait_ge(*s["g_S"].at(1))
                    for n in range(NC2):
                        v.wait_ge(*s["g_ws"].at(n + 1))
                        v.tensor_tensor(ch_(U, n), ch_(U, n), bank[6 + n % 2][:, 0:P], ALU.subtract).then_inc(s["g_vn"].sem, 1)
                        if n + 1 < NC2:
                            v.wait_ge(*s["g_kv"].at(n + 1))
                            v.wait_ge(*s["g_S"].at(n + 1))
                            v.scalar_tensor_tensor(SS[:, ((n + 1) % 2) * P:((n + 1) % 2 + 1) * P], SS[:, (n % 2) * P:(n % 2 + 1) * P], GE[:, n:n + 1],
                                                   bank[2 + n % 2][:, 0:P], ALU.mult, ALU.add).then_inc(s["g_S"].sem, 1)
                        fill()
                    fill()
                    fill()
                    v.wait_ge(*s_evac.at(out_done(blks[3])))
                    for hf in range(2):
                        v.wait_ge(*s["g_or"].at(hf + 1))
                        ch(v.scalar_tensor_tensor(w4(DD, hf), w4(DD, hf), hrow[:, 8:9], w4(AT, hf), ALU.mult, ALU.mult))
                        y = X(hd, 512 * hf, 512)
                        ins = v.tensor_tensor(y, DD[:, 512 * hf:512 * hf + 512], y, ALU.mult)
                        if hf:
                            ins.then_inc(s_unit.sem, 1)
                            v.wait_ge(*s_unit.at(u + 1))
                        else:
                            ch(ins)

                return dict(u=u, blks=blks, points=17 + 2 * LV + NC2, tail=5, act_first=lambda a: None, pe=pe, act=act, dve=dve)

            s_gln = sem("gln", 4 * GH)

            SF2 = A2(11, 2).rearrange("q (e x) -> q e x", e=2)

            def load_bias(g, p):
                for e in range(2):
                    g.dma_start(SF2[:, e, :], bass.AP(tensor=scratch["bias"], offset=(2 * p + e) * TB, ap=[[1, P], [1, 1024]])).then_inc(s_sf.sem, 16)

            s_sf = sem("sf")

            def swa_unit(p):
                u = n_units[0]
                n_units[0] += 1
                Q, K, V = (A2(i + 13 * (p % 2)) for i in range(3))
                VT, PT = A2(3), A2(4)
                blks = [block(I["win2"][0, 16 + 4 * i + p], KT, M2, rhs_h2, evac=plain(x, scale=HD ** -0.5 if i == 0 else 1.0))
                        for i, x in enumerate((Q, K, V))]
                LL = [A2(5), A2(6)]
                PR = [A2(7), A2(8)]
                W = A2(9, 2).rearrange("q (e x) -> q e x", e=2)
                F = SF2
                its = [(a_, e) for a_ in range(NC2) for e in range(2)]
                NI = len(its)
                halves = [[(h, 512 * h, min(512, P * (a_ + 1) - 512 * h)) for h in range((a_ + 4) // 4)] for a_, e in its]
                hfirst = [sum(len(x) for x in halves[:i]) for i in range(NI + 1)]
                NHF = hfirst[NI]
                even = lambda k: (k + 1) // 2
                s_f, s_fl, s_w, s_tp, s_vt = (sem(x, n) for x, n in (("sf", 32), ("sfl", 4), ("sw", 4), ("stp", 2), ("svt", 2)))
                s_s, s_tt = sem("ss", NHF), sem("stt", NHF)
                s_m, s_e, s_pn, s_o = (sem(x, NI) for x in "sm se spn so".split())
                s_ti, s_pa, s_pd, s_y = sem("sti", NHF), sem("spa", even(NHF)), sem("spd", NHF - even(NHF)), sem("sy", NC2)

                def pool(g):
                    if p == 0:
                        g.wait_ge(*s_unit.at(u))
                        load_bias(g, 0)
                    if p + 1 < SWA_PAIRS:
                        g.wait_ge(*s_fl.at(4))
                        load_bias(g, p + 1)

                def pe(pt, fill):
                    pt.wait_ge(*s_unit.at(u))
                    pt.wait_ge(*s_f.at(32))
                    for i in range(4):
                        pt.matmul(bank[2 + i][:, :], k2("flip"), F[:, i // 2, (i % 2) * 512:(i % 2) * 512 + 512], start=True, stop=True).then_inc(s_fl.sem, 1)
                    pt.wait_ge(*s_evac.at(out_done(blks[2])))
                    for f in range(2):
                        for m in range(4):
                            mm = pt.transpose(bank[6 + f][:, m * P:(m + 1) * P], V[:, (4 * f + m) * P:(4 * f + m + 1) * P], k2("ident"))
                        mm.then_inc(s_tp.sem, 1)
                    pt.wait_ge(*s_w.at(4))
                    pt.wait_ge(*s_vt.at(2))

                    def scores(i):
                        a_, e = its[i]
                        r = slice(64 * e, 64 * e + 64)
                        for h, k0, n in halves[i]:
                            hi = hfirst[i] + h
                            if hi >= 3:
                                pt.wait_ge(*s_tt.at(hi - 2))
                            pt.matmul(bank[2 + hi % 3][:, 0:n], Q[r, a_ * P:(a_ + 1) * P], K[r, k0:k0 + n], start=True, stop=True).then_inc(s_s.sem, 1)

                    def turn(i):
                        pt.wait_ge(*s_pn.at(i + 1))
                        for h, k0, n in halves[i]:
                            fi = hfirst[i] + h
                            if fi >= 2:
                                pt.wait_ge(*(s_pa if fi % 2 == 0 else s_pd).at(fi // 2))
                            for m in range(n // P):
                                mm = pt.transpose(bank[5 + fi % 2][:, m * P:(m + 1) * P], PR[i % 2][:, k0 + m * P:k0 + (m + 1) * P], k2("ident"))
                            mm.then_inc(s_ti.sem, 1)

                    def values(i):
                        a_, e = its[i]
                        k = hfirst[i + 1]
                        pt.wait_ge(*s_pa.at(even(k)))
                        if k > 1:
                            pt.wait_ge(*s_pd.at(k - even(k)))
                        if e == 0 and a_:
                            pt.wait_ge(*s_y.at(a_))
                        for kb in range(a_ + 1):
                            mm = pt.matmul(bank[7][64 * e:64 * e + 64, 0:P], VT[:, kb * P + 64 * e:kb * P + 64 * e + 64], PT[:, kb * P:(kb + 1) * P],
                                           start=kb == 0, stop=kb == a_)
                        mm.then_inc(s_o.sem, 1)

                    scores(0)
                    for i in range(NI):
                        if i + 1 < NI:
                            scores(i + 1)
                        turn(i)
                        fill()
                        values(i)

                def act(a, fill):
                    for i in range(4):
                        a.wait_ge(*s_fl.at(i + 1))
                        a.activation(W[:, i // 2, (i % 2) * 512:(i % 2) * 512 + 512], bank[2 + i][:, :], ACT.Copy).then_inc(s_w.sem, 1)
                    for f in range(2):
                        a.wait_ge(*s_tp.at(f + 1))
                        a.activation(VT[:, 512 * f:512 * f + 512], bank[6 + f][:, :], ACT.Copy).then_inc(s_vt.sem, 1)

                    def exps(i):
                        a_, e = its[i]
                        nk = P * (a_ + 1)
                        a.wait_ge(*s_m.at(i + 1))
                        if i >= 2:
                            a.wait_ge(*s_ti.at(hfirst[i - 1]))
                        sm = gsm[:, 14 + i % 2, :]
                        a.activation(PR[i % 2][:, 0:nk], LL[i % 2][:, 0:nk], ACT.Exp, bias=sm[:, 2:3], accum_out=sm[:, 3:4]).then_inc(s_e.sem, 1)

                    def evac(i):
                        for h, k0, n in halves[i]:
                            fi = hfirst[i] + h
                            if fi % 2 == 0:
                                a.wait_ge(*s_ti.at(fi + 1))
                                if i:
                                    a.wait_ge(*s_o.at(i))
                                a.activation(PT[:, k0:k0 + n], bank[5][:, 0:n], ACT.Copy).then_inc(s_pa.sem, 1)

                    exps(0)
                    for i in range(NI):
                        if i + 1 < NI:
                            exps(i + 1)
                        evac(i)
                        fill()

                def dve(v, fill):
                    ch = dve_chain(v)
                    v.wait_ge(*s_w.at(4))

                    def maxes(i):
                        a_, e = its[i]
                        sm = gsm[:, 14 + i % 2, :]
                        if i >= 2:
                            v.wait_ge(*s_e.at(i - 1))
                        for h, k0, n in halves[i]:
                            hi = hfirst[i] + h
                            v.wait_ge(*s_s.at(hi + 1))
                            x0 = 896 - P * a_ + k0
                            v.tensor_tensor_reduce(out=LL[i % 2][:, k0:k0 + n], in0=bank[2 + hi % 3][:, 0:n], in1=W[:, e, x0:x0 + n], scale=1.0,
                                                   scalar=-3.0e38, op0=ALU.add, op1=ALU.max, accum_out=sm[:, h:h + 1]).then_inc(s_tt.sem, 1)
                        v.wait_ge(*s_tt.at(hfirst[i + 1]))
                        if len(halves[i]) == 2:
                            v.tensor_scalar(sm[:, 2:3], sm[:, 0:1], sm[:, 1:2], -1.0, ALU.max, ALU.mult).then_inc(s_m.sem, 1)
                        else:
                            v.tensor_scalar(sm[:, 2:3], sm[:, 0:1], -1.0, None, ALU.mult).then_inc(s_m.sem, 1)

                    def result(i):
                        a_, e = its[i]
                        if e == 1:
                            v.wait_ge(*s_o.at(i + 1))
                            v.tensor_copy(X(4 + p, a_ * P, P), bank[7][:, 0:P]).then_inc(s_y.sem, 1)

                    maxes(0)
                    for i in range(NI):
                        a_, e = its[i]
                        nk = P * (a_ + 1)
                        sm = gsm[:, 14 + i % 2, :]
                        v.wait_ge(*s_e.at(i + 1))
                        ch(v.reciprocal(sm[:, 4:5], sm[:, 3:4]))
                        v.tensor_scalar(PR[i % 2][:, 0:nk], PR[i % 2][:, 0:nk], sm[:, 4:5], None, ALU.mult).then_inc(s_pn.sem, 1)
                        if i:
                            result(i - 1)
                        if i + 1 < NI:
                            maxes(i + 1)
                        for h, k0, n in halves[i]:
                            fi = hfirst[i] + h
                            if fi % 2:
                                v.wait_ge(*s_ti.at(fi + 1))
                                if i:
                                    v.wait_ge(*s_o.at(i))
                                v.tensor_copy(PT[:, k0:k0 + n], bank[6][:, 0:n]).then_inc(s_pd.sem, 1)
                        fill()
                    result(NI - 1)
                    v.wait_ge(*s_y.at(NC2))
                    v.engine_nop().then_inc(s_unit.sem, 1)
                    v.wait_ge(*s_unit.at(u + 1))

                return dict(u=u, blks=blks, points=NI, act_first=lambda a: None, pe=pe, act=act, dve=dve, pool=pool)

            phases.append(run_units([ba_unit()] + [gdn_unit(hd) for hd in range(GH)] + [swa_unit(p) for p in range(SWA_PAIRS)]))

            b2.close()
            b3 = top.enter_context(ExitStack())
            FF = sb("FF", [P, 2, FT, 512], F32R, b3)
            HF = sb("HF", [P, 2, KT, 512], F32R, b3)
            O3 = sb("O3", [P, KT, 512], F32, b3)
            c3 = sb("c3", [P, P + 1], F32, b3)
            HF0 = FT * 2 * 512
            AR0 = 2 * KT * SEQ + N2 + 48 + 9 + 512
            SQ3 = [Y[:, 2 * i:2 * i + 2, 0:CTX] for i in range(2)]
            RS3, RS4 = Y[:, 4:6, 0:CTX], Y[:, 6:8, 0:CTX]
            s_c3 = sem("const3")
            s_xr = [sem(f"xr{i}") for i in range(2)]
            res = ar2[:, HF0 + 2 * KT * 512 - AR0:HF0 + 3 * KT * 512 - AR0].rearrange("q (m t) -> q m t", t=512)

            def half_norm(c):
                return NormIn(2, [M2[c]], lambda part, m, t0, n: HF[:, part, m, :], SQ3, [RS3],
                              half2(A2(1)) if c == 0 else [O3[:, 6, :], O3[:, 7, :]],
                              (lambda: k2("mean")) if c == 0 else (lambda: c3[:, 0:P]), (lambda: k2("eps")) if c == 0 else (lambda: c3[:, P:P + 1]), 4 + c)

            def out2_phase():
                u = n_units[0]
                part_a = [block(I["wout2"][0, m], KT, M2[:1], rhs_h2) for m in range(KT)]
                part_b = [block(I["wout2"][0, m], KT, M2[1:], rhs_h2) for m in range(KT)]
                s_hi, s_lo = sem("m_hi", KT), sem("m_lo", KT)

                def pool(g):
                    g.wait_ge(*s_unit.at(u))
                    for c in range(2):
                        if c:
                            g.wait_ge(*ro.x_done(0, KT - 1))
                        g.dma_start(res, scratch["x2"].ap()[:, :, CTX + 512 * c:CTX + 512 * c + 512]).then_inc(s_xr[c].sem, 16)

                def pe(p):
                    for m, blk in enumerate(part_a):
                        whole(pe_block(p, blk, (lambda i: p.wait_ge(*s_lo.at(i + 1))) if m == 0 else None))
                        if m:
                            ro.pe_var(p, 0, m - 1)
                    for m, blk in enumerate(part_b):
                        whole(pe_block(p, blk))
                        ro.pe_var(p, *((1, m - 1) if m else (0, KT - 1)))
                        if m == 4:
                            ri.pe_var(p, 0)
                    ro.pe_var(p, 1, KT - 1)

                def act(a):
                    a.wait_ge(*s_unit.at(u))
                    for k in range(KT):
                        a.activation(H2[:, 0, k, :], X(k, 0, SEQ), ACT.Copy).then_inc(s_hi.sem, 1)
                    a.wait_ge(*s_lo.at(KT))

                    def evac(m):
                        return lambda a, ci, t0, n, ps: a.activation(X(m, t0, n), ps, ACT.Copy)

                    for m, blk in enumerate(part_a):
                        whole(act_block(a, blk, evac(m)))
                        ro.act_square(a, 0, m, s_evac.at(out_done(blk)))
                    for m, blk in enumerate(part_b):
                        whole(act_block(a, blk, evac(m)))
                        if m == 1:
                            ro.act_rstd(a, 0)
                        ro.act_square(a, 1, m, s_evac.at(out_done(blk)))
                        if m == 4:
                            ri.act_squares(a, 0, lambda m: ro.x_done(0, m))
                        if m == 5:
                            ri.act_rstd(a, 0)
                        if m == 6:
                            ri.act_hi(a, 0)
                    ro.act_rstd(a, 1)

                def dve(v):
                    for k in range(KT):
                        v.wait_ge(*s_hi.at(k + 1))
                        v.tensor_tensor(H2[:, 1, k, :], X(k, 0, SEQ), H2[:, 0, k, :].bitcast(F32), ALU.subtract).then_inc(s_lo.sem, 1)
                    for blk in part_a:
                        whole(dve_block(v, blk))
                    for m, blk in enumerate(part_b):
                        whole(dve_block(v, blk))
                        if m == 2:
                            v.wait_ge(*s_xr[0].at(16))
                            ro.dve_add(v, 0, range(0, 4))
                        if m == 3:
                            ro.dve_add(v, 0, range(4, KT))
                        if m == 6:
                            ri.dve_scale(v, 0)
                    v.wait_ge(*s_xr[1].at(16))
                    ro.dve_add(v, 1)

                return dict(pool=pool, pe=pe, act=act, dve=dve)

            ro = NormOut(1, M2, X, lambda m, t0, n: res[:, m, :], half2(A2(0)), A2(2)[:, 0:512], lambda: k2("mean"), lambda: k2("eps"), 2)
            ri = half_norm(0)
            phases.append(out2_phase())

            s_outd = sem("outd")

            def consts3_phase():
                def pool(g):
                    g.wait_ge(*ro.x_done(1, KT - 1))
                    g.dma_start(c3[:, :], I["c2"][:, C2["mean"][0]:C2["mean"][0] + P + 1]).then_inc(s_c3.sem, 16)
                return dict(pool=pool)

            phases.append(consts3_phase())

            def ffn(c, rin, free, nxt):
                t0c = 512 * c
                one = [(t0c, 512)]
                G1, U1, FP = ([O3[:, 2 * i, :], O3[:, 2 * i + 1, :]] for i in range(3))
                rh = lambda part, k, t0, n: HF[:, part, k, :]
                rf = lambda part, k, t0, n: FF[:, part, k, :]
                up = []
                for j in range(FT):
                    up.append((block(I["wgate"][0, j], KT, one, rh, pe_needs=[rin.done] if j == 0 else (), act_needs=[free] if j == 0 else ()),
                               block(I["wup"][0, j], KT, one, rh)))
                down = []
                for m in range(KT):
                    ks = [(0, 8), (8, 8), (16, 6)]
                    down.append([block(I["wdown"][m, :, k0 * P:(k0 + n) * P], n, one, rf, k0, k0 == 0, k0 == 16) for k0, n in ks])
                s_fp, s_fhi, s_flo = sem("f_p", FT), sem("f_hi", FT), sem("f_lo", FT)
                rout = NormOut(3, one, lambda m, t0, n: O3[:, m, :], X, SQ3, RS4, lambda: c3[:, 0:P], lambda: c3[:, P:P + 1], 2)
                NORM = FT - 4

                def pe(p):
                    for j, (g, w) in enumerate(up):
                        whole(pe_block(p, g))
                        whole(pe_block(p, w))
                        if nxt and j == NORM:
                            nxt.pe_var(p, 0)
                    for m, bl in enumerate(down):
                        for blk in bl:
                            whole(pe_block(p, blk, (lambda i: p.wait_ge(*s_flo.at(blk["k0"] + i + 1))) if m == 0 else None))
                        if m:
                            rout.pe_var(p, 0, m - 1)
                    rout.pe_var(p, 0, KT - 1)

                def act(a):
                    def rounded(j):
                        a.wait_ge(*s_fp.at(j + 1))
                        a.activation(FF[:, 0, j, :], FP[j % 2], ACT.Copy).then_inc(s_fhi.sem, 1)

                    if c == 0:
                        a.wait_ge(*s_c3.at(16))
                    for j, (g, w) in enumerate(up):
                        if j >= 2:
                            a.wait_ge(*s_fp.at(j - 1))
                        whole(act_block(a, g, lambda a, ci, t0, n, ps: a.activation(G1[j % 2], ps, ACT.Silu)))
                        if j:
                            rounded(j - 1)
                        whole(act_block(a, w, lambda a, ci, t0, n, ps: a.activation(U1[j % 2], ps, ACT.Copy)))
                        if nxt and j == NORM:
                            nxt.act_squares(a, 0)
                        if nxt and j == NORM + 1:
                            nxt.act_rstd(a, 0)
                    rounded(FT - 1)
                    a.wait_ge(*s_flo.at(FT))
                    for m, bl in enumerate(down):
                        for blk in bl:
                            whole(act_block(a, blk, lambda a, ci, t0, n, ps: a.activation(O3[:, m, :], ps, ACT.Copy)))
                        if nxt and m == 0:
                            nxt.act_hi(a, 0)
                        rout.act_square(a, 0, m, s_evac.at(out_done(bl[-1])))
                    rout.act_rstd(a, 0)

                def dve(v):
                    def rest(j):
                        v.wait_ge(*s_fhi.at(j + 1))
                        v.tensor_tensor(FF[:, 1, j, :], FP[j % 2], FF[:, 0, j, :].bitcast(F32), ALU.subtract).then_inc(s_flo.sem, 1)

                    for j, (g, w) in enumerate(up):
                        whole(dve_block(v, g))
                        if j:
                            rest(j - 1)
                        v.wait_ge(*s_evac.at(out_done(w)))
                        if j >= 2:
                            v.wait_ge(*s_flo.at(j - 1))
                        v.tensor_tensor(FP[j % 2], G1[j % 2], U1[j % 2], ALU.mult).then_inc(s_fp.sem, 1)
                        whole(dve_block(v, w))
                    rest(FT - 1)
                    for m, bl in enumerate(down):
                        for blk in bl:
                            whole(dve_block(v, blk))
                        if nxt and m == 0:
                            nxt.dve_scale(v, 0)
                    rout.dve_add(v, 0)

                def store(g):
                    g.wait_ge(*rout.x_done(0, KT - 1))
                    g.dma_start(out[:, :, t0c:t0c + 512], Y[:, :, CTX + t0c:CTX + t0c + 512]).then_inc(s_outd.sem, 16)

                return dict(pe=pe, act=act, dve=dve, pool=store), rout.x_done(0, KT - 1)

            ri2 = half_norm(1)
            first, o3_free = ffn(0, ri, ro.x_done(1, KT - 1), ri2)
            second, _ = ffn(1, ri2, o3_free, None)
            phases += [first, second]

            def end_phase():
                def pool(g):
                    g.wait_ge(*s_outd.at(32))
                return dict(pool=pool)

            phases.append(end_phase())

        blk = top.enter_context(nc.Block())

        @blk.sync
        def _(sp):
            sp_weights(sp)
            for ph in phases:
                if "sp" in ph:
                    ph["sp"](sp)

        @blk.gpsimd
        def _(pool):
            for ph in phases:
                if "pool" in ph:
                    ph["pool"](pool)

        @blk.scalar
        def _(act):
            for ph in phases:
                if "act" in ph:
                    ph["act"](act)

        @blk.tensor
        def _(pe):
            for ph in phases:
                if "pe" in ph:
                    ph["pe"](pe)

        @blk.vector
        def _(dve):
            for ph in phases:
                if "dve" in ph:
                    ph["dve"](dve)


def layout(inputs):
    f = np.float32
    a = {k: np.asarray(v) for k, v in inputs.items()}
    cols = lambda w: np.ascontiguousarray(w.reshape(w.shape[0], KT, P, -1, P).transpose(0, 3, 2, 1, 4).reshape(w.shape[0], -1, P, KT * P))
    feat = lambda v: np.ascontiguousarray(v.reshape(v.shape[0], -1, P).transpose(2, 0, 1))
    x = np.concatenate([a["ctx"][0], a["x"][0]], axis=0)
    put = {
        "xt": np.ascontiguousarray(x.T.reshape(KT, P, T).transpose(1, 0, 2)),
        "c2t": np.ascontiguousarray(np.stack([a["c"][0], a["c_ctx"]], axis=1).reshape(KT, P, 2).transpose(1, 0, 2)),
        "wmod": cols(a["w_mod"]), "bmod": feat(a["b_mod"]),
        "win": cols(a["w_in"]), "wout": cols(a["w_out"]),
        "convp": np.ascontiguousarray(np.concatenate([a["conv_w"], a["conv_b"][:, None]], axis=1).reshape(LAYERS, 4, 2, P).transpose(3, 0, 2, 1)),
        "decay": np.ascontiguousarray(a["ret_decay"].reshape(LAYERS * 12, 1)),
        "decayp": np.ascontiguousarray(a["ret_decay"].reshape(LAYERS, 2, PAIRS, 2).transpose(0, 3, 1, 2).reshape(LAYERS * 12, 1)),
        "rpb": np.ascontiguousarray(a["na_rpb"].reshape(LAYERS * 45, 2, RPB_W)),
        "lnp": np.ascontiguousarray(np.stack([a["ln_g"], a["ln_b"]], axis=1).reshape(LAYERS, 2, KT, P).transpose(3, 0, 1, 2)),
    }
    w2 = a["w_in_2"]
    small = GH * P * 4
    wide = np.concatenate([w2[:, :, :small], w2[:, :, small + 2 * GH:]], axis=2)
    ba = np.zeros((P, KT, P), f)
    ba[:, :, :2 * GH] = w2[0, :, small:small + 2 * GH].reshape(KT, P, 2 * GH).transpose(1, 0, 2)
    put.update({
        "win2": cols(wide), "wba": ba.reshape(P, KT * P),
        "cw2": np.ascontiguousarray(a["conv_w_2"][0].reshape(4, 12, P).transpose(2, 1, 0)),
        "dtb": a["dt_bias_2"], "alog": a["a_log_2"], "onorm": np.ascontiguousarray(a["onorm_g_2"].reshape(P, 1)),
        "relb": np.concatenate([a["rel_bias_2"], np.ones((1, 8), f)], axis=0),
        "gp2": np.ascontiguousarray(np.concatenate([a["g_mix_pre_2"], a["g_mix_post_2"], a["g_ffn_pre_2"], a["g_ffn_post_2"]], axis=0)
                                    .reshape(4, KT, P).transpose(2, 0, 1)),
        "wout2": cols(a["w_out_2"]), "wgate": cols(a["w_gate_2"]), "wup": cols(a["w_up_2"]),
        "wdown": np.ascontiguousarray(a["w_down_2"][0].reshape(FT, P, KT, P).transpose(2, 1, 0, 3).reshape(KT, P, FT * P)),
    })
    put.update(constants())
    return put


def program(nc, put):
    I = {}
    for name, v in put.items():
        t = nc.dram_tensor(f"in_{name}", v.shape, F32, kind="ExternalInput")
        I[name] = t.ap()
        I[name + "_t"] = t
    out = nc.dram_tensor("out_fm", [P, KT, SEQ], F32, kind="ExternalOutput").ap()
    scratch = {
        "x1": nc.dram_tensor("x1", [P, KT, T], F32, kind="Internal"),
        "br": nc.dram_tensor("branches", [P, KT, T], F32, kind="Internal"),
        "x2": nc.dram_tensor("x2", [P, KT, T], F32, kind="Internal"),
        "rpb": nc.dram_tensor("rpbpad", [LAYERS * 6 * RPB_H, 127], F32, kind="Internal"),
        "bias": nc.dram_tensor("biasrow", [8, TB], F32, kind="Internal"),
    }
    build(nc, I, out, scratch)


def kernel(**inputs):
    import concourse.bacc as bacc
    from concourse.bass_utils import run_bass_kernel_spmd as run

    put = layout(inputs)
    nc = bacc.Bacc("TRN2", target_bir_lowering=False, num_devices=1)
    program(nc, put)
    r = run(nc, [{f"in_{k}": v for k, v in put.items()}], core_ids=[0])
    fm = r.results[0]["out_fm"]
    return np.ascontiguousarray(fm.transpose(2, 1, 0).reshape(1, SEQ, D))
```
